# Optimizing a Trainium2 kernel written in Bass

```python
import math
import jax, jax.numpy as jnp
from jax import lax
import numpy as np

D_MODEL = 2048
BATCH = 1
SEQ = 256
DEPTH = 1

MIX_W = D_MODEL
GROUP_W = MIX_W // 4
HEAD_DIM = 64
CONV_A_CH = GROUP_W
CONV_A_K = 3
SWA_HEADS = GROUP_W // HEAD_DIM
SWA_KV_HEADS = 2
SWA_WINDOW = 128
SSM_D_INNER = GROUP_W
SSM_HEADDIM = 64
SSM_HEADS = SSM_D_INNER // SSM_HEADDIM
SSM_GROUPS = 2
SSM_STATE = 128
SSM_CONV_K = 4
SSM_CHUNK = 128
SSM_XBC = SSM_D_INNER + 2 * SSM_GROUPS * SSM_STATE
SB_HEADS = GROUP_W // HEAD_DIM
Q_BLOCK = 128
N_EXPERTS = 16
N_EXPERT_GROUPS = 4
EXPERTS_PER_GROUP = N_EXPERTS // N_EXPERT_GROUPS
TOPK_GROUPS = 1
TOP_K = 2
D_FF = 1024
MOE_BLOCK = 128
N_MOD = 6
EPS = 1e-6

IN_A = 3 * CONV_A_CH
IN_B = SWA_HEADS * HEAD_DIM + 2 * SWA_KV_HEADS * HEAD_DIM
IN_C = SSM_D_INNER + SSM_XBC + SSM_HEADS
IN_D = 3 * SB_HEADS * HEAD_DIM
IN_DIM = IN_A + IN_B + IN_C + IN_D

kernel_name = "hybrid_parallel_groups_adaln_moe"

def rmsnorm(x, g):
    xf = x.astype(jnp.float32)
    y = xf * lax.rsqrt(jnp.mean(xf * xf, axis=-1, keepdims=True) + EPS)
    return (y * g.astype(jnp.float32)).astype(x.dtype)

def adaln(x, g, shift, scale):
    return rmsnorm(x, g) * (1 + scale) + shift

def causal_depthwise_conv(u, w):
    k = w.shape[0]
    ch = u.shape[-1]
    return lax.conv_general_dilated(
        u, w[:, None, :].astype(u.dtype), window_strides=(1,), padding=((k - 1, 0),),
        dimension_numbers=('NWC', 'WIO', 'NWC'), feature_group_count=ch)

def alibi_slopes(n):
    return 2.0 ** (-8.0 * jnp.arange(1, n + 1, dtype=jnp.float32) / n)

def short_conv_mixer(p, conv_w):
    b_gate, c_gate, xh = jnp.split(p, 3, axis=-1)
    return b_gate * causal_depthwise_conv(c_gate * xh, conv_w)

def swa_sink_attention(q, k, v, sinks):
    b, s, hq, d = q.shape
    hkv = k.shape[2]
    g = hq // hkv
    w = Q_BLOCK
    nb = s // w
    qb = q.reshape(b, nb, w, hkv, g, d)

    def with_prev(t):
        tb = t.reshape(b, nb, w, hkv, d)
        prev = jnp.pad(tb, ((0, 0), (1, 0), (0, 0), (0, 0), (0, 0)))[:, :-1]
        return jnp.concatenate([prev, tb], axis=2)

    kb, vb = with_prev(k), with_prev(v)
    scores = jnp.einsum('bnqhgd,bnkhd->bnhgqk', qb, kb).astype(jnp.float32) / math.sqrt(d)
    qi = jnp.arange(w)[:, None]
    kj = jnp.arange(2 * w)[None, :]
    dist = qi + w - kj
    key_abs = jnp.arange(nb)[:, None] * w + jnp.arange(2 * w)[None, :] - w
    valid = ((dist >= 0) & (dist < SWA_WINDOW))[None] & (key_abs >= 0)[:, None, :]
    slopes = alibi_slopes(hq).reshape(hkv, g)
    scores = scores - slopes[:, :, None, None] * dist.astype(jnp.float32)
    scores = jnp.where(valid[None, :, None, None], scores, -jnp.inf)
    sink = jnp.broadcast_to(sinks.astype(jnp.float32).reshape(hkv, g)[None, None, :, :, None, None],
                            scores.shape[:-1] + (1,))
    probs = jax.nn.softmax(jnp.concatenate([scores, sink], axis=-1), axis=-1)[..., :-1]
    out = jnp.einsum('bnhgqk,bnkhd->bnqhgd', probs.astype(v.dtype), vb)
    return out.reshape(b, s, hq * d)

def mamba2_ssd_mixer(p, conv_w, conv_b, dt_bias, a_log, d_skip, norm_g):
    f32 = jnp.float32
    b, s, _ = p.shape
    z, xbc, dt_raw = jnp.split(p, [SSM_D_INNER, SSM_D_INNER + SSM_XBC], axis=-1)
    xbc = jax.nn.silu(causal_depthwise_conv(xbc, conv_w) + conv_b)
    xs, bm, cm = jnp.split(xbc, [SSM_D_INNER, SSM_D_INNER + SSM_GROUPS * SSM_STATE], axis=-1)
    h, pd, g, n, l = SSM_HEADS, SSM_HEADDIM, SSM_GROUPS, SSM_STATE, SSM_CHUNK
    nc = s // l
    rep = h // g
    xs = xs.astype(f32).reshape(b, nc, l, h, pd)
    bm = jnp.repeat(bm.astype(f32).reshape(b, nc, l, g, n), rep, axis=3)
    cm = jnp.repeat(cm.astype(f32).reshape(b, nc, l, g, n), rep, axis=3)
    dt = jax.nn.softplus(dt_raw.astype(f32) + dt_bias.astype(f32)).reshape(b, nc, l, h)
    a = -jnp.exp(a_log.astype(f32))
    da_cum = jnp.cumsum(dt * a, axis=2)
    seg = da_cum[:, :, :, None, :] - da_cum[:, :, None, :, :]
    causal = jnp.tril(jnp.ones((l, l), dtype=bool))
    decay = jnp.exp(jnp.where(causal[None, None, :, :, None], seg, -jnp.inf))
    xdt = xs * dt[..., None]
    cb = jnp.einsum('bclhn,bcshn->bclsh', cm, bm)
    y_diag = jnp.einsum('bclsh,bcshp->bclhp', cb * decay, xdt)
    decay_to_end = jnp.exp(da_cum[:, :, -1:, :] - da_cum)
    chunk_states = jnp.einsum('bclhn,bclh,bclhp->bchpn', bm, decay_to_end, xdt)
    chunk_decay = jnp.exp(da_cum[:, :, -1, :])

    def step(state, inp):
        st, dec = inp
        return state * dec[:, :, None, None] + st, state

    init = jnp.zeros((b, h, pd, n), f32)
    _, prev_states = lax.scan(step, init, (jnp.moveaxis(chunk_states, 1, 0), jnp.moveaxis(chunk_decay, 1, 0)))
    prev_states = jnp.moveaxis(prev_states, 0, 1)
    y_off = jnp.einsum('bclhn,bchpn,bclh->bclhp', cm, prev_states, jnp.exp(da_cum))
    y = y_diag + y_off + xs * d_skip.astype(f32)[:, None]
    y = y.reshape(b, s, SSM_D_INNER) * jax.nn.silu(z.astype(f32))
    return rmsnorm(y, norm_g).astype(p.dtype)

def stick_breaking_attention(q, k, v):
    b, s, h, d = q.shape
    nb = s // Q_BLOCK
    qb = jnp.moveaxis(q.reshape(b, nb, Q_BLOCK, h, d), 1, 0)
    key_pos = jnp.arange(s)

    def block(args):
        q_blk, start = args
        z = jnp.einsum('bqhd,bkhd->bhqk', q_blk, k).astype(jnp.float32) / math.sqrt(d)
        q_pos = start + jnp.arange(Q_BLOCK)
        strict = key_pos[None, :] < q_pos[:, None]
        log_keep = jnp.where(strict, -jax.nn.softplus(z), 0.0)
        after = lax.cumsum(log_keep, axis=3, reverse=True) - log_keep
        a = jnp.where(strict, jnp.exp(jax.nn.log_sigmoid(z) + after), 0.0)
        return jnp.einsum('bhqk,bkhd->bqhd', a.astype(v.dtype), v)

    out = lax.map(block, (qb, jnp.arange(nb, dtype=jnp.int32) * Q_BLOCK))
    return jnp.moveaxis(out, 0, 1).reshape(b, s, h * d)

def hybrid_mixer(h, w_in, w_out, conv_a_w, gn_a, sinks, gn_b, ssm_conv_w, ssm_conv_b,
                 dt_bias, a_log, d_skip, ssm_norm_g, gn_d):
    b, s, _ = h.shape
    proj = h @ w_in
    pa, pb, pc, pdd = jnp.split(proj, [IN_A, IN_A + IN_B, IN_A + IN_B + IN_C], axis=-1)
    ya = rmsnorm(short_conv_mixer(pa, conv_a_w), gn_a)
    nq = SWA_HEADS * HEAD_DIM
    nkv = SWA_KV_HEADS * HEAD_DIM
    qb_, kb_, vb_ = jnp.split(pb, [nq, nq + nkv], axis=-1)
    yb = swa_sink_attention(qb_.reshape(b, s, SWA_HEADS, HEAD_DIM),
                            kb_.reshape(b, s, SWA_KV_HEADS, HEAD_DIM),
                            vb_.reshape(b, s, SWA_KV_HEADS, HEAD_DIM), sinks)
    yb = rmsnorm(yb, gn_b)
    yc = mamba2_ssd_mixer(pc, ssm_conv_w, ssm_conv_b, dt_bias, a_log, d_skip, ssm_norm_g)
    qd, kd, vd = jnp.split(pdd, 3, axis=-1)
    yd = stick_breaking_attention(qd.reshape(b, s, SB_HEADS, HEAD_DIM),
                                  kd.reshape(b, s, SB_HEADS, HEAD_DIM),
                                  vd.reshape(b, s, SB_HEADS, HEAD_DIM))
    yd = rmsnorm(yd, gn_d)
    return jnp.concatenate([ya, yb, yc, yd], axis=-1) @ w_out

def grouped_moe(h, router_w, router_bias, w_gate, w_up, w_down):
    b, s, dm = h.shape
    tokens = h.reshape(-1, dm)
    t = tokens.shape[0]
    probs = jax.nn.softmax((tokens @ router_w).astype(jnp.float32), axis=-1)
    sel = probs + router_bias.astype(jnp.float32)
    grp = sel.reshape(t, N_EXPERT_GROUPS, EXPERTS_PER_GROUP)
    grp_score = lax.top_k(grp, TOP_K)[0].sum(-1)
    _, top_grp = lax.top_k(grp_score, TOPK_GROUPS)
    grp_mask = jax.nn.one_hot(top_grp, N_EXPERT_GROUPS).sum(1) > 0
    exp_mask = jnp.repeat(grp_mask, EXPERTS_PER_GROUP, axis=1)
    _, top_e = lax.top_k(jnp.where(exp_mask, sel, -jnp.inf), TOP_K)
    gate = jnp.take_along_axis(probs, top_e, axis=-1)
    gate = gate / jnp.sum(gate, axis=-1, keepdims=True)

    flat_e = top_e.reshape(-1).astype(jnp.int32)
    flat_tok = jnp.repeat(jnp.arange(t, dtype=jnp.int32), TOP_K)
    flat_w = gate.reshape(-1)
    order = jnp.argsort(flat_e)
    se, stok, sw = flat_e[order], flat_tok[order], flat_w[order]
    counts = jnp.zeros((N_EXPERTS,), jnp.int32).at[flat_e].add(1)
    starts = jnp.cumsum(counts) - counts
    padded = (counts + MOE_BLOCK - 1) // MOE_BLOCK * MOE_BLOCK
    pad_ends = jnp.cumsum(padded)
    pad_starts = pad_ends - padded
    dest = pad_starts[se] + (jnp.arange(t * TOP_K, dtype=jnp.int32) - starts[se])
    n_blocks = -(-(t * TOP_K + N_EXPERTS * MOE_BLOCK) // MOE_BLOCK)
    cap = n_blocks * MOE_BLOCK
    buf_tok = jnp.zeros((cap,), jnp.int32).at[dest].set(stok)
    buf_w = jnp.zeros((cap,), jnp.float32).at[dest].set(sw)
    xbuf = tokens[buf_tok].reshape(n_blocks, MOE_BLOCK, dm)
    blk_start = jnp.arange(n_blocks, dtype=jnp.int32) * MOE_BLOCK
    blk_e = jnp.minimum(jnp.searchsorted(pad_ends, blk_start, side='right'), N_EXPERTS - 1)

    def expert_block(args):
        xb, e = args
        hid = jax.nn.silu(xb @ w_gate[e]) * (xb @ w_up[e])
        return hid @ w_down[e]

    yb = lax.map(expert_block, (xbuf, blk_e)).reshape(cap, dm)
    yb = yb * buf_w[:, None].astype(yb.dtype)
    out = jnp.zeros_like(tokens).at[buf_tok].add(yb)
    return out.reshape(b, s, dm)

def setup_inputs(seed: int = 0) -> dict:
    key = jax.random.key(seed)
    ks = jax.random.split(key, 32)
    f32 = jnp.float32
    L, D = DEPTH, D_MODEL

    def nrm(k, shape, scale):
        return jax.random.normal(k, shape, f32) * scale

    dt0 = jnp.exp(jax.random.uniform(ks[14], (L, SSM_HEADS), f32, math.log(1e-3), math.log(1e-1)))
    return {
        "x": nrm(ks[0], (BATCH, SEQ, D), 1.0),
        "c": nrm(ks[1], (BATCH, D), 1.0),
        "w_mod": nrm(ks[2], (L, D, N_MOD * D), 0.5 * D ** -0.5),
        "b_mod": nrm(ks[3], (L, N_MOD * D), 0.01),
        "norm1_g": 1.0 + nrm(ks[4], (L, D), 0.02),
        "norm2_g": 1.0 + nrm(ks[5], (L, D), 0.02),
        "w_in": nrm(ks[6], (L, D, IN_DIM), D ** -0.5),
        "w_out": nrm(ks[7], (L, MIX_W, D), MIX_W ** -0.5),
        "conv_a_w": nrm(ks[8], (L, CONV_A_K, CONV_A_CH), CONV_A_K ** -0.5),
        "gn_a": 1.0 + nrm(ks[9], (L, GROUP_W), 0.02),
        "attn_sinks": nrm(ks[10], (L, SWA_HEADS), 1.0),
        "gn_b": 1.0 + nrm(ks[11], (L, GROUP_W), 0.02),
        "ssm_conv_w": nrm(ks[12], (L, SSM_CONV_K, SSM_XBC), SSM_CONV_K ** -0.5),
        "ssm_conv_b": nrm(ks[13], (L, SSM_XBC), 0.01),
        "dt_bias": dt0 + jnp.log(-jnp.expm1(-dt0)),
        "a_log": jnp.log(jax.random.uniform(ks[15], (L, SSM_HEADS), f32, 1.0, 16.0)),
        "d_skip": 1.0 + nrm(ks[16], (L, SSM_HEADS), 0.1),
        "ssm_norm_g": 1.0 + nrm(ks[17], (L, SSM_D_INNER), 0.02),
        "gn_d": 1.0 + nrm(ks[18], (L, GROUP_W), 0.02),
        "router_w": nrm(ks[19], (D, N_EXPERTS), D ** -0.5),
        "router_bias": nrm(ks[20], (N_EXPERTS,), 0.01),
        "moe_w_gate": nrm(ks[21], (L, N_EXPERTS, D, D_FF), D ** -0.5),
        "moe_w_up": nrm(ks[22], (L, N_EXPERTS, D, D_FF), D ** -0.5),
        "moe_w_down": nrm(ks[23], (L, N_EXPERTS, D_FF, D), D_FF ** -0.5),
        "final_g": 1.0 + nrm(ks[24], (D,), 0.02),
    }

def reference(x, c, w_mod, b_mod, norm1_g, norm2_g, w_in, w_out, conv_a_w, gn_a, attn_sinks, gn_b,
              ssm_conv_w, ssm_conv_b, dt_bias, a_log, d_skip, ssm_norm_g, gn_d, router_w, router_bias,
              moe_w_gate, moe_w_up, moe_w_down, final_g):
    b = x.shape[0]
    cond = jax.nn.silu(c)
    for l in range(DEPTH):
        mod = (cond @ w_mod[l] + b_mod[l]).reshape(b, N_MOD, 1, D_MODEL)
        h = adaln(x, norm1_g[l], mod[:, 0], mod[:, 1])
        mix = hybrid_mixer(h, w_in[l], w_out[l], conv_a_w[l], gn_a[l], attn_sinks[l], gn_b[l],
                           ssm_conv_w[l], ssm_conv_b[l], dt_bias[l], a_log[l], d_skip[l],
                           ssm_norm_g[l], gn_d[l])
        x = x + mod[:, 2] * mix
        h = adaln(x, norm2_g[l], mod[:, 3], mod[:, 4])
        x = x + mod[:, 5] * grouped_moe(h, router_w, router_bias, moe_w_gate[l], moe_w_up[l], moe_w_down[l])
    return rmsnorm(x, final_g)


_drawn_inputs = setup_inputs


def setup_inputs(seed=0):
    import zlib

    import numpy as np

    out = dict(_drawn_inputs(seed))
    spreads = {}
    factors = {'gn_a': 35.52,
     'gn_b': 41.034,
     'ssm_conv_b': 4.682,
     'ssm_norm_g': 43.319,
     'gn_d': 33.188,
     'final_g': 8.312,
     'norm2_g': 4.732}
    for name, (base, spread) in spreads.items():
        noise = np.random.default_rng([zlib.crc32(name.encode()), seed]).standard_normal(out[name].shape)
        drawn = base * np.exp(spread * noise) if base else spread * noise
        out[name] = __import__('jax').numpy.asarray(drawn.astype(out[name].dtype))
    for name, factor in factors.items():
        out[name] = (out[name] * factor).astype(out[name].dtype)
    return out
```

```python
from contextlib import ExitStack

import numpy as np
import concourse.bass as bass
from concourse import mybir

F32 = mybir.dt.float32
I32 = mybir.dt.int32
ALU = mybir.AluOpType
ACT = mybir.ActivationFunctionType
AX = mybir.AxisListType.X

D = 2048
SEQ = 256
P = 128
NT = SEQ // P
KT = D // P
GW = 512
NE = 16
FF = 1024
EXPERT = D * FF
EPS = 1e-6
SLOT = 4096
NSLOT = 6
NSLOT_B = 4
XH = 64
NOVER = 4
NV = NE + NOVER
BIG = 1e30

A_B, A_C, A_X = 0, 512, 1024
B_Q, B_KV = 1536, 2048
C_Z, C_XS, C_BC, C_DT = 2304, 2816, 3328, 3840
D_Q, D_K, D_V = 3848, 4360, 4872
GROUPS = [D_Q, D_K, D_V, C_XS, C_BC, B_Q, B_KV, C_Z, A_B, A_C, A_X]
G_DQ, G_DK, G_DV, G_XS, G_BC, G_BQ, G_BKV, G_Z, G_AB, G_AC, G_AX = range(11)

STEPS = [
    ("g", 0, 0), ("g", 0, 1), ("g", 1, 0), ("g", 1, 1), ("D1", 0), ("g", 2, 0), ("D2", 0), ("g", 2, 1),
    ("D3", 0), ("g", 3, 0), ("D1", 1), ("g", 3, 1), ("D2", 1), ("g", 4, 0), ("D3", 1), ("g", 4, 1),
    ("N", 3), ("DT", 0), ("g", 5, 0), ("C0", 0), ("g", 5, 1), ("C1", 0), ("g", 6, 1), ("C2", 0),
    ("g", 7, 0), ("C1", 1), ("g", 7, 1), ("C2", 1), ("g", 8, 0), ("N", 2), ("g", 8, 1), ("B1", 0),
    ("g", 9, 0), ("B2", 0), ("g", 9, 1), ("B3", 0), ("g", 10, 0), ("B1", 1), ("g", 10, 1), ("B2", 1),
    ("wo", 0, 0), ("B3", 1), ("wo", 1, 0), ("N", 1), ("N", 0), ("M2", 0), ("wo", 0, 1), ("M2", 1),
    ("wo", 1, 1), ("wo", 2, 0), ("wo", 2, 1), ("wo", 3, 0), ("wo", 3, 1), ("M3", 0), ("M3", 1),
]


def stream():
    items = [("mod", 0, k) for k in range(KT)]
    left = [("mod", r, k) for r in (1, 2) for k in range(KT)]
    n = 0
    for s in STEPS:
        if s[0] in ("g", "wo"):
            items.append(s)
            for _ in range(2 if n < 4 else 1):
                if left:
                    items.append(left.pop(0))
            n += 1
    assert not left
    return items


def trunk(nc, x, c, w_mod, b_mod, norm1_g, norm2_g, w_in, w_out, conv_a_w, gn_a, attn_sinks, gn_b,
          ssm_conv_w, ssm_conv_b, dt_bias, a_log, d_skip, ssm_norm_g, gn_d, router_w, router_bias,
          moe_w_gate, moe_w_up, moe_w_down, final_g, out):
    ctx = ExitStack()
    with ctx:
        mem = ctx.enter_context(nc.sbuf_tensor("mem", [P, 53120], F32))
        itab = ctx.enter_context(nc.sbuf_tensor("itab", [1, 64], I32))
        ps = ctx.enter_context(nc.psum_tensor("ps", [P, 4096], F32))

        def at(start, *shape):
            n = int(np.prod(shape))
            a = mem[:, start:start + n]
            if len(shape) == 2:
                a = a.rearrange("p (a b) -> p a b", b=shape[1])
            elif len(shape) == 3:
                a = a.rearrange("p (a b c) -> p a b c", b=shape[1], c=shape[2])
            return a

        def bank(b, n=1):
            return ps[:, 512 * b:512 * (b + n)]

        H1 = NSLOT * SLOT
        ACC_A, ACC_B = H1 + 4096, H1 + 8192
        REST = H1 + 12288
        X1, YT, XG, CONST = REST, REST + 4096, REST + 8192, REST + 8192 + 6144
        WC = NSLOT_B * SLOT
        WD = WC + 5120

        h1T = at(H1, KT, SEQ)
        acc = [at(ACC_A, 4096), at(ACC_B, 4096), at(ACC_A, 4096)]
        xtok = at(X1, NT, D)
        yT = at(YT, KT, SEQ)
        dq, dk, dv = at(X1, 4, SEQ), at(X1 + 1024, 4, SEQ), at(X1 + 2048, NT, GW)
        ab, ac, au = at(X1, 4, SEQ), at(X1 + 1024, 4, SEQ), at(X1 + 2048, 4, SEQ + 2)
        kdup = at(X1 + 3088, 2, SEQ)
        xraw = at(XG, 8, SEQ + 3)
        zg = at(XG, 4, SEQ)
        xc = at(XG + 2072, 8, SEQ)
        bq = at(XG + 4120, 4, SEQ)
        rstd_b = at(XG + 5144, SEQ)
        vB = at(XG + 5400, NT, P)
        params = at(XG, P)
        wo_tmp = at(XG, NT, GW)
        da_u = at(WC, 8, P)
        seg = at(WC + 1024, 8, P)
        cum_e = at(WC + 2048, 8, P)
        cbm = at(WC + 3072, 2, P)
        bm_tok = at(WC + 3328, 2 * P)
        xdt = at(WC + 3584, 8, 64)
        xw = at(WC + 4096, 8, 64)
        state = at(WC + 4608, 8, 64)
        s_a, s_b = at(WD, 4, SEQ), at(WD + 1024, 4, P)
        t_a, t_b = at(WD + 1536, 4, SEQ), at(WD + 2560, 4, P)
        s_all, t_all = at(WD, 1536), at(WD + 1536, 1536)
        x1 = xtok
        h2 = at(YT, NT, D)
        h2T = h1T
        xg = [at(XG + 3072 * u, KT, 192) for u in range(2)]
        y_sb = at(H1, D)
        pos1h = at(H1 + 2048, NT, P)
        gate1h = at(H1 + 2304, NT, 192)
        RT = H1 + 2688
        rt = [RT]

        def route(*shape):
            a = at(rt[0], *shape)
            rt[0] += int(np.prod(shape))
            return a

        probs, sel, chosen, second, gates, pos, posq = (route(NT, NE) for _ in range(7))
        gsc, gmask, q4, g8b, r1 = route(NT, 4), route(NT, 4), route(7, 8), route(8), route(NT)
        wdesc, cnt, cntq, ovr, ovc, ovx = (route(NE) for _ in range(6))
        ovm, ovt = route(NOVER, NE), route(NOVER, NE)
        ova, ove, ovo, flags = route(NOVER), route(NOVER), route(NOVER), route(64)
        posx_at = rt[0]
        posx = route(NV + 1, NT)
        gatex_at = rt[0]
        gatex = route(NV + 1, NT)
        assert rt[0] <= H1 + 4096, rt[0] - H1
        pgT = [at(ACC_B + 512 * u, 4, P) for u in range(2)]
        hid = at(ACC_B + 1024, FF)
        hidT = at(ACC_B + 2048, 8, 192)
        n2g_b = at(H1, D)
        junk = at(H1 + 2048, D)
        scale2_b, gate2_b = at(ACC_A, D), at(ACC_A + D, D)
        gate1_b, shift2_b = at(ACC_B, D), at(ACC_B + D, D)
        fin_b = at(ACC_A, D)

        cur = [CONST]

        def small(*shape):
            a = at(cur[0], *shape)
            cur[0] += int(np.prod(shape))
            return a

        ident, ones = small(P), small(P)
        upper = small(P)
        lower = small(P)
        strict = small(P)
        dist = small(SEQ)
        iota = small(192)
        cols = small(P)
        rw = small(KT, NE)
        wdt = small(KT, 8)
        dtb, alog, sink, rbias, dsk8, dsk = small(8), small(8), small(8), small(NE), small(8), small(4)
        cond, mod1, a1 = small(16), small(32), small(16)
        ss, rs, eps = small(2), small(2), small(1)
        dtv, dtw, dt, da, cum = small(16), small(16), small(16), small(16), small(16)
        ea, d2e = small(8), small(8)
        mx, den, es = small(8), small(8), small(8)
        assert cur[0] <= 53120, cur[0]
        squares = [ac, at(WD + 1536, 4, SEQ), at(WC + 1024, 4, SEQ), at(WD + 1536, 4, SEQ)]
        c_c, c_n1, c_ca, c_cw, c_cb = 0, 16, 32, 44, 76
        c_gn = [84, 88, 92, 96]
        NPAR = 100

        sems = {}

        def ev(name):
            if name not in sems:
                sems[name] = ctx.enter_context(nc.semaphore(name))
            return sems[name]

        ITEMS = stream()
        where = {it: n for n, it in enumerate(ITEMS)}
        NITEMS = len(ITEMS)
        slot_full = [ev(f"slot_full{s}") for s in range(NSLOT)]
        mod_used, proj_used = ev("mod_used"), ev("proj_used")
        mods = [it for it in ITEMS if it[0] == "mod"]
        pes = [it for it in ITEMS if it[0] != "mod"]
        mod_no = {it: n for n, it in enumerate(mods)}
        pe_no = {it: n for n, it in enumerate(pes)}
        FILLS = [len(range(s, NITEMS, NSLOT_B)) if s < NSLOT_B else 0 for s in range(NSLOT)]

        def used(it):
            return (mod_used, mod_no[it] + 1) if it[0] == "mod" else (proj_used, pe_no[it] + 1)

        def arrived(eng, it):
            n = where[it]
            eng.wait_ge(slot_full[n % NSLOT_B], 16 * (n // NSLOT_B + 1))
            return at((n % NSLOT_B) * SLOT, SLOT)

        def bcast_rows(src, n, rows=P):
            return bass.AP(src.tensor, src.offset, [[0, rows], [1, n]])

        def loop_sems(tag):
            return {n: ev(f"{tag}_{n}") for n in (
                "slot_used", "onehot_ready", "gathered", "xg_ready", "pg_transposed", "pg_ready", "silu_done",
                "hid_ready", "hid_transposed", "hidT_act", "hidT_dve", "y_ready", "combined", "added")}

        main, over = loop_sems("main"), loop_sems("over")

        block = ctx.enter_context(nc.Block())

        @block.sync
        def _(sp):
            sp.dma_start(mem[0:16, XG:XG + P], c.rearrange("b (k p) -> (b k) p", p=P)).then_inc(ev("params_in"), 16)
            sp.dma_start(mem[16:32, XG:XG + P], norm1_g.rearrange("b (k p) -> (b k) p", p=P)).then_inc(ev("params_in"), 16)
            sp.dma_start(mem[32:44, XG:XG + P], conv_a_w.rearrange("b w (k p) -> (b w k) p", p=P)).then_inc(ev("params_in"), 16)
            sp.dma_start(mem[44:76, XG:XG + P], ssm_conv_w.rearrange("b w (k p) -> (b w k) p", p=P)).then_inc(ev("params_in"), 16)
            sp.dma_start(mem[76:84, XG:XG + P], ssm_conv_b.rearrange("b (k p) -> (b k) p", p=P)).then_inc(ev("params_in"), 16)
            for i, g in enumerate((gn_a, gn_b, ssm_norm_g, gn_d)):
                sp.dma_start(mem[84 + 4 * i:88 + 4 * i, XG:XG + P], g.rearrange("b (k p) -> (b k) p", p=P)).then_inc(ev("params_in"), 16)
            for n, it in enumerate(ITEMS):
                if n >= NSLOT_B:
                    sp.wait_ge(*used(ITEMS[n - NSLOT_B]))
                dst = at((n % NSLOT_B) * SLOT, SLOT)
                if it[0] == "mod":
                    _, r, k = it
                    src = w_mod[0, k * P:(k + 1) * P, r * 4096:(r + 1) * 4096]
                elif it[0] == "g":
                    _, g, half = it
                    if g == G_BKV:
                        dst = dst.rearrange("p (k n) -> p k n", n=256)
                        src = w_in[0, :, B_KV:B_KV + 256].rearrange("(k p) n -> p k n", p=P)
                    else:
                        dst = dst.rearrange("p (k n) -> p k n", n=512)
                        src = w_in[0, half * 1024:(half + 1) * 1024, GROUPS[g]:GROUPS[g] + 512]\
                            .rearrange("(k p) n -> p k n", p=P)
                else:
                    _, n4, half = it
                    r0 = 1024 * (1 - half)
                    dst = dst.rearrange("p (k n) -> p k n", n=512)
                    src = w_out[0, r0:r0 + 1024, n4 * 512:(n4 + 1) * 512].rearrange("(k p) n -> p k n", p=P)
                sp.dma_start(dst, src).then_inc(slot_full[n % NSLOT_B], 16)

            def expert_chunk(j, start, sem=None, count=None):
                w, cols_w = (moe_w_down, D) if j >= 8 else ((moe_w_gate, moe_w_up)[j % 2], FF)
                tiles = SLOT // cols_w
                r0 = (j - 8) * tiles * P if j >= 8 else (j // 2) * tiles * P
                if sem is not None:
                    sp.wait_ge(sem, count)
                src = bass.AP(w.tensor, start + r0 * cols_w, [[cols_w, P], [P * cols_w, tiles], [1, cols_w]])
                dst = at((j % NSLOT) * SLOT, SLOT).rearrange("p (k n) -> p k n", n=cols_w)
                sp.dma_start(dst, src).then_inc(slot_full[j % NSLOT], 16)

            for j in range(NSLOT):
                if j < NSLOT_B:
                    last = max(n for n in range(NITEMS) if n % NSLOT_B == j)
                    sp.wait_ge(*used(ITEMS[last]))
                elif j == NSLOT_B:
                    sp.wait_ge(ev("N_scaled0"), 1)
                    sp.wait_ge(ev("N_scaled1"), 1)
                    sp.wait_ge(ev("N_scaled2"), 1)
                    sp.wait_ge(ev("N_scaled3"), 1)
                expert_chunk(j, 0)
            with sp.Fori(0, NE // 2 - 1) as i:
                starts = [(i * 2 + q) * EXPERT for q in range(3)]
                starts_down = [i * (2 * EXPERT) + q * EXPERT for q in range(3)]
                for m in range(24):
                    q, j = divmod(m + 6, 12)
                    expert_chunk(j, (starts if j < 8 else starts_down)[q], main["slot_used"], i * 24 + (m + 1))
            for m in range(24 * (NE // 2 - 1), 12 * NE - 6):
                sp.wait_ge(main["slot_used"], m + 1)
                expert_chunk((m + 6) % 12, (m + 6) // 12 * EXPERT)
            sp.wait_ge(ev("main_done"), 1)
            n_over = sp.value_load(itab[0:1, 0:1], min_val=0, max_val=NOVER)
            with sp.If(n_over > 0):
                def first_element(at_v):
                    e = sp.value_load(itab[0:1, bass.ds(at_v, 1)], min_val=0, max_val=NE - 1)
                    return e * EXPERT, (e * 2) * (EXPERT // 2)

                start = first_element(32)
                for j in range(NSLOT):
                    expert_chunk(j, start[0])
                with sp.Fori(0, NOVER - 1) as v:
                    here, after = first_element(v + 32), first_element(v + 33)
                    for m in range(12):
                        q, j = divmod(m + 6, 12)
                        expert_chunk(j, (after if q else here)[j // 8], over["slot_used"], v * 12 + (m + 1))
                start = first_element(32 + NOVER - 1)
                for j in range(NSLOT, 12):
                    expert_chunk(j, start[j // 8], over["slot_used"], 12 * (NOVER - 1) + j - NSLOT + 1)
            sp.wait_ge(ev("out_ready0"), 1)
            sp.dma_start(out[0, 0:P, :], x1[:, 0, :]).then_inc(ev("out_written"), 16)
            sp.wait_ge(ev("out_ready1"), 1)
            sp.dma_start(out[0, P:SEQ, :], x1[:, 1, :]).then_inc(ev("out_written"), 16)
            sp.wait_ge(ev("out_written"), 32)

        @block.gpsimd
        def _(pool):
            nc.gpsimd.memset(acc[0], 0.0).then_inc(ev("acc_zeroed0"), 1)
            nc.gpsimd.memset(acc[1], 0.0).then_inc(ev("acc_zeroed1"), 1)
            nc.gpsimd.memset(ident, 0.0)
            nc.gpsimd.memset(upper, 1.0)
            nc.gpsimd.memset(lower, 1.0)
            nc.gpsimd.memset(strict, 1.0)
            nc.gpsimd.memset(ones, 1.0).then_inc(ev("masks_filled"), 1)
            pool.wait_ge(ev("masks_filled"), 1)

            def select(m, op, fill, base, step, mult, name):
                nc.gpsimd.affine_select(out=m, in_=m, compare_op=op, fill=fill, base=base,
                                        pattern=[[step, m.shape[1]]], channel_multiplier=mult)\
                  .then_inc(ev(name), 1)

            select(ident, ALU.not_equal, 1.0, 0, -1, 1, "ident_ready")
            select(upper, ALU.is_ge, 0.0, 0, 1, -1, "masks_ready")
            select(lower, ALU.is_ge, 0.0, 0, -1, 1, "masks_ready")
            select(strict, ALU.is_gt, 0.0, 0, 1, -1, "masks_ready")
            nc.gpsimd.iota(dist, pattern=[[-1, SEQ]], base=P, channel_multiplier=1,
                           allow_small_or_imprecise_dtypes=True).then_inc(ev("dist_filled"), 1)
            pool.wait_ge(ev("dist_filled"), 1)
            select(dist, ALU.is_ge, BIG, P, -1, 1, "dist_cut")
            pool.wait_ge(ev("dist_cut"), 1)
            select(dist, ALU.is_gt, BIG, 0, 1, -1, "masks_ready")
            nc.gpsimd.iota(iota[:, 0:P], pattern=[[1, P]], base=0, channel_multiplier=0,
                           allow_small_or_imprecise_dtypes=True)
            nc.gpsimd.iota(iota[:, P:192], pattern=[[1, XH]], base=0, channel_multiplier=0,
                           allow_small_or_imprecise_dtypes=True).then_inc(ev("masks_ready"), 1)
            pool.wait_ge(ev("mod_cols"), 1)
            nc.gpsimd.memset(acc[2], 0.0).then_inc(ev("acc_zeroed2"), 1)

        @block.scalar
        def _(act):
            links = [0]

            def link(ins):
                links[0] += 1
                ins.then_inc(ev("act_link"), 1)
                act.wait_ge(ev("act_link"), links[0])

            act.dma_start(xtok, x[0].rearrange("(t p) d -> p t d", p=P)).then_inc(ev("x_in"), 16)
            act.wait_ge(ev("acc_zeroed0"), 1)
            act.dma_start(acc[0][0:1, :], b_mod[:, 0:4096]).then_inc(ev("bias_in0"), 16)
            act.wait_ge(ev("acc_zeroed1"), 1)
            act.dma_start(acc[1][0:1, :], b_mod[:, 4096:8192]).then_inc(ev("bias_in1"), 16)
            act.dma_start(wdt, w_in[0, :, C_DT:C_DT + 8].rearrange("(k p) n -> p k n", p=P)).then_inc(ev("small_in"), 16)
            act.dma_start(rw, router_w.rearrange("(k p) n -> p k n", p=P)).then_inc(ev("small_in"), 16)
            act.dma_start(dtb, dt_bias[0].partition_broadcast(P)).then_inc(ev("small_in"), 16)
            act.dma_start(alog, a_log[0].partition_broadcast(P)).then_inc(ev("small_in"), 16)
            act.dma_start(sink, attn_sinks[0].partition_broadcast(P)).then_inc(ev("small_in"), 16)
            act.dma_start(rbias, router_bias.partition_broadcast(P)).then_inc(ev("small_in"), 16)
            act.dma_start(dsk8, d_skip[0].partition_broadcast(P)).then_inc(ev("small_in"), 16)

            act.wait_ge(ev("params_T"), 1)
            nc.scalar.activation(cols[:, 0:NPAR], bank(0)[:, 0:NPAR], ACT.Copy).then_inc(ev("cols_ready"), 1)
            act.wait_ge(ev("cols_ready"), 1)
            nc.scalar.activation(cond, cols[:, 0:16], ACT.Silu).then_inc(ev("cond_ready"), 1)
            act.wait_ge(ev("x_in"), 16)
            for t in range(NT):
                link(nc.scalar.activation(at(H1, D), xtok[:, t, :], ACT.Square, accum_out=ss[:, t:t + 1]))
            act.wait_ge(ev("eps_ready"), 1)
            nc.scalar.activation(rs, ss, ACT.Sqrt, scale=1.0 / D, bias=eps).then_inc(ev("rms1"), 1)
            for b in range(4):
                act.wait_ge(ev("xT"), b + 1)
                nc.scalar.activation(h1T[:, 4 * b:4 * b + 4, :], bank(2 * b, 2).rearrange("p (k n) -> p k n", n=SEQ),
                                     ACT.Copy).then_inc(ev("h1_raw"), 1)
            act.wait_ge(ev("acc_zeroed2"), 1)
            act.dma_start(acc[2][0:1, :], b_mod[:, 8192:12288]).then_inc(ev("bias_in2"), 16)

            dest = {G_DQ: (dq, 0.125), G_DK: (dk, 1.0), G_DV: (dv, 1.0), G_XS: (xraw[:, 0:4, 3:], 1.0),
                    G_BC: (xraw[:, 4:8, 3:], 1.0), G_BQ: (bq, 0.125), G_Z: (zg, 1.0), G_AB: (ab, 1.0),
                    G_AC: (ac, 1.0)}
            for s in STEPS:
                k, n = s[0], s[1]
                if k == "g" and s[2] == 1:
                    two = bank(2 * (n % 2), 2)
                    if n == G_AX:
                        continue
                    act.wait_ge(proj_used, pe_no[s] + 1)
                    if n == G_BKV:
                        nc.scalar.activation(kdup, two[:, 0:512].rearrange("p (g n) -> p g n", n=SEQ), ACT.Copy)
                        ins = nc.scalar.activation(vB, two[:, 512:768].rearrange("p (t n) -> p t n", n=P), ACT.Copy)
                    elif n == G_DV:
                        ins = nc.scalar.activation(dv, two.rearrange("p (t n) -> p t n", n=GW), ACT.Copy)
                    else:
                        if n in (G_AB, G_AC):
                            act.wait_ge(ev("D_out"), 2)
                        if n == G_Z:
                            act.wait_ge(ev("conv_done"), 1)
                        d, sc = dest[n]
                        f = ACT.Silu if n == G_Z else ACT.Copy
                        ins = nc.scalar.activation(d, two.rearrange("p (k n) -> p k n", n=SEQ), f, scale=sc)
                    ins.then_inc(ev("group_out"), 1)
                elif k == "D1":
                    act.wait_ge(ev("D_scores"), n + 1)
                    if n == 1:
                        act.wait_ge(ev("D_out"), 1)
                    nc.scalar.activation(s_a, bank(4, 2).rearrange("p (h n) -> p h n", n=SEQ), ACT.Copy)
                    nc.scalar.activation(s_b.rearrange("p (a h) n -> p a h n", a=2),
                                         bank(6, 2).rearrange("p (a h n) -> p a h n", a=2, n=P)[:, :, 0:2, :],
                                         ACT.Copy).then_inc(ev("D_scores_out"), 1)
                    act.wait_ge(ev("D_scores_out"), n + 1)
                    link(nc.scalar.activation(t_all, s_all, ACT.Abs))
                    link(nc.scalar.activation(t_all, t_all, ACT.Exp, scale=-1.0))
                    nc.scalar.activation(t_all, t_all, ACT.Ln, bias=1.0).then_inc(ev("D_ln"), 1)
                elif k == "D2":
                    act.wait_ge(ev("D_logw"), n + 1)
                    nc.scalar.activation(s_all, s_all, ACT.Exp).then_inc(ev("D_exp"), 1)
                elif k in ("D3", "B3"):
                    act.wait_ge(ev(k[0] + "_mixed"), n + 1)
                    t0 = (12 if k == "D3" else 4) + 2 * n
                    nc.scalar.activation(yT[:, t0:t0 + 2, :], bank(7).rearrange("p (j n) -> p j n", n=SEQ),
                                         ACT.Copy).then_inc(ev(k[0] + "_out"), 1)
                elif k == "N":
                    act.wait_ge(ev(f"N_summed{n}"), 1)
                    nc.scalar.activation(rstd_b, bank(4)[:, 0:SEQ], ACT.Sqrt, scale=1.0 / GW, bias=eps)\
                      .then_inc(ev(f"N_root{n}"), 1)
                elif k == "DT":
                    act.wait_ge(ev("dt_raw"), 1)
                    act.wait_ge(ev("small_in"), 112)
                    link(nc.scalar.activation(dtw, dtv, ACT.Abs))
                    nc.scalar.activation(ea, alog, ACT.Exp)
                    link(nc.scalar.activation(dtw, dtw, ACT.Exp, scale=-1.0))
                    nc.scalar.activation(dtw, dtw, ACT.Ln, bias=1.0).then_inc(ev("dt_ln"), 1)
                    act.wait_ge(ev("conv_done"), 1)
                    nc.scalar.activation(xc, xc, ACT.Silu).then_inc(ev("xc_ready"), 1)
                elif k == "C1":
                    act.wait_ge(ev("C_seg"), n + 1)
                    nc.scalar.activation(seg, seg, ACT.Exp).then_inc(ev("C_exp"), 1)
                    if n == 0:
                        nc.scalar.activation(d2e, d2e, ACT.Exp).then_inc(ev("C_exp2"), 1)
                    else:
                        nc.scalar.activation(cum_e, cum_e, ACT.Exp).then_inc(ev("C_exp2"), 1)
                elif k == "C2" and n == 0:
                    act.wait_ge(ev("C_state"), 1)
                    nc.scalar.activation(state, bank(6).rearrange("p (h n) -> p h n", n=64), ACT.Copy)\
                      .then_inc(ev("C_state_out"), 1)
                elif k == "B1":
                    act.wait_ge(ev("B_shifted"), n + 1)
                    nc.scalar.activation(s_all, s_all, ACT.Exp)
                    nc.scalar.activation(es, es, ACT.Exp).then_inc(ev("B_exp"), 1)
                elif k == "B2":
                    act.wait_ge(ev("B_probsT"), n + 1)
                    nc.scalar.activation(t_a, bank(4, 2).rearrange("p (h n) -> p h n", n=SEQ), ACT.Copy)
                    nc.scalar.activation(t_b, bank(6).rearrange("p (h n) -> p h n", n=P), ACT.Copy)\
                      .then_inc(ev("B_probsT_out"), 1)
                elif k in ("M2", "M3"):
                    a = acc[1] if k == "M2" else acc[2]
                    act.wait_ge(ev(k + "_summed"), n + 1)
                    nc.scalar.activation(a[:, n * D:(n + 1) * D], bank(4, 4), ACT.Copy).then_inc(ev(k + "_out"), 1)
                if s == ("N", 0):
                    act.wait_ge(ev("N_scaled0"), 1)
                    act.wait_ge(ev("B_scores"), 2)
                    act.wait_ge(ev("D_mixed"), 2)
                    act.dma_start(xtok, x[0].rearrange("(t p) d -> p t d", p=P)).then_inc(ev("x_in"), 16)
                    act.wait_ge(proj_used, pe_no[("g", 10, 1)] + 1)
                    act.dma_start(n2g_b, norm2_g[0].partition_broadcast(P)).then_inc(ev("n2g_in"), 16)

            act.wait_ge(ev("x1_ready"), 4)
            for t in range(NT):
                link(nc.scalar.activation(junk, x1[:, t, :], ACT.Square, accum_out=ss[:, t:t + 1]))
            nc.scalar.activation(rs, ss, ACT.Sqrt, scale=1.0 / D, bias=eps).then_inc(ev("rms2"), 1)
            act.wait_ge(ev("h2_ready"), 2)
            act.dma_start(fin_b, final_g.partition_broadcast(P)).then_inc(ev("fin_in"), 16)
            for b in range(4):
                act.wait_ge(ev("h2T"), b + 1)
                nc.scalar.activation(h2T[:, 4 * b:4 * b + 4, :], bank(2 * b, 2).rearrange("p (k n) -> p k n", n=SEQ),
                                     ACT.Copy).then_inc(ev("h2T_out"), 1)
            act.wait_ge(ev("r_shifted"), 1)
            nc.scalar.activation(probs, probs, ACT.Exp).then_inc(ev("r_exp"), 1)

            def take_gathered(L, u, count):
                act.wait_ge(L["gathered"], count)
                src = bank(4, 4).rearrange("p (k n) -> p k n", n=P)
                nc.scalar.activation(xg[u][:, :, 0:P], src, ACT.Copy)
                nc.scalar.activation(xg[u][:, :, P:192], src[:, :, 0:XH], ACT.Copy).then_inc(L["xg_ready"], 1)

            def expert(L, i, u):
                take_gathered(L, 1 - u, i * 2 + (u + 2))
                act.wait_ge(L["slot_used"], i * 24 + (12 * u + 8))
                nc.scalar.activation(hid, bank(0, 2), ACT.Silu).then_inc(L["silu_done"], 1)
                act.wait_ge(L["hid_transposed"], i * 2 + (u + 1))
                src = bank(4).rearrange("p (f n) -> p f n", n=P)
                nc.scalar.activation(hidT[:, 0:4, 0:P], src, ACT.Copy)
                nc.scalar.activation(hidT[:, 0:4, P:192], src[:, :, 0:XH], ACT.Copy).then_inc(L["hidT_act"], 1)

            take_gathered(main, 0, 1)
            with act.Fori(0, NE // 2) as i:
                for u in range(2):
                    expert(main, i, u)
            act.wait_ge(ev("main_done"), 1)
            n_over = act.value_load(itab[0:1, 0:1], min_val=0, max_val=NOVER)
            with act.If(n_over > 0):
                take_gathered(over, 0, 1)
                with act.Fori(0, NOVER // 2) as i:
                    for u in range(2):
                        expert(over, i, u)
            act.wait_ge(ev("x1_final"), 1)
            for t in range(NT):
                link(nc.scalar.activation(h2[:, t, :], x1[:, t, :], ACT.Square, accum_out=ss[:, t:t + 1]))
            nc.scalar.activation(rs, ss, ACT.Sqrt, scale=1.0 / D, bias=eps).then_inc(ev("rms3"), 1)

        @block.tensor
        def _(pe):
            mm, tr = nc.tensor.matmul, nc.tensor.transpose
            pe.wait_ge(ev("params_in"), 144)
            pe.wait_ge(ev("ident_ready"), 1)
            tr(bank(0)[:, 0:NPAR], params[0:NPAR, :], ident[0:NPAR, 0:NPAR]).then_inc(ev("params_T"), 1)
            pe.wait_ge(ev("xn_ready"), 2)
            for b in range(4):
                if b == 0:
                    pe.wait_ge(ev("cols_ready"), 1)
                for kk in range(4):
                    for t in range(NT):
                        k = 4 * b + kk
                        ins = tr(bank(2 * b, 2)[:, kk * SEQ + t * P:kk * SEQ + (t + 1) * P],
                                 xtok[:, t, k * P:(k + 1) * P], ident)
                ins.then_inc(ev("xT"), 1)
            pe.wait_ge(mod_used, 16)
            pe.wait_ge(ev("h1_raw"), 1)
            for j in range(32):
                ins = mm(bank(0)[:, j:j + 1], acc[0][:, j * P:(j + 1) * P], ones[:, 0:1], start=True, stop=True)
            ins.then_inc(ev("mod_summed"), 1)
            pe.wait_ge(ev("h1_ready"), 1)

            def group(g, half):
                if half == 0 or g == G_BKV:
                    if g >= 2:
                        pe.wait_ge(ev("group_out"), g - 1)
                    elif g == 0:
                        pe.wait_ge(ev("mod_cols"), 1)
                    if g == 1:
                        pe.wait_ge(ev("h1_raw"), 4)
                w = arrived(pe, ("g", g, half))
                two = bank(2 * (g % 2), 2)
                if g == G_BKV:
                    w = w.rearrange("p (k n) -> p k n", n=256)
                    kk, vv = two[:, 0:512].rearrange("p (g n) -> p g n", n=SEQ), two[:, 512:768]
                    for kv in range(2):
                        for k in range(KT):
                            for a in range(2):
                                mm(kk[64 * a:64 * a + 64, kv, :], w[:, k, 64 * kv:64 * kv + 64], h1T[:, k, :],
                                   start=(k == 0), stop=(k == KT - 1))
                    for t in range(NT):
                        for k in range(KT):
                            ins = mm(vv[:, t * P:(t + 1) * P], h1T[:, k, t * P:(t + 1) * P], w[:, k, P:256],
                                     start=(k == 0), stop=(k == KT - 1))
                    ins.then_inc(proj_used, 1)
                    return
                w = w.rearrange("p (k n) -> p k n", n=512)
                if g == G_DV:
                    for t in range(NT):
                        for kk in range(8):
                            k = 8 * half + kk
                            ins = mm(two[:, t * 512:(t + 1) * 512], h1T[:, k, t * P:(t + 1) * P], w[:, kk, :],
                                     start=(k == 0), stop=(k == KT - 1))
                else:
                    for kk in range(8):
                        for m in range(4):
                            k = 8 * half + kk
                            ins = mm(two[:, m * SEQ:(m + 1) * SEQ], w[:, kk, m * P:(m + 1) * P], h1T[:, k, :],
                                     start=(k == 0 and m % 2 == 0), stop=(k == KT - 1 and m % 2 == 1),
                                     skip_group_check=True)
                ins.then_inc(proj_used, 1)

            def both(n):
                return bank(n).rearrange("p (j n) -> p j n", n=P)

            def values(w_a, w_b, v, head, done):
                for j in range(2):
                    for a in range(2):
                        o = bank(7)[64 * a:64 * a + 64, j * SEQ:(j + 1) * SEQ]
                        h = head(j, a)
                        mm(o, v[:, 0, h * 64:h * 64 + 64], w_a[:, 2 * a + j, :], start=True, stop=False)
                        ins = mm(o[:, P:SEQ], v[:, 1, h * 64:h * 64 + 64], w_b[:, 2 * a + j, :],
                                 start=False, stop=True)
                ins.then_inc(ev(done), 1)

            for s in STEPS:
                k, n = s[0], s[1]
                if k == "g":
                    group(n, s[2])
                elif k == "D1":
                    pe.wait_ge(ev("group_out"), 2)
                    if n == 0:
                        pe.wait_ge(ev("h1_raw"), 4)
                    else:
                        pe.wait_ge(ev("D_logw"), 1)
                        pe.wait_ge(ev("D_out"), 1)
                    for j in range(2):
                        for a in range(2):
                            kT, qT = dk[64 * a:64 * a + 64, 2 * n + j, :], dq[64 * a:64 * a + 64, 2 * n + j, :]
                            mm(bank(4 + a)[:, j * SEQ:(j + 1) * SEQ], kT[:, 0:P], qT, start=True, stop=True)
                    for j in range(2):
                        for a in range(2):
                            kT, qT = dk[64 * a:64 * a + 64, 2 * n + j, :], dq[64 * a:64 * a + 64, 2 * n + j, :]
                            ins = mm(bank(6 + a)[:, j * P:(j + 1) * P], kT[:, P:SEQ], qT[:, P:SEQ],
                                     start=True, stop=True)
                    ins.then_inc(ev("D_scores"), 1)
                elif k == "D2":
                    pe.wait_ge(ev("D_softp"), n + 1)
                    for a in range(2):
                        mm(bank(4 + a), lower, t_a[:, 2 * a:2 * a + 2, :], start=True, stop=False)
                        mm(bank(4 + a).rearrange("p (j n) -> p j n", n=SEQ)[:, :, P:SEQ], ones,
                           t_b[:, 2 * a:2 * a + 2, :], start=False, stop=True)
                    mm(bank(6), lower, t_b, start=True, stop=True).then_inc(ev("D_sums"), 1)
                elif k == "D3":
                    pe.wait_ge(ev("group_out"), G_DV + 1)
                    pe.wait_ge(ev("D_weights"), n + 1)
                    values(s_a, s_b, dv, lambda j, a: 2 * (2 * n + j) + a, "D_mixed")
                elif k == "N":
                    pe.wait_ge(ev(f"N_squares{n}"), 1)
                    if n == 0:
                        pe.wait_ge(ev("N_root1"), 1)
                    for j in range(4):
                        ins = mm(bank(4)[:, 0:SEQ], ones, squares[n][:, j, :], start=(j == 0), stop=(j == 3))
                    ins.then_inc(ev(f"N_summed{n}"), 1)
                elif k == "DT":
                    pe.wait_ge(ev("small_in"), 112)
                    pe.wait_ge(ev("D_out"), 2)
                    for t in range(NT):
                        for kk in range(KT):
                            ins = mm(bank(7)[:, t * 8:(t + 1) * 8], h1T[:, kk, t * P:(t + 1) * P], wdt[:, kk, :],
                                     start=(kk == 0), stop=(kk == KT - 1))
                    ins.then_inc(ev("dt_done"), 1)
                elif k == "C0":
                    pe.wait_ge(ev("da_ready"), 1)
                    for ch in range(NT):
                        ins = mm(bank(7)[:, ch * 8:(ch + 1) * 8], upper, da[:, ch * 8:(ch + 1) * 8],
                                 start=True, stop=True)
                    ins.then_inc(ev("cum_done"), 1)
                elif k == "C1":
                    pe.wait_ge(ev("C_dau"), n + 1)
                    pe.wait_ge(ev("xc_ready"), 1)
                    if n == 1:
                        pe.wait_ge(ev("C_state_out"), 1)
                        pe.wait_ge(ev("C_y"), 1)
                    tok = slice(n * P, (n + 1) * P)
                    for q in range(2):
                        mm(bank(4 + q), ones, da_u[:, 4 * q:4 * q + 4, :], start=True, stop=True)
                    for g in range(2):
                        mm(bank(6)[:, g * P:(g + 1) * P], xc[:, 4 + g, tok], xc[:, 6 + g, tok], start=True, stop=True)
                    if n == 0:
                        for g in range(2):
                            tr(bank(6)[:, 256 + g * P:256 + (g + 1) * P], xc[:, 4 + g, tok], ident)
                    for j in range(4):
                        ins = tr(bank(7)[:, j * P:(j + 1) * P], xc[:, j, tok], ident)
                    ins.then_inc(ev("C_parts"), 1)
                elif k == "C2":
                    pe.wait_ge(ev("C_mix"), n + 1)
                    if n == 0:
                        for g in range(2):
                            ins = mm(bank(6)[:, g * 256:(g + 1) * 256], bm_tok[:, g * P:(g + 1) * P],
                                     xw[:, 4 * g:4 * g + 4, :], start=True, stop=True)
                        ins.then_inc(ev("C_state"), 1)
                    for h in range(8):
                        o = bank(7)[64 * (h % 2):64 * (h % 2) + 64, (h // 2) * P:(h // 2 + 1) * P]
                        ins = mm(o, xdt[:, h, :], seg[:, h, :], start=True, stop=(n == 0))
                        if n == 1:
                            ins = mm(o, state[:, h, :], cum_e[:, h, :], start=False, stop=True)
                    ins.then_inc(ev("C_mixed"), 1)
                elif k == "B1":
                    pe.wait_ge(ev("group_out"), G_BKV + 1)
                    if n == 0:
                        pe.wait_ge(ev("N_root2"), 1)
                    else:
                        pe.wait_ge(ev("B_out"), 1)
                    for t, b0, width in ((1, 4, SEQ), (0, 6, P)):
                        for j in range(2):
                            for a in range(2):
                                rows = slice(64 * a, 64 * a + 64)
                                ins = mm(bank(b0 + a)[:, j * width:(j + 1) * width],
                                         bq[rows, 2 * n + j, t * P:(t + 1) * P], kdup[rows, n, 0:width],
                                         start=True, stop=True)
                    ins.then_inc(ev("B_scores"), 1)
                elif k == "B2":
                    pe.wait_ge(ev("B_probs"), n + 1)
                    for a in range(2):
                        for j in range(2):
                            h = 2 * a + j
                            tr(bank(4 + a)[:, j * SEQ:j * SEQ + P], s_b[:, h, :], ident)
                            tr(bank(4 + a)[:, j * SEQ + P:(j + 1) * SEQ], s_a[:, h, 0:P], ident)
                            ins = tr(bank(6)[:, h * P:(h + 1) * P], s_a[:, h, P:SEQ], ident)
                    ins.then_inc(ev("B_probsT"), 1)
                elif k == "B3":
                    pe.wait_ge(ev("B_probsT_out"), n + 1)
                    values(t_a, t_b, vB, lambda j, a: n, "B_mixed")
                elif k in ("M2", "M3"):
                    a = acc[1] if k == "M2" else acc[2]
                    pe.wait_ge(mod_used, 32 if k == "M2" else 48)
                    if s == ("M2", 0):
                        pe.wait_ge(ev("N_root0"), 1)
                        pe.wait_ge(ev("B_out"), 2)
                    elif s == ("M3", 0):
                        pe.wait_ge(ev("M2_out"), 2)
                    else:
                        pe.wait_ge(ev(k + "_out"), 1)
                    for q in range(4):
                        ins = mm(bank(4 + q), ones, a[:, n * D + q * 512:n * D + (q + 1) * 512], start=True, stop=True)
                    ins.then_inc(ev(k + "_summed"), 1)
                elif k == "wo":
                    half = s[2]
                    if half == 0:
                        pe.wait_ge(ev("N_scaled3"), 1)
                        pe.wait_ge(ev("N_scaled2"), 1)
                        if n == 0:
                            pe.wait_ge(ev("A_gated"), 1)
                        elif n == 1:
                            pe.wait_ge(ev("group_out"), 10)
                        else:
                            pe.wait_ge(ev("x1_ready"), n - 1)
                    else:
                        pe.wait_ge(ev("N_scaled1"), 1)
                        pe.wait_ge(ev("N_scaled0"), 1)
                    w = arrived(pe, s).rearrange("p (k n) -> p k n", n=512)
                    for t in range(NT):
                        for kk in range(8):
                            kt = 8 * (1 - half) + kk
                            ins = mm(bank(2 * (n % 2) + t), yT[:, kt, t * P:(t + 1) * P], w[:, kk, :],
                                     start=(half == 0 and kk == 0), stop=(half == 1 and kk == 7))
                    ins.then_inc(proj_used, 1)

            pe.wait_ge(ev("h2_ready"), 2)
            pe.wait_ge(ev("M3_out"), 2)
            for b in range(4):
                for kk in range(4):
                    for t in range(NT):
                        kt = 4 * b + kk
                        ins = tr(bank(2 * b, 2)[:, kk * SEQ + t * P:kk * SEQ + (t + 1) * P],
                                 h2[:, t, kt * P:(kt + 1) * P], ident)
                ins.then_inc(ev("h2T"), 1)
            pe.wait_ge(ev("h2T_out"), 4)
            for t in range(NT):
                for kt in range(KT):
                    ins = mm(bank(0)[:, t * NE:(t + 1) * NE], h2T[:, kt, t * P:(t + 1) * P], rw[:, kt, :],
                             start=(kt == 0), stop=(kt == KT - 1))
            ins.then_inc(ev("r_logits"), 1)
            pe.wait_ge(ev("r_sel"), 1)
            mm(bank(1)[:, 0:16], strict, chosen[:, 0, :], start=True, stop=True)
            mm(bank(1)[:, 16:32], strict, chosen[:, 1, :], start=True, stop=False)
            mm(bank(1)[:, 16:32], ones, chosen[:, 0, :], start=False, stop=True)
            mm(bank(1)[:, 32:48], ones, chosen[:, 0, :], start=True, stop=False)
            mm(bank(1)[:, 32:48], ones, chosen[:, 1, :], start=False, stop=True).then_inc(ev("r_pos"), 1)

            def many(at_v):
                return pe.value_load(itab[0:1, bass.ds(at_v, 1)], min_val=0, max_val=1)

            def gather(L, count, flag):
                pe.wait_ge(L["onehot_ready"], count)

                def columns(w):
                    for kt in range(KT):
                        for t in range(NT):
                            ins = mm(bank(4, 4)[:, kt * P:kt * P + w], h2[:, t, kt * P:(kt + 1) * P],
                                     pos1h[:, t, 0:w], start=(t == 0), stop=(t == NT - 1))
                    ins.then_inc(L["gathered"], 1)

                with pe.If(flag > 0):
                    columns(P)
                with pe.Else():
                    columns(XH)

            def transpose_gates(L, count):
                pe.wait_ge(L["xg_ready"], count)
                for r in range(2):
                    for t in range(NT):
                        ins = tr(bank(4)[:, (2 * r + t) * P:(2 * r + t + 1) * P],
                                 gate1h[:, t, XH * r:XH * r + P], ident)
                ins.then_inc(L["pg_transposed"], 1)

            def combine(L, u, t, flag):
                def rows(few):
                    for n in range(4):
                        r = slice(0, P) if not few else (slice(0, XH) if n % 2 == 0 else slice(XH, P))
                        ins = mm(bank(4 + n), pgT[u][r, 2 * (n % 2) + t, :], y_sb[r, n * 512:(n + 1) * 512],
                                 start=True, stop=True)
                    ins.then_inc(L["combined"], 1)

                with pe.If(flag > 0):
                    rows(False)
                with pe.Else():
                    rows(True)

            def expert(L, i, u, base, fills):
                few0 = many(i * 2 + (base + 8 + u))
                few1 = many(i * 2 + (base + 9 + u))
                fewp = many(i * 2 + (base + 7 + u))

                def chunk(j):
                    pe.wait_ge(slot_full[j % NSLOT], i * 64 + 16 * (fills[j % NSLOT] + 2 * u + j // NSLOT + 1))
                    return at((j % NSLOT) * SLOT, SLOT)

                def gate_up(q):
                    ws = [chunk(2 * q + m).rearrange("p (k n) -> p k n", n=FF) for m in range(2)]

                    def products(full):
                        for m in range(2):
                            for kk in range(4):
                                kt = 4 * q + kk
                                for hf in range(2):
                                    if full:
                                        o, x0 = bank(2 * m + hf), xg[u][:, kt, XH * hf:XH * hf + P]
                                    else:
                                        o = bank(2 * m + hf)[XH * hf:XH * hf + XH, :]
                                        x0 = xg[u][:, kt, 0:XH]
                                    ins = mm(o, x0, ws[m][:, kk, hf * 512:(hf + 1) * 512],
                                             start=(kt == 0), stop=(kt == KT - 1))
                            ins.then_inc(L["slot_used"], 1)

                    with pe.If(few0 > 0):
                        products(True)
                    with pe.Else():
                        products(False)

                pe.wait_ge(L["xg_ready"], i * 2 + (u + 1))
                pe.wait_ge(L["hid_ready"], i * 2 + (u + 1))
                gate_up(0)
                pe.wait_ge(L["y_ready"], i * 2 + (u + 1))
                pe.wait_ge(L["pg_ready"], i * 2 + (u + 1))
                combine(L, 1 - u, 0, fewp)
                gate_up(1)
                pe.wait_ge(L["added"], i * 4 + (2 * u + 1))
                combine(L, 1 - u, 1, fewp)
                gate_up(2)
                pe.wait_ge(L["added"], i * 4 + (2 * u + 2))
                gather(L, i * 2 + (u + 2), few1)
                gate_up(3)
                transpose_gates(L, i * 2 + (u + 2))
                pe.wait_ge(L["pg_ready"], i * 2 + (u + 2))
                pe.wait_ge(L["hid_ready"], i * 2 + (u + 2))
                for f in range(8):
                    ins = tr(bank(4, 2)[:, f * P:(f + 1) * P], hid[:, f * P:(f + 1) * P], ident)
                ins.then_inc(L["hid_transposed"], 1)
                pe.wait_ge(L["hidT_act"], i * 2 + (u + 1))
                pe.wait_ge(L["hidT_dve"], i * 2 + (u + 1))
                for q in range(4):
                    w = chunk(8 + q).rearrange("p (k n) -> p k n", n=D)

                    def products(full):
                        for kk in range(2):
                            f = 2 * q + kk
                            for n in range(4):
                                hf = n % 2
                                if full:
                                    o, x0 = bank(4 + n), hidT[:, f, XH * hf:XH * hf + P]
                                else:
                                    o, x0 = bank(4 + n)[XH * hf:XH * hf + XH, :], hidT[:, f, 0:XH]
                                ins = mm(o, x0, w[:, kk, n * 512:(n + 1) * 512], start=(f == 0), stop=(f == 7))
                        ins.then_inc(L["slot_used"], 1)

                    with pe.If(few0 > 0):
                        products(True)
                    with pe.Else():
                        products(False)

            def last_combine(L, n, base):
                flag = many(base + 8 + n - 1)
                pe.wait_ge(L["y_ready"], n + 1)
                combine(L, 1, 0, flag)
                pe.wait_ge(L["added"], 2 * n + 1)
                combine(L, 1, 1, flag)

            pe.wait_ge(ev("tables_ready"), 1)
            gather(main, 1, many(8))
            transpose_gates(main, 1)
            with pe.Fori(0, NE // 2) as i:
                for u in range(2):
                    expert(main, i, u, 0, FILLS)
            last_combine(main, NE, 0)
            pe.wait_ge(ev("main_done"), 1)
            n_over = pe.value_load(itab[0:1, 0:1], min_val=0, max_val=NOVER)
            with pe.If(n_over > 0):
                gather(over, 1, many(8 + NE))
                transpose_gates(over, 1)
                with pe.Fori(0, NOVER // 2) as i:
                    for u in range(2):
                        expert(over, i, u, NE, [f + 2 * NE for f in FILLS])
                last_combine(over, NOVER, NE)

        @block.vector
        def _(dve):
            V = nc.vector
            links = [0]

            def link(ins):
                links[0] += 1
                ins.then_inc(ev("dve_link"), 1)
                dve.wait_ge(ev("dve_link"), links[0])

            def tt(o, a, b, op):
                return V.tensor_tensor(o, a, b, op)

            def over_heads(a, n, w):
                return a.unsqueeze(1).broadcast_to([P, n, w])

            def over_cols(a, n, w):
                return a.unsqueeze(2).broadcast_to([P, n, w])

            def modulate(it):
                _, r, k = it
                w = arrived(dve, it)
                if k == 0:
                    dve.wait_ge(ev(f"bias_in{r}"), 16)
                else:
                    dve.wait_ge(mod_used, mod_no[it])
                V.scalar_tensor_tensor(acc[r], w, cond[:, k:k + 1], acc[r], ALU.mult, ALU.add).then_inc(mod_used, 1)

            V.memset(eps, EPS).then_inc(ev("eps_ready"), 1)
            dve.wait_ge(ev("cond_ready"), 1)
            V.memset(xraw[:, :, 0:3], 0.0)
            for k in range(KT):
                modulate(("mod", 0, k))
                if k == 3:
                    dve.wait_ge(ev("rms1"), 1)
                    link(V.reciprocal(rs, rs))
                    for t in range(NT):
                        V.tensor_scalar(xtok[:, t, :], xtok[:, t, :], rs[:, t:t + 1], None, ALU.mult)\
                         .then_inc(ev("xn_ready"), 1)
            dve.wait_ge(ev("mod_summed"), 1)
            V.tensor_copy(mod1, bank(0)[:, 0:32]).then_inc(ev("mod_cols"), 1)
            dve.wait_ge(ev("mod_cols"), 1)
            link(V.scalar_tensor_tensor(a1, mod1[:, 16:32], 1.0, cols[:, c_n1:c_n1 + 16], ALU.add, ALU.mult))
            dve.wait_ge(ev("h1_raw"), 4)
            for k in range(KT):
                ins = V.tensor_scalar(h1T[:, k, :], h1T[:, k, :], a1[:, k:k + 1], mod1[:, k:k + 1], ALU.mult, ALU.add)
            ins.then_inc(ev("h1_ready"), 1)

            strict4 = over_heads(strict, 4, P)
            for n_step, s in enumerate(STEPS):
                k, n = s[0], s[1]
                if k in ("g", "wo"):
                    at_item = where[s] + 1
                    while at_item < NITEMS and ITEMS[at_item][0] == "mod":
                        modulate(ITEMS[at_item])
                        at_item += 1
                if s == ("g", 10, 1):
                    dve.wait_ge(ev("group_out"), 10)
                    dve.wait_ge(proj_used, pe_no[s] + 1)
                    link(V.memset(au[:, :, 0:2], 0.0))
                    V.tensor_tensor(au[:, :, 2:], bank(0, 2).rearrange("p (k n) -> p k n", n=SEQ), ac, ALU.mult)\
                     .then_inc(ev("A_gated"), 1)
                    dve.wait_ge(ev("A_gated"), 1)
                    for w in range(3):
                        for j in range(4):
                            cf = cols[:, c_ca + 4 * w + j:c_ca + 4 * w + j + 1]
                            if w == 0:
                                ins = V.tensor_scalar(ac[:, j, :], au[:, j, 0:SEQ], cf, None, ALU.mult)
                            else:
                                ins = V.scalar_tensor_tensor(ac[:, j, :], au[:, j, w:w + SEQ], cf, ac[:, j, :],
                                                             ALU.mult, ALU.add)
                        link(ins)
                    link(tt(yT[:, 0:4, :], ac, ab, ALU.mult))
                elif k == "D1":
                    dve.wait_ge(ev("D_ln"), n + 1)
                    link(V.scalar_tensor_tensor(t_all, s_all, 0.0, t_all, ALU.max, ALU.add))
                    tt(t_a[:, :, 0:P], t_a[:, :, 0:P], strict4, ALU.mult)
                    tt(t_b, t_b, strict4, ALU.mult).then_inc(ev("D_softp"), 1)
                elif k == "D2":
                    dve.wait_ge(ev("D_sums"), n + 1)
                    tt(s_a, s_a, bank(4, 2).rearrange("p (h n) -> p h n", n=SEQ), ALU.subtract)
                    link(tt(s_b, s_b, bank(6).rearrange("p (h n) -> p h n", n=P), ALU.subtract))
                    V.tensor_scalar(s_a[:, :, 0:P], s_a[:, :, 0:P], 0.0, None, ALU.min)
                    V.tensor_scalar(s_b, s_b, 0.0, None, ALU.min).then_inc(ev("D_logw"), 1)
                    dve.wait_ge(ev("D_exp"), n + 1)
                    tt(s_a[:, :, 0:P], s_a[:, :, 0:P], strict4, ALU.mult)
                    tt(s_b, s_b, strict4, ALU.mult).then_inc(ev("D_weights"), 1)
                elif k == "DT":
                    dve.wait_ge(ev("dt_done"), 1)
                    dve.wait_ge(ev("small_in"), 112)
                    tt(dtv.rearrange("p (t h) -> p t h", h=8), bank(7)[:, 0:16].rearrange("p (t h) -> p t h", h=8),
                       over_heads(dtb, NT, 8), ALU.add).then_inc(ev("dt_raw"), 1)
                    dve.wait_ge(ev("dt_ln"), 1)
                    link(V.scalar_tensor_tensor(dt, dtv, 0.0, dtw, ALU.max, ALU.add))
                    V.scalar_tensor_tensor(da.rearrange("p (t h) -> p t h", h=8), dt.rearrange("p (t h) -> p t h", h=8),
                                           -1.0, over_heads(ea, NT, 8), ALU.mult, ALU.mult).then_inc(ev("da_ready"), 1)
                    for a in range(2):
                        V.tensor_copy(dsk[64 * a:64 * a + 64, :],
                                      dsk8.rearrange("p (j a) -> p a j", a=2)[64 * a:64 * a + 64, a, :])
                    dve.wait_ge(ev("group_out"), G_BC + 1)
                    for w in range(4):
                        for j in range(8):
                            cf = cols[:, c_cw + 8 * w + j:c_cw + 8 * w + j + 1]
                            if w == 0:
                                ins = V.tensor_scalar(xc[:, j, :], xraw[:, j, 0:SEQ], cf,
                                                      cols[:, c_cb + j:c_cb + j + 1], ALU.mult, ALU.add)
                            else:
                                ins = V.scalar_tensor_tensor(xc[:, j, :], xraw[:, j, w:w + SEQ], cf, xc[:, j, :],
                                                             ALU.mult, ALU.add)
                        if w < 3:
                            link(ins)
                    ins.then_inc(ev("conv_done"), 1)
                elif k == "C0":
                    dve.wait_ge(ev("cum_done"), 1)
                    V.tensor_copy(cum, bank(7)[:, 0:16])
                    tt(da_u, over_heads(upper, 8, P), over_cols(da[:, 0:8], 8, P), ALU.mult).then_inc(ev("C_dau"), 1)
                    dve.wait_ge(ev("C_dau"), 1)
                elif k == "C1":
                    dve.wait_ge(ev("C_parts"), n + 1)
                    cumb = bank(4, 2).rearrange("p (h n) -> p h n", n=P)
                    cc = cum[:, 8 * n:8 * n + 8]
                    tt(seg, cumb, over_cols(cc, 8, P), ALU.subtract)
                    if n == 0:
                        link(tt(d2e, cumb[:, :, P - 1], cc, ALU.subtract))
                    else:
                        link(V.tensor_copy(cum_e, cumb))
                    V.tensor_scalar(seg, seg, 0.0, None, ALU.min).then_inc(ev("C_seg"), 1)
                    tt(cbm, bank(6)[:, 0:256].rearrange("p (g n) -> p g n", n=P), over_heads(upper, 2, P), ALU.mult)
                    if n == 0:
                        V.tensor_copy(bm_tok, bank(6)[:, 256:512])
                    link(tt(xdt, bank(7).rearrange("p (h n) -> p h n", n=64), over_cols(dt[:, 8 * n:8 * n + 8], 8, 64),
                            ALU.mult))
                    dve.wait_ge(ev("C_exp2"), n + 1)
                    if n == 0:
                        tt(xw, xdt, over_cols(d2e, 8, 64), ALU.mult)
                    else:
                        for g in range(2):
                            ce = cum_e[:, 4 * g:4 * g + 4, :]
                            tt(ce, ce, over_heads(xc[:, 6 + g, P:SEQ], 4, P), ALU.mult)
                    dve.wait_ge(ev("C_exp"), n + 1)
                    for g in range(2):
                        sg = seg[:, 4 * g:4 * g + 4, :]
                        ins = tt(sg, sg, over_heads(cbm[:, g, :], 4, P), ALU.mult)
                    ins.then_inc(ev("C_mix"), 1)
                    if n == 0:
                        tt(da_u, over_heads(upper, 8, P), over_cols(da[:, 8:16], 8, P), ALU.mult)\
                            .then_inc(ev("C_dau"), 1)
                elif k == "C2":
                    dve.wait_ge(ev("C_mixed"), n + 1)
                    tok = slice(n * P, (n + 1) * P)
                    for j in range(4):
                        ins = V.scalar_tensor_tensor(yT[:, 8 + j, tok], xc[:, j, tok], dsk[:, j:j + 1],
                                                     bank(7)[:, j * P:(j + 1) * P], ALU.mult, ALU.add)
                    ins.then_inc(ev("C_y"), 1)
                elif k == "B1":
                    dve.wait_ge(ev("B_scores"), n + 1)
                    dve.wait_ge(ev("masks_ready"), 5)
                    if n == 1:
                        dve.wait_ge(ev("B_out"), 1)
                    for a in range(2):
                        for j in range(2):
                            slope = 2.0 ** -(4 * n + 2 * j + a + 1)
                            V.scalar_tensor_tensor(s_a[:, 2 * a + j, :], dist, -slope,
                                                   bank(4 + a)[:, j * SEQ:(j + 1) * SEQ], ALU.mult, ALU.add)
                            ins = V.scalar_tensor_tensor(s_b[:, 2 * a + j, :], dist[:, P:SEQ], -slope,
                                                         bank(6 + a)[:, j * P:(j + 1) * P], ALU.mult, ALU.add)
                    link(ins)
                    V.reduce_max(mx[:, 0:4], s_b, AX)
                    link(V.reduce_max(mx[:, 4:8], s_a, AX))
                    sk = sink[:, 4 * n:4 * n + 4].rearrange("p (j a) -> p a j", a=2)
                    for q in range(2):
                        m = mx[:, 4 * q:4 * q + 4].rearrange("p (a j) -> p a j", a=2)
                        ins = tt(m, m, sk, ALU.max)
                    link(ins)
                    for q in range(2):
                        m, e = (z[:, 4 * q:4 * q + 4].rearrange("p (a j) -> p a j", a=2) for z in (mx, es))
                        tt(e, sk, m, ALU.subtract)
                    tt(s_b, s_b, over_cols(mx[:, 0:4], 4, P), ALU.subtract)
                    tt(s_a, s_a, over_cols(mx[:, 4:8], 4, SEQ), ALU.subtract).then_inc(ev("B_shifted"), 1)
                    dve.wait_ge(ev("B_exp"), n + 1)
                    V.reduce_sum(den[:, 0:4], s_b, AX)
                    link(V.reduce_sum(den[:, 4:8], s_a, AX))
                    link(tt(den, den, es, ALU.add))
                    link(V.reciprocal(den, den))
                    tt(s_b, s_b, over_cols(den[:, 0:4], 4, P), ALU.mult)
                    tt(s_a, s_a, over_cols(den[:, 4:8], 4, SEQ), ALU.mult).then_inc(ev("B_probs"), 1)
                elif k == "N":
                    yg = yT[:, 4 * n:4 * n + 4, :]
                    if n == 3:
                        dve.wait_ge(ev("D_out"), 2)
                    elif n == 1:
                        dve.wait_ge(ev("B_out"), 2)
                    elif n == 2:
                        dve.wait_ge(ev("C_y"), 2)
                        dve.wait_ge(ev("group_out"), G_Z + 1)
                        link(tt(yg, yg, zg, ALU.mult))
                    tt(squares[n], yg, yg, ALU.mult).then_inc(ev(f"N_squares{n}"), 1)
                    dve.wait_ge(ev(f"N_root{n}"), 1)
                    link(V.reciprocal(rstd_b, rstd_b))
                    for j in range(4):
                        ins = V.scalar_tensor_tensor(yg[:, j, :], yg[:, j, :], cols[:, c_gn[n] + j:c_gn[n] + j + 1],
                                                     rstd_b, ALU.mult, ALU.mult)
                    ins.then_inc(ev(f"N_scaled{n}"), 1)
                elif k == "wo" and s[2] == 1:
                    dve.wait_ge(proj_used, pe_no[s] + 1)
                    dve.wait_ge(ev("M2_out"), 1)
                    dve.wait_ge(ev("x_in"), 32)
                    if n > 0:
                        dve.wait_ge(ev("x1_ready"), n)
                    c5 = slice(n * 512, (n + 1) * 512)
                    link(tt(wo_tmp, bank(2 * (n % 2), 2).rearrange("p (t n) -> p t n", n=512),
                            over_heads(gate1_b[:, c5], NT, 512), ALU.mult))
                    tt(x1[:, :, c5], x1[:, :, c5], wo_tmp, ALU.add).then_inc(ev("x1_ready"), 1)

            dve.wait_ge(ev("M3_out"), 1)
            dve.wait_ge(ev("n2g_in"), 16)
            V.scalar_tensor_tensor(scale2_b, scale2_b, 1.0, n2g_b, ALU.add, ALU.mult)
            dve.wait_ge(ev("rms2"), 1)
            link(V.reciprocal(rs, rs))
            for t in range(NT):
                link(V.scalar_tensor_tensor(h2[:, t, :], x1[:, t, :], rs[:, t:t + 1], scale2_b, ALU.mult, ALU.mult))
                if t == 0:
                    dve.wait_ge(ev("M2_out"), 2)
                tt(h2[:, t, :], h2[:, t, :], shift2_b, ALU.add).then_inc(ev("h2_ready"), 1)

            def per(a):
                return over_cols(a, NT, NE)

            dve.wait_ge(ev("r_logits"), 1)
            link(V.tensor_copy(probs, bank(0)[:, 0:32].rearrange("p (t e) -> p t e", e=NE)))
            link(V.reduce_max(r1, probs, AX))
            tt(probs, probs, per(r1), ALU.subtract).then_inc(ev("r_shifted"), 1)
            V.tensor_scalar(wdesc, iota[:, 0:NE], -1.0, 16.0, ALU.mult, ALU.add)
            dve.wait_ge(ev("r_exp"), 1)
            link(V.reduce_sum(r1, probs, AX))
            link(V.reciprocal(r1, r1))
            link(tt(probs, probs, per(r1), ALU.mult))
            link(tt(sel, probs, over_heads(rbias, NT, NE), ALU.add))
            s4 = sel.rearrange("p t (g e) -> p (t g) e", e=4)
            tt(q4[:, 0, :], s4[:, :, 0], s4[:, :, 1], ALU.max)
            tt(q4[:, 1, :], s4[:, :, 0], s4[:, :, 1], ALU.min)
            tt(q4[:, 2, :], s4[:, :, 2], s4[:, :, 3], ALU.max)
            link(tt(q4[:, 3, :], s4[:, :, 2], s4[:, :, 3], ALU.min))
            tt(q4[:, 4, :], q4[:, 0, :], q4[:, 2, :], ALU.max)
            tt(q4[:, 5, :], q4[:, 0, :], q4[:, 2, :], ALU.min)
            link(tt(q4[:, 6, :], q4[:, 1, :], q4[:, 3, :], ALU.max))
            link(tt(q4[:, 6, :], q4[:, 5, :], q4[:, 6, :], ALU.max))
            link(tt(gsc, q4[:, 4, :].rearrange("p (t g) -> p t g", g=4), q4[:, 6, :].rearrange("p (t g) -> p t g", g=4),
                    ALU.add))

            def first_best(o, v, n):
                link(V.reduce_max(r1, v, AX))
                link(tt(o, v, over_cols(r1, NT, n), ALU.is_equal))
                link(tt(o, o, over_heads(wdesc[:, 0:n], NT, n), ALU.mult))
                link(V.reduce_max(r1, o, AX))
                link(tt(o, o, over_cols(r1, NT, n), ALU.is_equal))

            first_best(gmask, gsc, 4)
            g8 = gmask.rearrange("p t g -> p (t g)")
            V.tensor_scalar(g8b, g8, -1.0, BIG, ALU.add, ALU.mult)
            link(tt(s4, s4, over_cols(g8, 8, 4), ALU.mult))
            link(tt(s4, s4, over_cols(g8b, 8, 4), ALU.add))
            first_best(chosen, sel, NE)
            link(V.scalar_tensor_tensor(sel, chosen, -3.0 * BIG, sel, ALU.mult, ALU.add))
            first_best(second, sel, NE)
            tt(chosen, chosen, second, ALU.add).then_inc(ev("r_sel"), 1)
            dve.wait_ge(ev("r_sel"), 1)
            link(tt(gates, probs, chosen, ALU.mult))
            link(V.reduce_sum(r1, gates, AX))
            link(V.reciprocal(r1, r1))
            link(tt(gates, gates, per(r1), ALU.mult))
            dve.wait_ge(ev("r_pos"), 1)
            V.tensor_copy(cnt, bank(1)[:, 32:48])
            link(V.scalar_tensor_tensor(pos, bank(1)[:, 0:32].rearrange("p (t e) -> p t e", e=NE), 1.0, chosen,
                                        ALU.add, ALU.mult))
            link(V.tensor_scalar(pos, pos, -1.0, None, ALU.add))
            V.tensor_copy(posx[:, 0:NE, :], pos.rearrange("p t e -> p e t"))
            V.tensor_copy(gatex[:, 0:NE, :], gates.rearrange("p t e -> p e t"))
            V.memset(posx[:, NV, :], -1.0)
            V.memset(gatex[:, NV, :], 0.0)
            V.memset(flags, 0.0)
            link(V.tensor_scalar(ovr, cnt, float(P), None, ALU.is_gt))
            link(V.tensor_tensor_scan(ovc, ones[:, 0:NE], ovr, 0.0, ALU.mult, ALU.add))
            link(tt(ovx, ovc, ovr, ALU.subtract))
            link(tt(ovm, over_heads(ovx, NOVER, NE), over_cols(iota[:, 0:NOVER], NOVER, NE), ALU.is_equal))
            link(tt(ovm, ovm, over_heads(ovr, NOVER, NE), ALU.mult))
            V.reduce_sum(ova, ovm, AX)
            link(tt(ovt, ovm, over_heads(iota[:, 0:NE], NOVER, NE), ALU.mult))
            link(V.reduce_sum(ove, ovt, AX))
            link(V.tensor_scalar(ova, ova, -1.0, None, ALU.add))

            def pick(o, table):
                link(tt(ovt, ovm, over_heads(table, NOVER, NE), ALU.mult))
                link(V.reduce_sum(o, ovt, AX))

            V.tensor_scalar(cntq, cnt, -float(P), None, ALU.add)
            link(V.tensor_scalar(posq, pos, -float(P), None, ALU.add))
            for t in range(NT):
                pick(ovo, posq[:, t, :])
                link(tt(posx[:, NE:NV, t], ovo, ova, ALU.add))
                pick(gatex[:, NE:NV, t], gates[:, t, :])
            pick(ovo, cntq)
            V.tensor_scalar(flags[:, 8:8 + NE], cnt, float(XH), None, ALU.is_gt)
            link(V.tensor_scalar(flags[:, 8 + NE:8 + NV], ovo, float(XH), None, ALU.is_gt))
            V.tensor_copy(flags[:, 0:1], ovc[:, NE - 1:NE])
            link(V.tensor_copy(flags[:, 32:32 + NOVER], ove))
            V.tensor_copy(itab[0:1, 0:40], flags[0:1, 0:40]).then_inc(ev("tables_ready"), 1)

            def onehot(L, col):
                for t in range(NT):
                    pc = mem[:, bass.ds(col * NT + (posx_at + t), 1)]
                    gc = mem[:, bass.ds(col * NT + (gatex_at + t), 1)]
                    V.tensor_scalar(pos1h[:, t, :], iota[:, 0:P], pc, None, ALU.is_equal)
                    ins = V.tensor_scalar(gate1h[:, t, :], iota, pc, gc, ALU.is_equal, ALU.mult)
                ins.then_inc(L["onehot_ready"], 1)

            def take_gates(L, u, count):
                dve.wait_ge(L["pg_transposed"], count)
                V.tensor_copy(pgT[u], bank(4).rearrange("p (r n) -> p r n", n=P)).then_inc(L["pg_ready"], 1)

            def add_combined(L, t, count):
                dve.wait_ge(L["combined"], count)
                tt(x1[:, t, :], x1[:, t, :], bank(4, 4), ALU.add).then_inc(L["added"], 1)

            def expert(L, i, u, base):
                dve.wait_ge(L["pg_transposed"], i * 2 + (u + 1))
                onehot(L, i * 2 + (base + u + 1))
                for t in range(NT):
                    add_combined(L, t, i * 4 + (2 * u + t + 1))
                take_gates(L, 1 - u, i * 2 + (u + 2))
                dve.wait_ge(L["silu_done"], i * 2 + (u + 1))
                tt(hid, hid, bank(2, 2), ALU.mult).then_inc(L["hid_ready"], 1)
                dve.wait_ge(L["hid_transposed"], i * 2 + (u + 1))
                src = bank(5).rearrange("p (f n) -> p f n", n=P)
                V.tensor_copy(hidT[:, 4:8, XH:192], src)
                V.tensor_copy(hidT[:, 4:8, 0:XH], src[:, :, XH:P]).then_inc(L["hidT_dve"], 1)
                dve.wait_ge(L["slot_used"], i * 24 + (12 * u + 12))
                tt(y_sb, bank(4, 4), gate2_b, ALU.mult).then_inc(L["y_ready"], 1)

            def start_pass(L, first):
                V.memset(hid, 0.0).then_inc(L["hid_ready"], 1)
                V.memset(pgT[1], 0.0)
                V.memset(y_sb, 0.0).then_inc(L["y_ready"], 1)
                onehot(L, first)
                take_gates(L, 0, 1)

            dve.wait_ge(ev("tables_ready"), 1)
            dve.wait_ge(ev("M3_out"), 2)
            start_pass(main, 0)
            with dve.Fori(0, NE // 2) as i:
                for u in range(2):
                    expert(main, i, u, 0)
            add_combined(main, 0, 2 * NE + 1)
            add_combined(main, 1, 2 * NE + 2)
            V.memset(y_sb, 0.0).then_inc(ev("main_done"), 1)
            n_over = dve.value_load(itab[0:1, 0:1], min_val=0, max_val=NOVER)
            with dve.If(n_over > 0):
                start_pass(over, NE)
                with dve.Fori(0, NOVER // 2) as i:
                    for u in range(2):
                        expert(over, i, u, NE)
                add_combined(over, 0, 2 * NOVER + 1)
                add_combined(over, 1, 2 * NOVER + 2)
            V.memset(r1, 0.0).then_inc(ev("x1_final"), 1)
            dve.wait_ge(ev("rms3"), 1)
            dve.wait_ge(ev("fin_in"), 16)
            link(V.reciprocal(rs, rs))
            for t in range(NT):
                V.scalar_tensor_tensor(x1[:, t, :], x1[:, t, :], rs[:, t:t + 1], fin_b, ALU.mult, ALU.mult)\
                 .then_inc(ev(f"out_ready{t}"), 1)


_INS = ["x", "c", "w_mod", "b_mod", "norm1_g", "norm2_g", "w_in", "w_out", "conv_a_w", "gn_a", "attn_sinks",
        "gn_b", "ssm_conv_w", "ssm_conv_b", "dt_bias", "a_log", "d_skip", "ssm_norm_g", "gn_d", "router_w",
        "router_bias", "moe_w_gate", "moe_w_up", "moe_w_down", "final_g"]


def kernel(**inputs):
    import numpy as _np
    import concourse.bacc as _bacc
    from concourse import mybir as _mybir
    from concourse.bass_utils import run_bass_kernel_spmd as _run

    nc = _bacc.Bacc("TRN2", target_bir_lowering=False, num_devices=1)
    arrays, args = {}, []
    for name in _INS:
        a = _np.ascontiguousarray(inputs[name])
        arrays[f"in_{name}"] = a
        args.append(nc.dram_tensor(f"in_{name}", a.shape, _mybir.dt.from_np(a.dtype), kind="ExternalInput").ap())
    out = nc.dram_tensor("out_0", (1, SEQ, D), F32, kind="ExternalOutput").ap()
    trunk(nc, *args, out)
    r = _run(nc, [arrays], core_ids=[0])
    return r.results[0]["out_0"]
```

```python
from contextlib import ExitStack

import numpy as np
import concourse.bass as bass
from concourse import mybir

F32 = mybir.dt.float32
I32 = mybir.dt.int32
ALU = mybir.AluOpType
ACT = mybir.ActivationFunctionType
AX = mybir.AxisListType.X

D = 2048
SEQ = 256
P = 128
NT = SEQ // P
KT = D // P
GW = 512
NE = 16
FF = 1024
EXPERT = D * FF
EPS = 1e-6
SLOT = 4096
NSLOT = 6
NSLOT_B = 4
XH = 64
NOVER = 4
NV = NE + NOVER
BIG = 1e30

A_B, A_C, A_X = 0, 512, 1024
B_Q, B_KV = 1536, 2048
C_Z, C_XS, C_BC, C_DT = 2304, 2816, 3328, 3840
D_Q, D_K, D_V = 3848, 4360, 4872
GROUPS = [D_Q, D_K, D_V, C_XS, C_BC, B_Q, B_KV, C_Z, A_B, A_C, A_X]
G_DQ, G_DK, G_DV, G_XS, G_BC, G_BQ, G_BKV, G_Z, G_AB, G_AC, G_AX = range(11)

STEPS = [
    ("g", 0, 0), ("g", 0, 1), ("g", 1, 0), ("g", 1, 1), ("D1", 0), ("g", 2, 0), ("D2", 0), ("g", 2, 1),
    ("D3", 0), ("g", 3, 0), ("D1", 1), ("g", 3, 1), ("D2", 1), ("g", 4, 0), ("D3", 1), ("g", 4, 1),
    ("N", 3), ("DT", 0), ("g", 5, 0), ("C0", 0), ("g", 5, 1), ("C1", 0), ("g", 6, 1), ("C2", 0),
    ("g", 7, 0), ("C1", 1), ("g", 7, 1), ("C2", 1), ("g", 8, 0), ("N", 2), ("g", 8, 1), ("B1", 0),
    ("g", 9, 0), ("B2", 0), ("g", 9, 1), ("B3", 0), ("g", 10, 0), ("B1", 1), ("g", 10, 1), ("B2", 1),
    ("wo", 0, 0), ("B3", 1), ("wo", 1, 0), ("N", 1), ("N", 0), ("M", 0), ("wo", 0, 1), ("M", 1),
    ("wo", 1, 1), ("wo", 2, 0), ("M", 2), ("R", 0), ("wo", 2, 1), ("R", 1), ("wo", 3, 0), ("R", 2),
    ("wo", 3, 1), ("R", 3), ("M", 3),
]


def stream():
    items = [("mod", 0, k) for k in range(KT)]
    left = [("mod", r, k) for r in (1, 2) for k in range(KT)]
    n = 0
    for s in STEPS:
        if s[0] in ("g", "wo"):
            items.append(s)
            for _ in range(2 if n % 3 == 0 and n > 5 else 1):
                if left:
                    items.append(left.pop(0))
            n += 1
    assert not left
    return items


def trunk(nc, x, c, w_mod, b_mod, norm1_g, norm2_g, w_in, w_out, conv_a_w, gn_a, attn_sinks, gn_b,
          ssm_conv_w, ssm_conv_b, dt_bias, a_log, d_skip, ssm_norm_g, gn_d, router_w, router_bias,
          moe_w_gate, moe_w_up, moe_w_down, final_g, out):
    ctx = ExitStack()
    with ctx:
        mem = ctx.enter_context(nc.sbuf_tensor("mem", [P, 53120], F32))
        itab = ctx.enter_context(nc.sbuf_tensor("itab", [1, 64], I32))
        ps = ctx.enter_context(nc.psum_tensor("ps", [P, 4096], F32))

        def at(start, *shape):
            n = int(np.prod(shape))
            a = mem[:, start:start + n]
            if len(shape) == 2:
                a = a.rearrange("p (a b) -> p a b", b=shape[1])
            elif len(shape) == 3:
                a = a.rearrange("p (a b c) -> p a b c", b=shape[1], c=shape[2])
            return a

        def bank(b, n=1):
            return ps[:, 512 * b:512 * (b + n)]

        H1 = NSLOT * SLOT
        ACC_A, ACC_B = H1 + 4096, H1 + 8192
        REST = H1 + 12288
        X1, YT, XG, CONST = REST, REST + 4096, REST + 8192, REST + 8192 + 6144
        WC = NSLOT_B * SLOT
        WD = WC + 5120

        h1T = at(H1, KT, SEQ)
        acc = [at(ACC_A, 4096), at(ACC_B, 4096), at(ACC_A, 4096)]
        xtok = at(X1, NT, D)
        yT = at(YT, KT, SEQ)
        dq, dk, dv = at(X1, 4, SEQ), at(X1 + 1024, 4, SEQ), at(X1 + 2048, NT, GW)
        ab, ac, au = at(X1, 4, SEQ), at(X1 + 1024, 4, SEQ), at(X1 + 2048, 4, SEQ + 2)
        kdup = at(X1 + 3088, 2, SEQ)
        xraw = at(XG, 8, SEQ + 3)
        zg = at(XG, 4, SEQ)
        xc = at(XG + 2072, 8, SEQ)
        bq = at(XG + 4120, 4, SEQ)
        rstd_b = at(XG + 5144, SEQ)
        vB = at(XG + 5400, NT, P)
        params = at(XG, P)
        wo_tmp = at(XG, NT, GW)
        da_u = at(WC, 8, P)
        seg = at(WC + 1024, 8, P)
        cum_e = at(WC + 2048, 8, P)
        cbm = at(WC + 3072, 2, P)
        bm_tok = at(WC + 3328, 2 * P)
        xdt = at(WC + 3584, 8, 64)
        xw = at(WC + 4096, 8, 64)
        state = at(WC + 4608, 8, 64)
        s_a, s_b = at(WD, 4, SEQ), at(WD + 1024, 4, P)
        t_a, t_b = at(WD + 1536, 4, SEQ), at(WD + 2560, 4, P)
        s_all, t_all = at(WD, 1536), at(WD + 1536, 1536)
        x1 = xtok
        xacc = at(YT, NT, D)
        xaT = h1T
        xg = [at(XG + 3072 * u, KT, 192) for u in range(2)]
        y_sb = at(H1, D)
        pos1h = at(H1 + 2048, NT, P)
        gate1h = at(H1 + 2304, NT, 192)
        RT = H1 + 2688
        rt = [RT]

        def route(*shape):
            a = at(rt[0], *shape)
            rt[0] += int(np.prod(shape))
            return a

        probs, sel, chosen, second, gates, pos, posq = (route(NT, NE) for _ in range(7))
        gsc, gmask, q4, g8b, r1 = route(NT, 4), route(NT, 4), route(7, 8), route(8), route(NT)
        wdesc, cnt, cntq, ovr, ovc, ovx, shift_l = (route(NE) for _ in range(7))
        ovm, ovt = route(NOVER, NE), route(NOVER, NE)
        ova, ove, ovo, flags = route(NOVER), route(NOVER), route(NOVER), route(64)
        posx_at = rt[0]
        posx = route(NV + 1, NT)
        gatex_at = rt[0]
        gatex = route(NV + 1, NT)
        assert rt[0] <= H1 + 4096, rt[0] - H1
        pgT = [at(ACC_B + 512 * u, 4, P) for u in range(2)]
        hid = at(ACC_B + 1024, FF)
        hidT = at(ACC_B + 2048, 8, 192)
        junk = at(XG + 1024, 512)
        rw_sh = at(XG + 1536, KT, NE)
        junk_f = hid[:, 0:512]
        gate1_b, gate2_b = at(ACC_B, D), at(ACC_A + D, D)
        fin_b = at(ACC_A, D)

        cur = [CONST]

        def small(*shape):
            a = at(cur[0], *shape)
            cur[0] += int(np.prod(shape))
            return a

        ident, ones = small(P), small(P)
        upper = small(P)
        lower = small(P)
        strict = small(P)
        dist = small(SEQ)
        iota = small(192)
        cols = small(P)
        rw = small(KT, NE)
        wdt = small(KT, 8)
        dtb, alog, sink, rbias, dsk8, dsk = small(8), small(8), small(8), small(NE), small(8), small(4)
        cond, mod1, a1 = small(16), small(32), small(16)
        sh2, a2 = small(16), small(16)
        ss, rs, rs2, rs3, eps = small(2), small(2), small(2), small(2), small(1)
        ss8, ssf = small(NT, 4), small(NT, 4)
        dtv, dtw, dt, da, cum = small(16), small(16), small(16), small(16), small(16)
        ea, d2e = small(8), small(8)
        mx, den, es = small(8), small(8), small(8)
        assert cur[0] <= 53120, cur[0]
        squares = [ac, at(WD + 1536, 4, SEQ), at(WC + 1024, 4, SEQ), at(WD + 1536, 4, SEQ)]
        c_c, c_n1, c_ca, c_cw, c_cb = 0, 16, 32, 44, 76
        c_gn = [84, 88, 92, 96]
        c_n2 = 100
        NPAR = 116

        sems = {}

        def ev(name):
            if name not in sems:
                sems[name] = ctx.enter_context(nc.semaphore(name))
            return sems[name]

        ITEMS = stream()
        where = {it: n for n, it in enumerate(ITEMS)}
        NITEMS = len(ITEMS)
        slot_full = [ev(f"slot_full{s}") for s in range(NSLOT)]
        mod_used, proj_used = ev("mod_used"), ev("proj_used")
        mods = [it for it in ITEMS if it[0] == "mod"]
        pes = [it for it in ITEMS if it[0] != "mod"]
        mod_no = {it: n for n, it in enumerate(mods)}
        pe_no = {it: n for n, it in enumerate(pes)}
        FILLS = [len(range(s, NITEMS, NSLOT_B)) if s < NSLOT_B else 0 for s in range(NSLOT)]

        def used(it):
            return (mod_used, mod_no[it] + 1) if it[0] == "mod" else (proj_used, pe_no[it] + 1)

        def arrived(eng, it):
            n = where[it]
            eng.wait_ge(slot_full[n % NSLOT_B], 16 * (n // NSLOT_B + 1))
            return at((n % NSLOT_B) * SLOT, SLOT)

        def bcast_rows(src, n, rows=P):
            return bass.AP(src.tensor, src.offset, [[0, rows], [1, n]])

        def loop_sems(tag):
            return {n: ev(f"{tag}_{n}") for n in (
                "slot_used", "onehot_ready", "gathered", "xg_ready", "pg_transposed", "pg_ready", "silu_done",
                "hid_ready", "hid_transposed", "xg_scaled", "squared", "hidT_act", "hidT_dve", "y_ready", "combined", "added_lo", "added_hi")}

        main, over = loop_sems("main"), loop_sems("over")

        block = ctx.enter_context(nc.Block())

        @block.sync
        def _(sp):
            sp.dma_start(mem[0:16, XG:XG + P], c.rearrange("b (k p) -> (b k) p", p=P)).then_inc(ev("params_in"), 16)
            sp.dma_start(mem[16:32, XG:XG + P], norm1_g.rearrange("b (k p) -> (b k) p", p=P)).then_inc(ev("params_in"), 16)
            sp.dma_start(mem[32:44, XG:XG + P], conv_a_w.rearrange("b w (k p) -> (b w k) p", p=P)).then_inc(ev("params_in"), 16)
            sp.dma_start(mem[44:76, XG:XG + P], ssm_conv_w.rearrange("b w (k p) -> (b w k) p", p=P)).then_inc(ev("params_in"), 16)
            sp.dma_start(mem[76:84, XG:XG + P], ssm_conv_b.rearrange("b (k p) -> (b k) p", p=P)).then_inc(ev("params_in"), 16)
            for i, g in enumerate((gn_a, gn_b, ssm_norm_g, gn_d)):
                sp.dma_start(mem[84 + 4 * i:88 + 4 * i, XG:XG + P], g.rearrange("b (k p) -> (b k) p", p=P)).then_inc(ev("params_in"), 16)
            sp.dma_start(mem[100:116, XG:XG + P], norm2_g.rearrange("b (k p) -> (b k) p", p=P)).then_inc(ev("params_in"), 16)
            for n, it in enumerate(ITEMS):
                if n >= NSLOT_B:
                    sp.wait_ge(*used(ITEMS[n - NSLOT_B]))
                dst = at((n % NSLOT_B) * SLOT, SLOT)
                if it[0] == "mod":
                    _, r, k = it
                    src = w_mod[0, k * P:(k + 1) * P, r * 4096:(r + 1) * 4096]
                elif it[0] == "g":
                    _, g, half = it
                    if g == G_BKV:
                        dst = dst.rearrange("p (k n) -> p k n", n=256)
                        src = w_in[0, :, B_KV:B_KV + 256].rearrange("(k p) n -> p k n", p=P)
                    else:
                        dst = dst.rearrange("p (k n) -> p k n", n=512)
                        src = w_in[0, half * 1024:(half + 1) * 1024, GROUPS[g]:GROUPS[g] + 512]\
                            .rearrange("(k p) n -> p k n", p=P)
                else:
                    _, n4, half = it
                    r0 = 1024 * (1 - half)
                    dst = dst.rearrange("p (k n) -> p k n", n=512)
                    src = w_out[0, r0:r0 + 1024, n4 * 512:(n4 + 1) * 512].rearrange("(k p) n -> p k n", p=P)
                sp.dma_start(dst, src).then_inc(slot_full[n % NSLOT_B], 16)

            def expert_chunk(j, start, sem=None, count=None):
                if sem is not None:
                    sp.wait_ge(sem, count)
                if j < 8:
                    w, first, pitch, width = (moe_w_gate, moe_w_up)[j % 2], (j // 2) * 512 * FF, FF, FF
                else:
                    w, first, pitch, width = moe_w_down, (j - 8) * 512, D, 512
                tiles = SLOT // width
                src = bass.AP(w.tensor, start + first, [[pitch, P], [P * pitch, tiles], [1, width]])
                dst = at((j % NSLOT) * SLOT, SLOT).rearrange("p (k n) -> p k n", n=width)
                sp.dma_start(dst, src).then_inc(slot_full[j % NSLOT], 16)

            for j in range(NSLOT):
                if j < NSLOT_B:
                    last = max(n for n in range(NITEMS) if n % NSLOT_B == j)
                    sp.wait_ge(*used(ITEMS[last]))
                elif j == NSLOT_B:
                    sp.wait_ge(ev("N_scaled0"), 1)
                    sp.wait_ge(ev("N_scaled1"), 1)
                    sp.wait_ge(ev("N_scaled2"), 1)
                    sp.wait_ge(ev("N_scaled3"), 1)
                expert_chunk(j, 0)
            with sp.Fori(0, NE // 2 - 1) as i:
                starts = [(i * 2 + q) * EXPERT for q in range(3)]
                starts_down = [i * (2 * EXPERT) + q * EXPERT for q in range(3)]
                for m in range(24):
                    q, j = divmod(m + 6, 12)
                    expert_chunk(j, (starts if j < 8 else starts_down)[q], main["slot_used"], i * 24 + (m + 1))
            for m in range(24 * (NE // 2 - 1), 12 * NE - 6):
                sp.wait_ge(main["slot_used"], m + 1)
                expert_chunk((m + 6) % 12, (m + 6) // 12 * EXPERT)
            sp.wait_ge(ev("main_done"), 1)
            n_over = sp.value_load(itab[0:1, 0:1], min_val=0, max_val=NOVER)
            with sp.If(n_over > 0):
                def first_element(at_v):
                    e = sp.value_load(itab[0:1, bass.ds(at_v, 1)], min_val=0, max_val=NE - 1)
                    return e * EXPERT, (e * 2) * (EXPERT // 2)

                start = first_element(32)
                for j in range(NSLOT):
                    expert_chunk(j, start[0])
                with sp.Fori(0, NOVER - 1) as v:
                    here, after = first_element(v + 32), first_element(v + 33)
                    for m in range(12):
                        q, j = divmod(m + 6, 12)
                        expert_chunk(j, (after if q else here)[j // 8], over["slot_used"], v * 12 + (m + 1))
                start = first_element(32 + NOVER - 1)
                for j in range(NSLOT, 12):
                    expert_chunk(j, start[j // 8], over["slot_used"], 12 * (NOVER - 1) + j - NSLOT + 1)
            for n in range(4):
                t, half = divmod(n, 2)
                sp.wait_ge(ev("out_ready"), n + 1)
                sp.dma_start(out[0, t * P:(t + 1) * P, half * 1024:(half + 1) * 1024],
                             xacc[:, t, half * 1024:(half + 1) * 1024]).then_inc(ev("out_written"), 16)
            sp.wait_ge(ev("out_written"), 64)

        @block.gpsimd
        def _(pool):
            nc.gpsimd.memset(acc[0], 0.0).then_inc(ev("acc_zeroed0"), 1)
            nc.gpsimd.memset(acc[1], 0.0).then_inc(ev("acc_zeroed1"), 1)
            nc.gpsimd.memset(ident, 0.0)
            nc.gpsimd.memset(upper, 1.0)
            nc.gpsimd.memset(lower, 1.0)
            nc.gpsimd.memset(strict, 1.0)
            nc.gpsimd.memset(ones, 1.0).then_inc(ev("masks_filled"), 1)
            pool.wait_ge(ev("masks_filled"), 1)

            def select(m, op, fill, base, step, mult, name):
                nc.gpsimd.affine_select(out=m, in_=m, compare_op=op, fill=fill, base=base,
                                        pattern=[[step, m.shape[1]]], channel_multiplier=mult)\
                  .then_inc(ev(name), 1)

            select(ident, ALU.not_equal, 1.0, 0, -1, 1, "ident_ready")
            select(upper, ALU.is_ge, 0.0, 0, 1, -1, "masks_ready")
            select(lower, ALU.is_ge, 0.0, 0, -1, 1, "masks_ready")
            select(strict, ALU.is_gt, 0.0, 0, 1, -1, "masks_ready")
            nc.gpsimd.iota(dist, pattern=[[-1, SEQ]], base=P, channel_multiplier=1,
                           allow_small_or_imprecise_dtypes=True).then_inc(ev("dist_filled"), 1)
            pool.wait_ge(ev("dist_filled"), 1)
            select(dist, ALU.is_ge, BIG, P, -1, 1, "dist_cut")
            pool.wait_ge(ev("dist_cut"), 1)
            select(dist, ALU.is_gt, BIG, 0, 1, -1, "masks_ready")
            nc.gpsimd.iota(iota[:, 0:P], pattern=[[1, P]], base=0, channel_multiplier=0,
                           allow_small_or_imprecise_dtypes=True)
            nc.gpsimd.iota(iota[:, P:192], pattern=[[1, XH]], base=0, channel_multiplier=0,
                           allow_small_or_imprecise_dtypes=True).then_inc(ev("masks_ready"), 1)
            pool.wait_ge(ev("mod_cols"), 1)
            nc.gpsimd.memset(acc[2], 0.0).then_inc(ev("acc_zeroed2"), 1)
            pool.wait_ge(ev("x1_ready"), 4)
            nc.gpsimd.tensor_copy(xacc, x1).then_inc(ev("xacc_ready"), 1)

        @block.scalar
        def _(act):
            links = [0]

            def link(ins):
                links[0] += 1
                ins.then_inc(ev("act_link"), 1)
                act.wait_ge(ev("act_link"), links[0])

            act.dma_start(xtok, x[0].rearrange("(t p) d -> p t d", p=P)).then_inc(ev("x_in"), 16)
            act.wait_ge(ev("acc_zeroed0"), 1)
            act.dma_start(acc[0][0:1, :], b_mod[:, 0:4096]).then_inc(ev("bias_in0"), 16)
            act.wait_ge(ev("acc_zeroed1"), 1)
            act.dma_start(acc[1][0:1, :], b_mod[:, 4096:8192]).then_inc(ev("bias_in1"), 16)
            act.dma_start(wdt, w_in[0, :, C_DT:C_DT + 8].rearrange("(k p) n -> p k n", p=P)).then_inc(ev("small_in"), 16)
            act.dma_start(rw, router_w.rearrange("(k p) n -> p k n", p=P)).then_inc(ev("small_in"), 16)
            act.dma_start(dtb, dt_bias[0].partition_broadcast(P)).then_inc(ev("small_in"), 16)
            act.dma_start(alog, a_log[0].partition_broadcast(P)).then_inc(ev("small_in"), 16)
            act.dma_start(sink, attn_sinks[0].partition_broadcast(P)).then_inc(ev("small_in"), 16)
            act.dma_start(rbias, router_bias.partition_broadcast(P)).then_inc(ev("small_in"), 16)
            act.dma_start(dsk8, d_skip[0].partition_broadcast(P)).then_inc(ev("small_in"), 16)

            act.wait_ge(ev("params_T"), 1)
            nc.scalar.activation(cols[:, 0:NPAR], bank(0)[:, 0:NPAR], ACT.Copy).then_inc(ev("cols_ready"), 1)
            act.wait_ge(ev("cols_ready"), 1)
            nc.scalar.activation(cond, cols[:, 0:16], ACT.Silu).then_inc(ev("cond_ready"), 1)
            act.wait_ge(ev("x_in"), 16)
            for t in range(NT):
                link(nc.scalar.activation(at(H1, D), xtok[:, t, :], ACT.Square, accum_out=ss[:, t:t + 1]))
            act.wait_ge(ev("eps_ready"), 1)
            nc.scalar.activation(rs, ss, ACT.Sqrt, scale=1.0 / D, bias=eps).then_inc(ev("rms1"), 1)
            for b in range(4):
                act.wait_ge(ev("xT"), b + 1)
                nc.scalar.activation(h1T[:, 4 * b:4 * b + 4, :], bank(2 * b, 2).rearrange("p (k n) -> p k n", n=SEQ),
                                     ACT.Copy).then_inc(ev("h1_raw"), 1)
            act.wait_ge(ev("acc_zeroed2"), 1)
            act.dma_start(acc[2][0:1, :], b_mod[:, 8192:12288]).then_inc(ev("bias_in2"), 16)

            dest = {G_DQ: (dq, 0.125), G_DK: (dk, 1.0), G_DV: (dv, 1.0), G_XS: (xraw[:, 0:4, 3:], 1.0),
                    G_BC: (xraw[:, 4:8, 3:], 1.0), G_BQ: (bq, 0.125), G_Z: (zg, 1.0), G_AB: (ab, 1.0),
                    G_AC: (ac, 1.0)}
            for s in STEPS:
                k, n = s[0], s[1]
                if k == "g" and s[2] == 1:
                    two = bank(2 * (n % 2), 2)
                    if n == G_AX:
                        continue
                    act.wait_ge(proj_used, pe_no[s] + 1)
                    if n == G_BKV:
                        for kv in range(2):
                            for a in range(2):
                                nc.scalar.activation(kdup[64 * a:64 * a + 64, kv, :], two[64 * kv:64 * kv + 64, 0:SEQ],
                                                     ACT.Copy)
                        ins = nc.scalar.activation(vB, two[:, 512:768].rearrange("p (t n) -> p t n", n=P), ACT.Copy)
                    elif n == G_DV:
                        ins = nc.scalar.activation(dv, two.rearrange("p (t n) -> p t n", n=GW), ACT.Copy)
                    else:
                        if n in (G_AB, G_AC):
                            act.wait_ge(ev("D_out"), 2)
                        if n == G_Z:
                            act.wait_ge(ev("conv_done"), 1)
                        d, sc = dest[n]
                        f = ACT.Silu if n == G_Z else ACT.Copy
                        ins = nc.scalar.activation(d, two.rearrange("p (k n) -> p k n", n=SEQ), f, scale=sc)
                    ins.then_inc(ev("group_out"), 1)
                elif k == "D1":
                    act.wait_ge(ev("D_scores"), n + 1)
                    if n == 1:
                        act.wait_ge(ev("D_out"), 1)
                    nc.scalar.activation(s_a, bank(4, 2).rearrange("p (h n) -> p h n", n=SEQ), ACT.Copy)
                    nc.scalar.activation(s_b.rearrange("p (a h) n -> p a h n", a=2),
                                         bank(6, 2).rearrange("p (a h n) -> p a h n", a=2, n=P)[:, :, 0:2, :],
                                         ACT.Copy).then_inc(ev("D_scores_out"), 1)
                    act.wait_ge(ev("D_scores_out"), n + 1)
                    link(nc.scalar.activation(t_all, s_all, ACT.Abs))
                    link(nc.scalar.activation(t_all, t_all, ACT.Exp, scale=-1.0))
                    nc.scalar.activation(t_all, t_all, ACT.Ln, bias=1.0).then_inc(ev("D_ln"), 1)
                elif k == "D2":
                    act.wait_ge(ev("D_logw"), n + 1)
                    nc.scalar.activation(s_all, s_all, ACT.Exp).then_inc(ev("D_exp"), 1)
                elif k in ("D3", "B3"):
                    act.wait_ge(ev(k[0] + "_mixed"), n + 1)
                    t0 = (12 if k == "D3" else 4) + 2 * n
                    nc.scalar.activation(yT[:, t0:t0 + 2, :], bank(7).rearrange("p (j n) -> p j n", n=SEQ),
                                         ACT.Copy).then_inc(ev(k[0] + "_out"), 1)
                elif k == "N":
                    act.wait_ge(ev(f"N_summed{n}"), 1)
                    nc.scalar.activation(rstd_b, bank(4)[:, 0:SEQ], ACT.Sqrt, scale=1.0 / GW, bias=eps)\
                      .then_inc(ev(f"N_root{n}"), 1)
                elif k == "DT":
                    act.wait_ge(ev("dt_raw"), 1)
                    act.wait_ge(ev("small_in"), 112)
                    link(nc.scalar.activation(dtw, dtv, ACT.Abs))
                    nc.scalar.activation(ea, alog, ACT.Exp)
                    link(nc.scalar.activation(dtw, dtw, ACT.Exp, scale=-1.0))
                    nc.scalar.activation(dtw, dtw, ACT.Ln, bias=1.0).then_inc(ev("dt_ln"), 1)
                    act.wait_ge(ev("conv_done"), 1)
                    nc.scalar.activation(xc, xc, ACT.Silu).then_inc(ev("xc_ready"), 1)
                elif k == "C1":
                    act.wait_ge(ev("C_seg"), n + 1)
                    nc.scalar.activation(seg, seg, ACT.Exp).then_inc(ev("C_exp"), 1)
                    if n == 0:
                        nc.scalar.activation(d2e, d2e, ACT.Exp).then_inc(ev("C_exp2"), 1)
                    else:
                        nc.scalar.activation(cum_e, cum_e, ACT.Exp).then_inc(ev("C_exp2"), 1)
                elif k == "C2" and n == 0:
                    act.wait_ge(ev("C_state"), 1)
                    nc.scalar.activation(state, bank(6).rearrange("p (h n) -> p h n", n=64), ACT.Copy)\
                      .then_inc(ev("C_state_out"), 1)
                elif k == "B1":
                    act.wait_ge(ev("B_shifted"), n + 1)
                    nc.scalar.activation(s_all, s_all, ACT.Exp)
                    nc.scalar.activation(es, es, ACT.Exp).then_inc(ev("B_exp"), 1)
                elif k == "B2":
                    act.wait_ge(ev("B_probsT"), n + 1)
                    nc.scalar.activation(t_a, bank(4, 2).rearrange("p (h n) -> p h n", n=SEQ), ACT.Copy)
                    nc.scalar.activation(t_b, bank(6).rearrange("p (h n) -> p h n", n=P), ACT.Copy)\
                      .then_inc(ev("B_probsT_out"), 1)
                elif k == "M" and n == 0:
                    act.wait_ge(ev("M_summed0"), 1)
                    nc.scalar.activation(gate1_b, bank(4, 4), ACT.Copy).then_inc(ev("M_out0"), 1)
                elif k == "R":
                    act.wait_ge(ev("x1_ready"), n + 1)
                    for t in range(NT):
                        link(nc.scalar.activation(junk, x1[:, t, n * 512:(n + 1) * 512], ACT.Square,
                                                  accum_out=ss8[:, t, n:n + 1]))
                    act.wait_ge(ev("R_transposed"), n + 1)
                    act.wait_ge(ev("a2_ready"), 1)
                    for kk in range(4):
                        ins = nc.scalar.activation(xaT[:, 4 * n + kk, :], bank(4, 2)[:, kk * SEQ:(kk + 1) * SEQ],
                                                   ACT.Copy, scale=a2[:, 4 * n + kk:4 * n + kk + 1])
                    ins.then_inc(ev("xaT_ready"), 1)
                    if n == 3:
                        act.wait_ge(ev("ss_summed"), 1)
                        nc.scalar.activation(rs2, ss, ACT.Sqrt, scale=1.0 / D, bias=eps).then_inc(ev("rms2"), 1)
                if s == ("N", 0):
                    act.wait_ge(ev("N_scaled0"), 1)
                    act.wait_ge(ev("B_scores"), 2)
                    act.wait_ge(ev("D_mixed"), 2)
                    act.dma_start(xtok, x[0].rearrange("(t p) d -> p t d", p=P)).then_inc(ev("x_in"), 16)

            act.wait_ge(ev("r_shifted"), 1)
            nc.scalar.activation(probs, probs, ACT.Exp).then_inc(ev("r_exp"), 1)
            act.wait_ge(ev("M_summed3"), 1)
            nc.scalar.activation(gate2_b, bank(4, 4), ACT.Copy).then_inc(ev("M_out3"), 1)
            act.wait_ge(ev("M_summed2"), 1)
            act.dma_start(fin_b, final_g.partition_broadcast(P)).then_inc(ev("fin_in"), 16)

            def take_gathered(L, u, count):
                act.wait_ge(L["gathered"], count)
                for kt in range(KT):
                    ins = nc.scalar.activation(xg[u][:, kt, 0:P], bank(4, 4)[:, kt * P:(kt + 1) * P], ACT.Identity,
                                               scale=a2[:, kt:kt + 1], bias=sh2[:, kt:kt + 1])
                ins.then_inc(L["xg_scaled"], 1)
                act.wait_ge(L["xg_scaled"], count)
                nc.scalar.activation(xg[u][:, :, P:192], xg[u][:, :, 0:XH], ACT.Copy).then_inc(L["xg_ready"], 1)

            def final_squares(L, n):
                for q in range(4):
                    if q < 2:
                        act.wait_ge(L["added_lo"], 2 * n + q)
                    else:
                        act.wait_ge(L["added_hi"], 2 * n + q - 1)
                    for t in range(NT):
                        nc.scalar.activation(junk_f, xacc[:, t, q * 512:(q + 1) * 512], ACT.Square,
                                             accum_out=ss8[:, t, q:q + 1]).then_inc(L["squared"], 1)
                        act.wait_ge(L["squared"], NT * q + t + 1)

            def expert(L, i, u):
                take_gathered(L, 1 - u, i * 2 + (u + 2))
                act.wait_ge(L["slot_used"], i * 24 + (12 * u + 8))
                nc.scalar.activation(hid, bank(0, 2), ACT.Silu).then_inc(L["silu_done"], 1)
                act.wait_ge(L["hid_transposed"], i * 2 + (u + 1))
                src = bank(4).rearrange("p (f n) -> p f n", n=P)
                nc.scalar.activation(hidT[:, 0:4, 0:P], src, ACT.Copy)
                nc.scalar.activation(hidT[:, 0:4, P:192], src[:, :, 0:XH], ACT.Copy).then_inc(L["hidT_act"], 1)

            act.wait_ge(ev("tables_ready"), 1)
            n_over = act.value_load(itab[0:1, 0:1], min_val=0, max_val=NOVER)
            take_gathered(main, 0, 1)
            with act.Fori(0, NE // 2) as i:
                for u in range(2):
                    expert(main, i, u)
            final_squares(main, NE)
            with act.If(n_over > 0):
                take_gathered(over, 0, 1)
                with act.Fori(0, NOVER // 2) as i:
                    for u in range(2):
                        expert(over, i, u)
                final_squares(over, NOVER)
            nc.scalar.activation(ssf, ss8, ACT.Copy).then_inc(ev("final_squared"), 1)
            act.wait_ge(ev("final_summed"), 1)
            nc.scalar.activation(rs3, ss, ACT.Sqrt, scale=1.0 / D, bias=eps).then_inc(ev("rms3"), 1)

        @block.tensor
        def _(pe):
            mm, tr = nc.tensor.matmul, nc.tensor.transpose
            pe.wait_ge(ev("params_in"), 160)
            pe.wait_ge(ev("ident_ready"), 1)
            tr(bank(0)[:, 0:NPAR], params[0:NPAR, :], ident[0:NPAR, 0:NPAR]).then_inc(ev("params_T"), 1)
            pe.wait_ge(ev("xn_ready"), 2)
            for b in range(4):
                if b == 0:
                    pe.wait_ge(ev("cols_ready"), 1)
                for kk in range(4):
                    for t in range(NT):
                        k = 4 * b + kk
                        ins = tr(bank(2 * b, 2)[:, kk * SEQ + t * P:kk * SEQ + (t + 1) * P],
                                 xtok[:, t, k * P:(k + 1) * P], ident)
                ins.then_inc(ev("xT"), 1)
            pe.wait_ge(mod_used, 14)
            pe.wait_ge(ev("h1_raw"), 1)
            for _ in range(6):
                mm(bank(1), ones, xtok[:, 0, 0:512], start=True, stop=True)
            pe.wait_ge(mod_used, 16)
            for j in range(32):
                ins = mm(bank(0)[:, j:j + 1], acc[0][:, j * P:(j + 1) * P], ones[:, 0:1], start=True, stop=True)
            ins.then_inc(ev("mod_summed"), 1)

            def group(g, half):
                if half == 0 or g == G_BKV:
                    if g >= 2:
                        pe.wait_ge(ev("group_out"), g - 1)
                    elif g == 0:
                        pe.wait_ge(ev("mod_cols"), 1)
                    if g == 1:
                        pe.wait_ge(ev("h1_raw"), 4)
                w = arrived(pe, ("g", g, half))
                two = bank(2 * (g % 2), 2)
                if g == G_BKV:
                    w = w.rearrange("p (k n) -> p k n", n=256)
                    kk, vv = two[:, 0:SEQ], two[:, 512:768]
                    for k in range(KT):
                        mm(kk, w[:, k, 0:P], h1T[:, k, :], start=(k == 0), stop=(k == KT - 1))
                    for t in range(NT):
                        for k in range(KT):
                            ins = mm(vv[:, t * P:(t + 1) * P], h1T[:, k, t * P:(t + 1) * P], w[:, k, P:256],
                                     start=(k == 0), stop=(k == KT - 1))
                    ins.then_inc(proj_used, 1)
                    return
                w = w.rearrange("p (k n) -> p k n", n=512)
                if g == G_DV:
                    for t in range(NT):
                        for kk in range(8):
                            k = 8 * half + kk
                            ins = mm(two[:, t * 512:(t + 1) * 512], h1T[:, k, t * P:(t + 1) * P], w[:, kk, :],
                                     start=(k == 0), stop=(k == KT - 1))
                else:
                    for kk in range(8):
                        if g == 0:
                            pe.wait_ge(ev("h1_ready"), 8 * half + kk + 1)
                        for m in range(4):
                            k = 8 * half + kk
                            ins = mm(two[:, m * SEQ:(m + 1) * SEQ], w[:, kk, m * P:(m + 1) * P], h1T[:, k, :],
                                     start=(k == 0 and m % 2 == 0), stop=(k == KT - 1 and m % 2 == 1),
                                     skip_group_check=True)
                ins.then_inc(proj_used, 1)

            def both(n):
                return bank(n).rearrange("p (j n) -> p j n", n=P)

            def values(w_a, w_b, v, head, done):
                for j in range(2):
                    for a in range(2):
                        o = bank(7)[64 * a:64 * a + 64, j * SEQ:(j + 1) * SEQ]
                        h = head(j, a)
                        mm(o, v[:, 0, h * 64:h * 64 + 64], w_a[:, 2 * a + j, :], start=True, stop=False)
                        ins = mm(o[:, P:SEQ], v[:, 1, h * 64:h * 64 + 64], w_b[:, 2 * a + j, :],
                                 start=False, stop=True)
                ins.then_inc(ev(done), 1)

            def router(n):
                for kt in range(4 * n, 4 * n + 4):
                    for t in range(NT):
                        ins = mm(bank(6)[:, t * NE:(t + 1) * NE], xaT[:, kt, t * P:(t + 1) * P], rw[:, kt, :],
                                 start=(kt == 0 and t == 0), stop=(kt == KT - 1 and t == 1), skip_group_check=True)
                return ins

            for s in STEPS:
                k, n = s[0], s[1]
                if k == "g":
                    group(n, s[2])
                elif k == "D1":
                    pe.wait_ge(ev("group_out"), 2)
                    if n == 0:
                        pe.wait_ge(ev("h1_raw"), 4)
                    else:
                        pe.wait_ge(ev("D_logw"), 1)
                        pe.wait_ge(ev("D_out"), 1)
                    for j in range(2):
                        for a in range(2):
                            kT, qT = dk[64 * a:64 * a + 64, 2 * n + j, :], dq[64 * a:64 * a + 64, 2 * n + j, :]
                            mm(bank(4 + a)[:, j * SEQ:(j + 1) * SEQ], kT[:, 0:P], qT, start=True, stop=True)
                    for j in range(2):
                        for a in range(2):
                            kT, qT = dk[64 * a:64 * a + 64, 2 * n + j, :], dq[64 * a:64 * a + 64, 2 * n + j, :]
                            ins = mm(bank(6 + a)[:, j * P:(j + 1) * P], kT[:, P:SEQ], qT[:, P:SEQ],
                                     start=True, stop=True)
                    ins.then_inc(ev("D_scores"), 1)
                elif k == "D2":
                    pe.wait_ge(ev("D_softp"), n + 1)
                    for a in range(2):
                        mm(bank(4 + a), lower, t_a[:, 2 * a:2 * a + 2, :], start=True, stop=False)
                        mm(bank(4 + a).rearrange("p (j n) -> p j n", n=SEQ)[:, :, P:SEQ], ones,
                           t_b[:, 2 * a:2 * a + 2, :], start=False, stop=True)
                    mm(bank(6), lower, t_b, start=True, stop=True).then_inc(ev("D_sums"), 1)
                elif k == "D3":
                    pe.wait_ge(ev("group_out"), G_DV + 1)
                    pe.wait_ge(ev("D_weights"), n + 1)
                    values(s_a, s_b, dv, lambda j, a: 2 * (2 * n + j) + a, "D_mixed")
                elif k == "N":
                    pe.wait_ge(ev(f"N_squares{n}"), 1)
                    if n == 0:
                        pe.wait_ge(ev("N_root1"), 1)
                    for j in range(4):
                        ins = mm(bank(4)[:, 0:SEQ], ones, squares[n][:, j, :], start=(j == 0), stop=(j == 3))
                    ins.then_inc(ev(f"N_summed{n}"), 1)
                elif k == "DT":
                    pe.wait_ge(ev("small_in"), 112)
                    pe.wait_ge(ev("D_out"), 2)
                    for t in range(NT):
                        for kk in range(KT):
                            ins = mm(bank(7)[:, t * 8:(t + 1) * 8], h1T[:, kk, t * P:(t + 1) * P], wdt[:, kk, :],
                                     start=(kk == 0), stop=(kk == KT - 1))
                    ins.then_inc(ev("dt_done"), 1)
                elif k == "C0":
                    pe.wait_ge(ev("da_ready"), 1)
                    for ch in range(NT):
                        ins = mm(bank(7)[:, ch * 8:(ch + 1) * 8], upper, da[:, ch * 8:(ch + 1) * 8],
                                 start=True, stop=True)
                    ins.then_inc(ev("cum_done"), 1)
                elif k == "C1":
                    pe.wait_ge(ev("C_dau"), n + 1)
                    pe.wait_ge(ev("xc_ready"), 1)
                    if n == 1:
                        pe.wait_ge(ev("C_state_out"), 1)
                        pe.wait_ge(ev("C_y"), 1)
                    tok = slice(n * P, (n + 1) * P)
                    for q in range(2):
                        mm(bank(4 + q), ones, da_u[:, 4 * q:4 * q + 4, :], start=True, stop=True)
                    for g in range(2):
                        mm(bank(6)[:, g * P:(g + 1) * P], xc[:, 4 + g, tok], xc[:, 6 + g, tok], start=True, stop=True)
                    if n == 0:
                        for g in range(2):
                            tr(bank(6)[:, 256 + g * P:256 + (g + 1) * P], xc[:, 4 + g, tok], ident)
                    for j in range(4):
                        ins = tr(bank(7)[:, j * P:(j + 1) * P], xc[:, j, tok], ident)
                    ins.then_inc(ev("C_parts"), 1)
                elif k == "C2":
                    pe.wait_ge(ev("C_mix"), n + 1)
                    if n == 0:
                        for g in range(2):
                            ins = mm(bank(6)[:, g * 256:(g + 1) * 256], bm_tok[:, g * P:(g + 1) * P],
                                     xw[:, 4 * g:4 * g + 4, :], start=True, stop=True)
                        ins.then_inc(ev("C_state"), 1)
                    for h in range(8):
                        o = bank(7)[64 * (h % 2):64 * (h % 2) + 64, (h // 2) * P:(h // 2 + 1) * P]
                        ins = mm(o, xdt[:, h, :], seg[:, h, :], start=True, stop=(n == 0))
                        if n == 1:
                            ins = mm(o, state[:, h, :], cum_e[:, h, :], start=False, stop=True)
                    ins.then_inc(ev("C_mixed"), 1)
                elif k == "B1":
                    pe.wait_ge(ev("group_out"), G_BKV + 1)
                    if n == 0:
                        pe.wait_ge(ev("N_root2"), 1)
                    else:
                        pe.wait_ge(ev("B_out"), 1)
                    for t, b0, width in ((1, 4, SEQ), (0, 6, P)):
                        for j in range(2):
                            for a in range(2):
                                rows = slice(64 * a, 64 * a + 64)
                                ins = mm(bank(b0 + a)[:, j * width:(j + 1) * width],
                                         bq[rows, 2 * n + j, t * P:(t + 1) * P], kdup[rows, n, 0:width],
                                         start=True, stop=True)
                    ins.then_inc(ev("B_scores"), 1)
                elif k == "B2":
                    pe.wait_ge(ev("B_probs"), n + 1)
                    for a in range(2):
                        for j in range(2):
                            h = 2 * a + j
                            tr(bank(4 + a)[:, j * SEQ:j * SEQ + P], s_b[:, h, :], ident)
                            tr(bank(4 + a)[:, j * SEQ + P:(j + 1) * SEQ], s_a[:, h, 0:P], ident)
                            ins = tr(bank(6)[:, h * P:(h + 1) * P], s_a[:, h, P:SEQ], ident)
                    ins.then_inc(ev("B_probsT"), 1)
                elif k == "B3":
                    pe.wait_ge(ev("B_probsT_out"), n + 1)
                    values(t_a, t_b, vB, lambda j, a: n, "B_mixed")
                elif k == "M" and n in (0, 3):
                    a = acc[2][:, D:] if n else acc[1][:, 0:D]
                    pe.wait_ge(mod_used, 48 if n else 32)
                    if n == 0:
                        pe.wait_ge(ev("N_root0"), 1)
                        pe.wait_ge(ev("B_out"), 2)
                    else:
                        pe.wait_ge(ev("logits_read"), 1)
                    for q in range(4):
                        ins = mm(bank(4 + q), ones, a[:, q * 512:(q + 1) * 512], start=True, stop=True)
                    ins.then_inc(ev(f"M_summed{n}"), 1)
                elif k == "M":
                    a = acc[1][:, D:] if n == 1 else acc[2][:, 0:D]
                    pe.wait_ge(mod_used, 32 if n == 1 else 48)
                    pe.wait_ge(ev("M_out0"), 1)
                    for j in range(KT):
                        ins = mm(bank(7)[:, 16 * (n - 1) + j:16 * (n - 1) + j + 1], a[:, j * P:(j + 1) * P],
                                 ones[:, 0:1], start=True, stop=True)
                    ins.then_inc(ev(f"M_summed{n}"), 1)
                elif k == "R":
                    pe.wait_ge(ev("x1_ready"), n + 1)
                    if n > 0:
                        pe.wait_ge(ev("xaT_ready"), n)
                    else:
                        pe.wait_ge(ev("M_out0"), 1)
                    for kk in range(4):
                        for t in range(NT):
                            kt = 4 * n + kk
                            ins = tr(bank(4, 2)[:, kk * SEQ + t * P:kk * SEQ + (t + 1) * P],
                                     x1[:, t, kt * P:(kt + 1) * P], ident)
                    ins.then_inc(ev("R_transposed"), 1)
                    if n == 1:
                        pe.wait_ge(ev("rw_sh_ready"), 1)
                        mm(bank(7)[:, 64:320], ones, rw_sh, start=True, stop=True)
                    if n > 0:
                        router(n - 1)
                    if n == 3:
                        pe.wait_ge(ev("xaT_ready"), 4)
                        router(3).then_inc(ev("r_logits"), 1)
                elif k == "wo":
                    half = s[2]
                    if half == 0:
                        pe.wait_ge(ev("N_scaled3"), 1)
                        pe.wait_ge(ev("N_scaled2"), 1)
                        if n == 0:
                            pe.wait_ge(ev("A_gated"), 1)
                        elif n == 1:
                            pe.wait_ge(ev("group_out"), 10)
                        else:
                            pe.wait_ge(ev("x1_ready"), n - 1)
                    else:
                        pe.wait_ge(ev("N_scaled1"), 1)
                        pe.wait_ge(ev("N_scaled0"), 1)
                    w = arrived(pe, s).rearrange("p (k n) -> p k n", n=512)
                    for t in range(NT):
                        for kk in range(8):
                            kt = 8 * (1 - half) + kk
                            ins = mm(bank(2 * (n % 2) + t), yT[:, kt, t * P:(t + 1) * P], w[:, kk, :],
                                     start=(half == 0 and kk == 0), stop=(half == 1 and kk == 7))
                    ins.then_inc(proj_used, 1)

            pe.wait_ge(ev("r_sel"), 1)
            mm(bank(1)[:, 0:16], strict, chosen[:, 0, :], start=True, stop=True)
            mm(bank(1)[:, 16:32], strict, chosen[:, 1, :], start=True, stop=False)
            mm(bank(1)[:, 16:32], ones, chosen[:, 0, :], start=False, stop=True)
            mm(bank(1)[:, 32:48], ones, chosen[:, 0, :], start=True, stop=False)
            mm(bank(1)[:, 32:48], ones, chosen[:, 1, :], start=False, stop=True).then_inc(ev("r_pos"), 1)

            def many(at_v):
                return pe.value_load(itab[0:1, bass.ds(at_v, 1)], min_val=0, max_val=1)

            def gather(L, count, flag):
                pe.wait_ge(L["onehot_ready"], count)

                def columns(w):
                    for kt in range(KT):
                        for t in range(NT):
                            ins = mm(bank(4, 4)[:, kt * P:kt * P + w], x1[:, t, kt * P:(kt + 1) * P],
                                     pos1h[:, t, 0:w], start=(t == 0), stop=(t == NT - 1))
                    ins.then_inc(L["gathered"], 1)

                with pe.If(flag > 0):
                    columns(P)
                with pe.Else():
                    columns(XH)

            def transpose_gates(L, count):
                pe.wait_ge(L["xg_ready"], count)
                for r in range(2):
                    for t in range(NT):
                        ins = tr(bank(4)[:, (2 * r + t) * P:(2 * r + t + 1) * P],
                                 gate1h[:, t, XH * r:XH * r + P], ident)
                ins.then_inc(L["pg_transposed"], 1)

            def combine(L, u, q, b):
                for h in range(2):
                    c0 = q * 512 + 256 * h
                    for t in range(NT):
                        ins = mm(bank(b + t)[:, 256 * h:256 * h + 256], pgT[u][:, 2 * h + t, :],
                                 y_sb[:, c0:c0 + 256], start=True, stop=True)
                ins.then_inc(L["combined"], 1)

            def expert(L, i, u, base, fills):
                few0 = many(i * 2 + (base + 8 + u))
                few1 = many(i * 2 + (base + 9 + u))

                def chunk(j):
                    pe.wait_ge(slot_full[j % NSLOT], i * 64 + 16 * (fills[j % NSLOT] + 2 * u + j // NSLOT + 1))
                    return at((j % NSLOT) * SLOT, SLOT)

                def gate_up(q):
                    ws = [chunk(2 * q + m).rearrange("p (k n) -> p k n", n=FF) for m in range(2)]

                    def products(full):
                        for m in range(2):
                            for kk in range(4):
                                kt = 4 * q + kk
                                for hf in range(2):
                                    if full:
                                        o, x0 = bank(2 * m + hf), xg[u][:, kt, XH * hf:XH * hf + P]
                                    else:
                                        o = bank(2 * m + hf)[XH * hf:XH * hf + XH, :]
                                        x0 = xg[u][:, kt, 0:XH]
                                    ins = mm(o, x0, ws[m][:, kk, hf * 512:(hf + 1) * 512],
                                             start=(kt == 0), stop=(kt == KT - 1))
                            ins.then_inc(L["slot_used"], 1)

                    with pe.If(few0 > 0):
                        products(True)
                    with pe.Else():
                        products(False)

                def down(q):
                    w = chunk(8 + q).rearrange("p (k n) -> p k n", n=512)

                    def products(full):
                        for f in range(8):
                            for h in range(2):
                                cs = slice(256 * h, 256 * h + 256)
                                if full:
                                    ins = mm(bank(4 + q)[:, cs], hidT[:, f, XH * h:XH * h + P], w[:, f, cs],
                                             start=(f == 0 and h == 0), stop=(f == 7 and h == 1),
                                             skip_group_check=True)
                                else:
                                    ins = mm(bank(4 + q)[XH * h:XH * h + XH, cs], hidT[:, f, 0:XH], w[:, f, cs],
                                             start=(f == 0), stop=(f == 7))
                        ins.then_inc(L["slot_used"], 1)

                    with pe.If(few0 > 0):
                        products(True)
                    with pe.Else():
                        products(False)

                pe.wait_ge(L["xg_ready"], i * 2 + (u + 1))
                pe.wait_ge(L["hid_ready"], i * 2 + (u + 1))
                pe.wait_ge(L["added_lo"], i * 4 + (2 * u + 1))
                gate_up(0)
                pe.wait_ge(L["y_ready"], i * 8 + (4 * u + 1))
                pe.wait_ge(L["added_hi"], i * 4 + (2 * u + 1))
                combine(L, 1 - u, 3, 4)
                gate_up(1)
                gate_up(2)
                pe.wait_ge(L["added_hi"], i * 4 + (2 * u + 2))
                gather(L, i * 2 + (u + 2), few1)
                gate_up(3)
                transpose_gates(L, i * 2 + (u + 2))
                pe.wait_ge(L["pg_ready"], i * 2 + (u + 2))
                pe.wait_ge(L["hid_ready"], i * 2 + (u + 2))
                for f in range(8):
                    ins = tr(bank(4, 2)[:, f * P:(f + 1) * P], hid[:, f * P:(f + 1) * P], ident)
                ins.then_inc(L["hid_transposed"], 1)
                pe.wait_ge(L["hidT_act"], i * 2 + (u + 1))
                pe.wait_ge(L["hidT_dve"], i * 2 + (u + 1))
                down(0)
                down(1)
                pe.wait_ge(L["y_ready"], i * 8 + (4 * u + 2))
                combine(L, u, 0, 0)
                down(2)
                pe.wait_ge(L["y_ready"], i * 8 + (4 * u + 3))
                combine(L, u, 1, 2)
                down(3)
                pe.wait_ge(L["y_ready"], i * 8 + (4 * u + 4))
                combine(L, u, 2, 4)

            def last_combine(L, n):
                pe.wait_ge(L["y_ready"], 4 * n + 1)
                pe.wait_ge(L["added_hi"], 2 * n + 1)
                combine(L, 1, 3, 4)

            pe.wait_ge(ev("tables_ready"), 1)
            pe.wait_ge(ev("M_out3"), 1)
            gather(main, 1, many(8))
            transpose_gates(main, 1)
            pe.wait_ge(main["pg_ready"], 1)
            with pe.Fori(0, NE // 2) as i:
                for u in range(2):
                    expert(main, i, u, 0, FILLS)
            last_combine(main, NE)
            pe.wait_ge(ev("main_done"), 1)
            n_over = pe.value_load(itab[0:1, 0:1], min_val=0, max_val=NOVER)
            with pe.If(n_over > 0):
                gather(over, 1, many(8 + NE))
                transpose_gates(over, 1)
                pe.wait_ge(over["pg_ready"], 1)
                with pe.Fori(0, NOVER // 2) as i:
                    for u in range(2):
                        expert(over, i, u, NE, [f + 2 * NE for f in FILLS])
                last_combine(over, NOVER)

        @block.vector
        def _(dve):
            V = nc.vector
            links = [0]

            def link(ins):
                links[0] += 1
                ins.then_inc(ev("dve_link"), 1)
                dve.wait_ge(ev("dve_link"), links[0])

            def tt(o, a, b, op):
                return V.tensor_tensor(o, a, b, op)

            def over_heads(a, n, w):
                return a.unsqueeze(1).broadcast_to([P, n, w])

            def over_cols(a, n, w):
                return a.unsqueeze(2).broadcast_to([P, n, w])

            def modulate(it):
                _, r, k = it
                w = arrived(dve, it)
                if k == 0:
                    dve.wait_ge(ev(f"bias_in{r}"), 16)
                else:
                    dve.wait_ge(mod_used, mod_no[it])
                V.scalar_tensor_tensor(acc[r], w, cond[:, k:k + 1], acc[r], ALU.mult, ALU.add).then_inc(mod_used, 1)

            V.memset(eps, EPS).then_inc(ev("eps_ready"), 1)
            dve.wait_ge(ev("cond_ready"), 1)
            V.memset(xraw[:, :, 0:3], 0.0)
            for k in range(KT):
                modulate(("mod", 0, k))
                if k == 3:
                    dve.wait_ge(ev("rms1"), 1)
                    link(V.reciprocal(rs, rs))
                    for t in range(NT):
                        V.tensor_scalar(xtok[:, t, :], xtok[:, t, :], rs[:, t:t + 1], None, ALU.mult)\
                         .then_inc(ev("xn_ready"), 1)
            dve.wait_ge(ev("mod_summed"), 1)
            V.tensor_copy(mod1, bank(0)[:, 0:32]).then_inc(ev("mod_cols"), 1)
            dve.wait_ge(ev("mod_cols"), 1)
            link(V.scalar_tensor_tensor(a1, mod1[:, 16:32], 1.0, cols[:, c_n1:c_n1 + 16], ALU.add, ALU.mult))
            dve.wait_ge(ev("h1_raw"), 4)
            for k in range(KT):
                V.tensor_scalar(h1T[:, k, :], h1T[:, k, :], a1[:, k:k + 1], mod1[:, k:k + 1], ALU.mult, ALU.add)\
                 .then_inc(ev("h1_ready"), 1)

            strict4 = over_heads(strict, 4, P)
            for n_step, s in enumerate(STEPS):
                k, n = s[0], s[1]
                if k in ("g", "wo"):
                    at_item = where[s] + 1
                    while at_item < NITEMS and ITEMS[at_item][0] == "mod":
                        modulate(ITEMS[at_item])
                        at_item += 1
                if s == ("g", 10, 1):
                    dve.wait_ge(ev("group_out"), 10)
                    dve.wait_ge(proj_used, pe_no[s] + 1)
                    link(V.memset(au[:, :, 0:2], 0.0))
                    V.tensor_tensor(au[:, :, 2:], bank(0, 2).rearrange("p (k n) -> p k n", n=SEQ), ac, ALU.mult)\
                     .then_inc(ev("A_gated"), 1)
                    dve.wait_ge(ev("A_gated"), 1)
                    for w in range(3):
                        for j in range(4):
                            cf = cols[:, c_ca + 4 * w + j:c_ca + 4 * w + j + 1]
                            if w == 0:
                                ins = V.tensor_scalar(ac[:, j, :], au[:, j, 0:SEQ], cf, None, ALU.mult)
                            else:
                                ins = V.scalar_tensor_tensor(ac[:, j, :], au[:, j, w:w + SEQ], cf, ac[:, j, :],
                                                             ALU.mult, ALU.add)
                        link(ins)
                    link(tt(yT[:, 0:4, :], ac, ab, ALU.mult))
                elif k == "D1":
                    dve.wait_ge(ev("D_ln"), n + 1)
                    link(V.scalar_tensor_tensor(t_all, s_all, 0.0, t_all, ALU.max, ALU.add))
                    tt(t_a[:, :, 0:P], t_a[:, :, 0:P], strict4, ALU.mult)
                    tt(t_b, t_b, strict4, ALU.mult).then_inc(ev("D_softp"), 1)
                elif k == "D2":
                    dve.wait_ge(ev("D_sums"), n + 1)
                    tt(s_a, s_a, bank(4, 2).rearrange("p (h n) -> p h n", n=SEQ), ALU.subtract)
                    link(tt(s_b, s_b, bank(6).rearrange("p (h n) -> p h n", n=P), ALU.subtract))
                    V.tensor_scalar(s_a[:, :, 0:P], s_a[:, :, 0:P], 0.0, None, ALU.min)
                    V.tensor_scalar(s_b, s_b, 0.0, None, ALU.min).then_inc(ev("D_logw"), 1)
                    dve.wait_ge(ev("D_exp"), n + 1)
                    tt(s_a[:, :, 0:P], s_a[:, :, 0:P], strict4, ALU.mult)
                    tt(s_b, s_b, strict4, ALU.mult).then_inc(ev("D_weights"), 1)
                elif k == "DT":
                    dve.wait_ge(ev("dt_done"), 1)
                    dve.wait_ge(ev("small_in"), 112)
                    tt(dtv.rearrange("p (t h) -> p t h", h=8), bank(7)[:, 0:16].rearrange("p (t h) -> p t h", h=8),
                       over_heads(dtb, NT, 8), ALU.add).then_inc(ev("dt_raw"), 1)
                    dve.wait_ge(ev("dt_ln"), 1)
                    link(V.scalar_tensor_tensor(dt, dtv, 0.0, dtw, ALU.max, ALU.add))
                    V.scalar_tensor_tensor(da.rearrange("p (t h) -> p t h", h=8), dt.rearrange("p (t h) -> p t h", h=8),
                                           -1.0, over_heads(ea, NT, 8), ALU.mult, ALU.mult).then_inc(ev("da_ready"), 1)
                    for a in range(2):
                        V.tensor_copy(dsk[64 * a:64 * a + 64, :],
                                      dsk8.rearrange("p (j a) -> p a j", a=2)[64 * a:64 * a + 64, a, :])
                    dve.wait_ge(ev("group_out"), G_BC + 1)
                    for w in range(4):
                        for j in range(8):
                            cf = cols[:, c_cw + 8 * w + j:c_cw + 8 * w + j + 1]
                            if w == 0:
                                ins = V.tensor_scalar(xc[:, j, :], xraw[:, j, 0:SEQ], cf,
                                                      cols[:, c_cb + j:c_cb + j + 1], ALU.mult, ALU.add)
                            else:
                                ins = V.scalar_tensor_tensor(xc[:, j, :], xraw[:, j, w:w + SEQ], cf, xc[:, j, :],
                                                             ALU.mult, ALU.add)
                        if w < 3:
                            link(ins)
                    ins.then_inc(ev("conv_done"), 1)
                elif k == "C0":
                    dve.wait_ge(ev("cum_done"), 1)
                    V.tensor_copy(cum, bank(7)[:, 0:16])
                    tt(da_u, over_heads(upper, 8, P), over_cols(da[:, 0:8], 8, P), ALU.mult).then_inc(ev("C_dau"), 1)
                    dve.wait_ge(ev("C_dau"), 1)
                elif k == "C1":
                    dve.wait_ge(ev("C_parts"), n + 1)
                    cumb = bank(4, 2).rearrange("p (h n) -> p h n", n=P)
                    cc = cum[:, 8 * n:8 * n + 8]
                    tt(seg, cumb, over_cols(cc, 8, P), ALU.subtract)
                    if n == 0:
                        link(tt(d2e, cumb[:, :, P - 1], cc, ALU.subtract))
                    else:
                        link(V.tensor_copy(cum_e, cumb))
                    V.tensor_scalar(seg, seg, 0.0, None, ALU.min).then_inc(ev("C_seg"), 1)
                    tt(cbm, bank(6)[:, 0:256].rearrange("p (g n) -> p g n", n=P), over_heads(upper, 2, P), ALU.mult)
                    if n == 0:
                        V.tensor_copy(bm_tok, bank(6)[:, 256:512])
                    link(tt(xdt, bank(7).rearrange("p (h n) -> p h n", n=64), over_cols(dt[:, 8 * n:8 * n + 8], 8, 64),
                            ALU.mult))
                    dve.wait_ge(ev("C_exp2"), n + 1)
                    if n == 0:
                        tt(xw, xdt, over_cols(d2e, 8, 64), ALU.mult)
                    else:
                        for g in range(2):
                            ce = cum_e[:, 4 * g:4 * g + 4, :]
                            tt(ce, ce, over_heads(xc[:, 6 + g, P:SEQ], 4, P), ALU.mult)
                    dve.wait_ge(ev("C_exp"), n + 1)
                    for g in range(2):
                        sg = seg[:, 4 * g:4 * g + 4, :]
                        ins = tt(sg, sg, over_heads(cbm[:, g, :], 4, P), ALU.mult)
                    ins.then_inc(ev("C_mix"), 1)
                    if n == 0:
                        tt(da_u, over_heads(upper, 8, P), over_cols(da[:, 8:16], 8, P), ALU.mult)\
                            .then_inc(ev("C_dau"), 1)
                elif k == "C2":
                    dve.wait_ge(ev("C_mixed"), n + 1)
                    tok = slice(n * P, (n + 1) * P)
                    for j in range(4):
                        ins = V.scalar_tensor_tensor(yT[:, 8 + j, tok], xc[:, j, tok], dsk[:, j:j + 1],
                                                     bank(7)[:, j * P:(j + 1) * P], ALU.mult, ALU.add)
                    ins.then_inc(ev("C_y"), 1)
                elif k == "B1":
                    dve.wait_ge(ev("B_scores"), n + 1)
                    dve.wait_ge(ev("masks_ready"), 5)
                    if n == 1:
                        dve.wait_ge(ev("B_out"), 1)
                    for a in range(2):
                        for j in range(2):
                            slope = 2.0 ** -(4 * n + 2 * j + a + 1)
                            V.scalar_tensor_tensor(s_a[:, 2 * a + j, :], dist, -slope,
                                                   bank(4 + a)[:, j * SEQ:(j + 1) * SEQ], ALU.mult, ALU.add)
                            ins = V.scalar_tensor_tensor(s_b[:, 2 * a + j, :], dist[:, P:SEQ], -slope,
                                                         bank(6 + a)[:, j * P:(j + 1) * P], ALU.mult, ALU.add)
                    link(ins)
                    V.reduce_max(mx[:, 0:4], s_b, AX)
                    link(V.reduce_max(mx[:, 4:8], s_a, AX))
                    sk = sink[:, 4 * n:4 * n + 4].rearrange("p (j a) -> p a j", a=2)
                    for q in range(2):
                        m = mx[:, 4 * q:4 * q + 4].rearrange("p (a j) -> p a j", a=2)
                        ins = tt(m, m, sk, ALU.max)
                    link(ins)
                    for q in range(2):
                        m, e = (z[:, 4 * q:4 * q + 4].rearrange("p (a j) -> p a j", a=2) for z in (mx, es))
                        tt(e, sk, m, ALU.subtract)
                    tt(s_b, s_b, over_cols(mx[:, 0:4], 4, P), ALU.subtract)
                    tt(s_a, s_a, over_cols(mx[:, 4:8], 4, SEQ), ALU.subtract).then_inc(ev("B_shifted"), 1)
                    dve.wait_ge(ev("B_exp"), n + 1)
                    V.reduce_sum(den[:, 0:4], s_b, AX)
                    link(V.reduce_sum(den[:, 4:8], s_a, AX))
                    link(tt(den, den, es, ALU.add))
                    link(V.reciprocal(den, den))
                    tt(s_b, s_b, over_cols(den[:, 0:4], 4, P), ALU.mult)
                    tt(s_a, s_a, over_cols(den[:, 4:8], 4, SEQ), ALU.mult).then_inc(ev("B_probs"), 1)
                elif k == "N":
                    yg = yT[:, 4 * n:4 * n + 4, :]
                    if n == 3:
                        dve.wait_ge(ev("D_out"), 2)
                    elif n == 1:
                        dve.wait_ge(ev("B_out"), 2)
                    elif n == 2:
                        dve.wait_ge(ev("C_y"), 2)
                        dve.wait_ge(ev("group_out"), G_Z + 1)
                        link(tt(yg, yg, zg, ALU.mult))
                    tt(squares[n], yg, yg, ALU.mult).then_inc(ev(f"N_squares{n}"), 1)
                    dve.wait_ge(ev(f"N_root{n}"), 1)
                    link(V.reciprocal(rstd_b, rstd_b))
                    for j in range(4):
                        ins = V.scalar_tensor_tensor(yg[:, j, :], yg[:, j, :], cols[:, c_gn[n] + j:c_gn[n] + j + 1],
                                                     rstd_b, ALU.mult, ALU.mult)
                    ins.then_inc(ev(f"N_scaled{n}"), 1)
                elif k == "wo" and s[2] == 1:
                    dve.wait_ge(proj_used, pe_no[s] + 1)
                    dve.wait_ge(ev("M_out0"), 1)
                    dve.wait_ge(ev("x_in"), 32)
                    if n > 0:
                        dve.wait_ge(ev("x1_ready"), n)
                    c5 = slice(n * 512, (n + 1) * 512)
                    link(tt(wo_tmp, bank(2 * (n % 2), 2).rearrange("p (t n) -> p t n", n=512),
                            over_heads(gate1_b[:, c5], NT, 512), ALU.mult))
                    tt(x1[:, :, c5], x1[:, :, c5], wo_tmp, ALU.add).then_inc(ev("x1_ready"), 1)

                elif s == ("M", 1):
                    dve.wait_ge(ev("M_summed1"), 1)
                    link(V.tensor_copy(sh2, bank(7)[:, 0:16]))
                    tt(rw_sh, rw, over_cols(sh2, KT, NE), ALU.mult).then_inc(ev("rw_sh_ready"), 1)
                elif s == ("M", 2):
                    dve.wait_ge(ev("M_summed2"), 1)
                    V.scalar_tensor_tensor(a2, bank(7)[:, 16:32], 1.0, cols[:, c_n2:c_n2 + 16], ALU.add, ALU.mult)\
                     .then_inc(ev("a2_ready"), 1)

            dve.wait_ge(ev("xaT_ready"), 4)
            V.reduce_sum(ss, ss8, AX).then_inc(ev("ss_summed"), 1)
            dve.wait_ge(ev("rms2"), 1)
            link(V.reciprocal(rs2, rs2))

            def per(a):
                return over_cols(a, NT, NE)

            dve.wait_ge(ev("r_logits"), 1)
            V.reduce_sum(shift_l, bank(7)[:, 64:320].rearrange("p (k e) -> p e k", e=NE), AX)
            link(tt(probs, bank(6)[:, 0:32].rearrange("p (t e) -> p t e", e=NE), per(rs2), ALU.mult))
            tt(probs, probs, over_heads(shift_l, NT, NE), ALU.add).then_inc(ev("logits_read"), 1)
            dve.wait_ge(ev("logits_read"), 1)
            link(V.reduce_max(r1, probs, AX))
            tt(probs, probs, per(r1), ALU.subtract).then_inc(ev("r_shifted"), 1)
            V.tensor_scalar(wdesc, iota[:, 0:NE], -1.0, 16.0, ALU.mult, ALU.add)
            dve.wait_ge(ev("r_exp"), 1)
            link(V.reduce_sum(r1, probs, AX))
            link(V.reciprocal(r1, r1))
            link(tt(probs, probs, per(r1), ALU.mult))
            link(tt(sel, probs, over_heads(rbias, NT, NE), ALU.add))
            s4 = sel.rearrange("p t (g e) -> p (t g) e", e=4)
            tt(q4[:, 0, :], s4[:, :, 0], s4[:, :, 1], ALU.max)
            tt(q4[:, 1, :], s4[:, :, 0], s4[:, :, 1], ALU.min)
            tt(q4[:, 2, :], s4[:, :, 2], s4[:, :, 3], ALU.max)
            link(tt(q4[:, 3, :], s4[:, :, 2], s4[:, :, 3], ALU.min))
            tt(q4[:, 4, :], q4[:, 0, :], q4[:, 2, :], ALU.max)
            tt(q4[:, 5, :], q4[:, 0, :], q4[:, 2, :], ALU.min)
            link(tt(q4[:, 6, :], q4[:, 1, :], q4[:, 3, :], ALU.max))
            link(tt(q4[:, 6, :], q4[:, 5, :], q4[:, 6, :], ALU.max))
            link(tt(gsc, q4[:, 4, :].rearrange("p (t g) -> p t g", g=4), q4[:, 6, :].rearrange("p (t g) -> p t g", g=4),
                    ALU.add))

            def first_best(o, v, n):
                link(V.reduce_max(r1, v, AX))
                link(tt(o, v, over_cols(r1, NT, n), ALU.is_equal))
                link(tt(o, o, over_heads(wdesc[:, 0:n], NT, n), ALU.mult))
                link(V.reduce_max(r1, o, AX))
                link(tt(o, o, over_cols(r1, NT, n), ALU.is_equal))

            first_best(gmask, gsc, 4)
            g8 = gmask.rearrange("p t g -> p (t g)")
            V.tensor_scalar(g8b, g8, -1.0, BIG, ALU.add, ALU.mult)
            link(tt(s4, s4, over_cols(g8, 8, 4), ALU.mult))
            link(tt(s4, s4, over_cols(g8b, 8, 4), ALU.add))
            first_best(chosen, sel, NE)
            link(V.scalar_tensor_tensor(sel, chosen, -3.0 * BIG, sel, ALU.mult, ALU.add))
            first_best(second, sel, NE)
            tt(chosen, chosen, second, ALU.add).then_inc(ev("r_sel"), 1)
            dve.wait_ge(ev("r_sel"), 1)
            link(tt(gates, probs, chosen, ALU.mult))
            link(V.reduce_sum(r1, gates, AX))
            link(V.reciprocal(r1, r1))
            link(tt(gates, gates, per(r1), ALU.mult))
            dve.wait_ge(ev("r_pos"), 1)
            V.tensor_copy(cnt, bank(1)[:, 32:48])
            link(V.scalar_tensor_tensor(pos, bank(1)[:, 0:32].rearrange("p (t e) -> p t e", e=NE), 1.0, chosen,
                                        ALU.add, ALU.mult))
            link(V.tensor_scalar(pos, pos, -1.0, None, ALU.add))
            V.tensor_copy(posx[:, 0:NE, :], pos.rearrange("p t e -> p e t"))
            V.tensor_copy(gatex[:, 0:NE, :], gates.rearrange("p t e -> p e t"))
            V.memset(posx[:, NV, :], -1.0)
            V.memset(gatex[:, NV, :], 0.0)
            V.memset(flags, 0.0)
            link(V.tensor_scalar(ovr, cnt, float(P), None, ALU.is_gt))
            link(V.tensor_tensor_scan(ovc, ones[:, 0:NE], ovr, 0.0, ALU.mult, ALU.add))
            link(tt(ovx, ovc, ovr, ALU.subtract))
            link(tt(ovm, over_heads(ovx, NOVER, NE), over_cols(iota[:, 0:NOVER], NOVER, NE), ALU.is_equal))
            link(tt(ovm, ovm, over_heads(ovr, NOVER, NE), ALU.mult))
            V.reduce_sum(ova, ovm, AX)
            link(tt(ovt, ovm, over_heads(iota[:, 0:NE], NOVER, NE), ALU.mult))
            link(V.reduce_sum(ove, ovt, AX))
            link(V.tensor_scalar(ova, ova, -1.0, None, ALU.add))

            def pick(o, table):
                link(tt(ovt, ovm, over_heads(table, NOVER, NE), ALU.mult))
                link(V.reduce_sum(o, ovt, AX))

            V.tensor_scalar(cntq, cnt, -float(P), None, ALU.add)
            link(V.tensor_scalar(posq, pos, -float(P), None, ALU.add))
            for t in range(NT):
                pick(ovo, posq[:, t, :])
                link(tt(posx[:, NE:NV, t], ovo, ova, ALU.add))
                pick(gatex[:, NE:NV, t], gates[:, t, :])
            pick(ovo, cntq)
            V.tensor_scalar(flags[:, 8:8 + NE], cnt, float(XH), None, ALU.is_gt)
            link(V.tensor_scalar(flags[:, 8 + NE:8 + NV], ovo, float(XH), None, ALU.is_gt))
            V.tensor_copy(flags[:, 0:1], ovc[:, NE - 1:NE])
            link(V.tensor_copy(flags[:, 32:32 + NOVER], ove))
            V.tensor_copy(itab[0:1, 0:40], flags[0:1, 0:40]).then_inc(ev("tables_ready"), 1)

            def onehot(L, col):
                for t in range(NT):
                    pc = mem[:, bass.ds(col * NT + (posx_at + t), 1)]
                    gc = mem[:, bass.ds(col * NT + (gatex_at + t), 1)]
                    V.tensor_scalar(pos1h[:, t, :], iota[:, 0:P], pc, rs2[:, t:t + 1], ALU.is_equal, ALU.mult)
                    ins = V.tensor_scalar(gate1h[:, t, :], iota, pc, gc, ALU.is_equal, ALU.mult)
                ins.then_inc(L["onehot_ready"], 1)

            def take_gates(L, u, count):
                dve.wait_ge(L["pg_transposed"], count)
                V.tensor_copy(pgT[u], bank(4).rearrange("p (r n) -> p r n", n=P)).then_inc(L["pg_ready"], 1)

            def add_combined(L, q, b, sem, count):
                dve.wait_ge(L["combined"], count)
                xq = xacc[:, :, q * 512:(q + 1) * 512]
                tt(xq, xq, bank(b, 2).rearrange("p (t n) -> p t n", n=512), ALU.add).then_inc(L[sem], 1)

            def expert(L, i, u, base):
                dve.wait_ge(L["pg_transposed"], i * 2 + (u + 1))
                onehot(L, i * 2 + (base + u + 1))
                add_combined(L, 3, 4, "added_hi", i * 8 + (4 * u + 1))
                take_gates(L, 1 - u, i * 2 + (u + 2))
                dve.wait_ge(L["silu_done"], i * 2 + (u + 1))
                tt(hid, hid, bank(2, 2), ALU.mult).then_inc(L["hid_ready"], 1)
                dve.wait_ge(L["hid_transposed"], i * 2 + (u + 1))
                src = bank(5).rearrange("p (f n) -> p f n", n=P)
                V.tensor_copy(hidT[:, 4:8, XH:192], src)
                V.tensor_copy(hidT[:, 4:8, 0:XH], src[:, :, XH:P]).then_inc(L["hidT_dve"], 1)
                for q in range(4):
                    c5 = slice(q * 512, (q + 1) * 512)
                    dve.wait_ge(L["slot_used"], i * 24 + (12 * u + 9 + q))
                    tt(y_sb[:, c5], bank(4 + q), gate2_b[:, c5], ALU.mult).then_inc(L["y_ready"], 1)
                    if q > 0:
                        add_combined(L, q - 1, 2 * (q - 1) if q < 3 else 4, "added_lo" if q < 3 else "added_hi",
                                     i * 8 + (4 * u + q + 1))

            def start_pass(L, first):
                V.memset(hid, 0.0).then_inc(L["hid_ready"], 1)
                V.memset(pgT[1], 0.0).then_inc(L["added_lo"], 1)
                V.memset(y_sb[:, 0:1024], 0.0).then_inc(L["added_hi"], 1)
                V.memset(y_sb[:, 1024:D], 0.0).then_inc(L["y_ready"], 1)
                onehot(L, first)
                take_gates(L, 0, 1)

            dve.wait_ge(ev("tables_ready"), 1)
            start_pass(main, 0)
            n_over = dve.value_load(itab[0:1, 0:1], min_val=0, max_val=NOVER)
            dve.wait_ge(ev("M_out3"), 1)
            dve.wait_ge(ev("xacc_ready"), 1)
            with dve.Fori(0, NE // 2) as i:
                for u in range(2):
                    expert(main, i, u, 0)
            add_combined(main, 3, 4, "added_hi", 4 * NE + 1)
            V.memset(r1, 0.0).then_inc(ev("main_done"), 1)
            with dve.If(n_over > 0):
                dve.wait_ge(main["squared"], 8)
                start_pass(over, NE)
                with dve.Fori(0, NOVER // 2) as i:
                    for u in range(2):
                        expert(over, i, u, NE)
                add_combined(over, 3, 4, "added_hi", 4 * NOVER + 1)
            dve.wait_ge(ev("final_squared"), 1)
            V.reduce_sum(ss, ssf, AX).then_inc(ev("final_summed"), 1)
            dve.wait_ge(ev("rms3"), 1)
            dve.wait_ge(ev("fin_in"), 16)
            link(V.reciprocal(rs3, rs3))
            for t in range(NT):
                for h in range(2):
                    half = slice(h * 1024, (h + 1) * 1024)
                    V.scalar_tensor_tensor(xacc[:, t, half], xacc[:, t, half], rs3[:, t:t + 1], fin_b[:, half],
                                           ALU.mult, ALU.mult).then_inc(ev("out_ready"), 1)


_INS = ["x", "c", "w_mod", "b_mod", "norm1_g", "norm2_g", "w_in", "w_out", "conv_a_w", "gn_a", "attn_sinks",
        "gn_b", "ssm_conv_w", "ssm_conv_b", "dt_bias", "a_log", "d_skip", "ssm_norm_g", "gn_d", "router_w",
        "router_bias", "moe_w_gate", "moe_w_up", "moe_w_down", "final_g"]


def kernel(**inputs):
    import numpy as _np
    import concourse.bacc as _bacc
    from concourse import mybir as _mybir
    from concourse.bass_utils import run_bass_kernel_spmd as _run

    nc = _bacc.Bacc("TRN2", target_bir_lowering=False, num_devices=1)
    arrays, args = {}, []
    for name in _INS:
        a = _np.ascontiguousarray(inputs[name])
        arrays[f"in_{name}"] = a
        args.append(nc.dram_tensor(f"in_{name}", a.shape, _mybir.dt.from_np(a.dtype), kind="ExternalInput").ap())
    out = nc.dram_tensor("out_0", (1, SEQ, D), F32, kind="ExternalOutput").ap()
    trunk(nc, *args, out)
    r = _run(nc, [arrays], core_ids=[0])
    return r.results[0]["out_0"]
```

```python
from contextlib import ExitStack

import numpy as np
import concourse.bass as bass
from concourse import mybir

F32 = mybir.dt.float32
I32 = mybir.dt.int32
ALU = mybir.AluOpType
ACT = mybir.ActivationFunctionType
AX = mybir.AxisListType.X

D = 2048
SEQ = 256
P = 128
NT = SEQ // P
KT = D // P
GW = 512
NE = 16
FF = 1024
EXPERT = D * FF
EPS = 1e-6
SLOT = 4096
NSLOT = 6
NSLOT_B = 4
XH = 64
NOVER = 4
NV = NE + NOVER
BIG = 1e30

A_B, A_C, A_X = 0, 512, 1024
B_Q, B_KV = 1536, 2048
C_Z, C_XS, C_BC, C_DT = 2304, 2816, 3328, 3840
D_Q, D_K, D_V = 3848, 4360, 4872
FIRSTW = 3 * GW + 2 * P
GROUPS = [D_Q, D_K, D_V, C_XS, C_BC, B_Q, B_KV, C_Z, A_B, A_C, A_X]
G_DQ, G_DK, G_DV, G_XS, G_BC, G_BQ, G_BKV, G_Z, G_AB, G_AC, G_AX = range(11)

STEPS = [
    ("g", 3, 0), ("D1", 0), ("g", 3, 1), ("D2", 0), ("g", 4, 0), ("D3", 0), ("D1", 1), ("g", 4, 1),
    ("D2", 1), ("g", 5, 0), ("D3", 1), ("N", 3), ("DT", 0), ("g", 5, 1), ("C0", 0), ("g", 7, 0), ("C1", 0),
    ("g", 7, 1), ("C2", 0), ("C1", 1), ("g", 8, 0), ("C2", 1), ("g", 8, 1), ("N", 2),
    ("g", 9, 0), ("B1", 0), ("g", 9, 1), ("B2", 0), ("g", 10, 0), ("B3", 0), ("B1", 1), ("g", 10, 1), ("B2", 1),
    ("wo", 0, 0), ("B3", 1), ("N", 0), ("wo", 1, 0), ("N", 1), ("M", 0), ("wo", 0, 1), ("M", 1),
    ("wo", 1, 1), ("wo", 2, 0), ("M", 2), ("R", 0), ("wo", 2, 1), ("R", 1), ("wo", 3, 0), ("R", 2),
    ("wo", 3, 1), ("R", 3), ("M", 3),
]


def expert_at(v):
    return v // 4 + 4 * (v % 4)


def stream():
    items = []
    for j in range(KT // 2):
        items += [("cols", 2 * j), ("cols", 2 * j + 1), ("first", j)]
    left = [("mod", r, k) for r in (1, 2) for k in range(KT)]
    n = 0
    for s in STEPS:
        if s[0] in ("g", "wo"):
            items.append(s)
            for _ in range(1 if n % 3 == 2 else 2):
                if left:
                    items.append(left.pop(0))
            n += 1
    assert not left
    return items


def trunk(nc, x, c, w_mod, b_mod, norm1_g, norm2_g, w_in, w_out, conv_a_w, gn_a, attn_sinks, gn_b,
          ssm_conv_w, ssm_conv_b, dt_bias, a_log, d_skip, ssm_norm_g, gn_d, router_w, router_bias,
          moe_w_gate, moe_w_up, moe_w_down, final_g, out):
    ctx = ExitStack()
    with ctx:
        mem = ctx.enter_context(nc.sbuf_tensor("mem", [P, 53120], F32))
        itab = ctx.enter_context(nc.sbuf_tensor("itab", [1, 64], I32))
        ps = ctx.enter_context(nc.psum_tensor("ps", [P, 4096], F32))

        def at(start, *shape):
            n = int(np.prod(shape))
            a = mem[:, start:start + n]
            if len(shape) == 2:
                a = a.rearrange("p (a b) -> p a b", b=shape[1])
            elif len(shape) == 3:
                a = a.rearrange("p (a b c) -> p a b c", b=shape[1], c=shape[2])
            return a

        def bank(b, n=1):
            return ps[:, 512 * b:512 * (b + n)]

        H1 = NSLOT * SLOT
        ACC_A, ACC_B = H1 + 4096, H1 + 8192
        REST = H1 + 12288
        X1, YT, XG, CONST = REST, REST + 4096, REST + 8192, REST + 8192 + 6144
        WC = NSLOT_B * SLOT
        WD = WC + 5120

        h1T = at(H1, KT, SEQ)
        acc = [None, at(ACC_B, 4096), at(ACC_A, 4096)]
        xtok = at(X1, NT, D)
        yT = at(YT, KT, SEQ)
        dq, dk, dv = at(X1, 4, SEQ), at(X1 + 1024, 4, SEQ), at(X1 + 2048, NT, GW)
        ab, ac, au = at(X1, 4, SEQ), at(X1 + 1024, 4, SEQ), at(X1 + 2048, 4, SEQ + 2)
        kdup = at(X1 + 3088, 2, SEQ)
        xraw = at(XG, 8, SEQ + 3)
        zg = at(XG, 4, SEQ)
        xc = at(XG + 2072, 8, SEQ)
        bq = at(XG + 4120, 4, SEQ)
        rstd_b = at(XG + 5144, SEQ)
        vB = at(XG + 5400, NT, P)
        ACT_TILES = 7
        prod = at(YT, KT, 2 * P)
        red = at(XG + 2072, NT, 2 * P)
        diag = at(XG + 2584, NT, P)
        b1 = at(XG + 2840, 32)
        params_b = at(XG + P, P)
        params = at(XG, P)
        wo_tmp = at(XG, NT, GW)
        da_u = at(WC, 8, P)
        seg = at(WC + 1024, 8, P)
        cum_e = at(WC + 2048, 8, P)
        dtT = at(WC + 2048, SEQ)
        cbm = at(WC + 3072, 2, P)
        bm_tok = at(WC + 3328, 2 * P)
        xdt = at(WC + 3584, 8, 64)
        xw = at(WC + 4096, 8, 64)
        state = at(WC + 4608, 8, 64)
        s_a, s_b = at(WD, 4, SEQ), at(WD + 1024, 4, P)
        t_a, t_b = at(WD + 1536, 4, SEQ), at(WD + 2560, 4, P)
        s_all, t_all = at(WD, 1536), at(WD + 1536, 1536)
        x1 = xtok
        xacc = at(YT, NT, D)
        xaT = h1T
        xg = [at(XG + 3072 * u, KT, 192) for u in range(2)]
        y_sb = at(H1, D)
        pos1h = at(H1 + 2048, NT, P)
        gate1h = at(H1 + 2304, NT, 192)
        RT = H1 + 2688
        rt = [RT]

        def route(*shape):
            a = at(rt[0], *shape)
            rt[0] += int(np.prod(shape))
            return a

        probs, sel, chosen, second, gates, pos, posq = (route(NT, NE) for _ in range(7))
        gsc, gmask, q4, g8b, r1 = route(NT, 4), route(NT, 4), route(7, 8), route(8), route(NT)
        wdesc, cnt, cntq, ovr, ovc, ovx, shift_l = (route(NE) for _ in range(7))
        ovm, ovt = route(NOVER, NE), route(NOVER, NE)
        ova, ove, ovo, flags = route(NOVER), route(NOVER), route(NOVER), route(64)
        posx_at = rt[0]
        posx = route(NV + 1, NT)
        gatex_at = rt[0]
        gatex = route(NV + 1, NT)
        assert rt[0] <= H1 + 4096, rt[0] - H1
        pgT = [at(ACC_B + 512 * u, 4, P) for u in range(2)]
        hid = at(ACC_B + 1024, FF)
        hidT = at(ACC_B + 2048, 8, 192)
        junk = at(XG + 1024, 512)
        rw_sh = at(XG + 1536, KT, NE)
        junk_f = hid[:, 0:512]
        gate1_b, gate2_b = at(ACC_B, D), at(ACC_A + D, D)
        fin_b = at(ACC_A, D)

        cur = [CONST]

        def small(*shape):
            a = at(cur[0], *shape)
            cur[0] += int(np.prod(shape))
            return a

        ident, ones = small(P), small(P)
        upper = small(P)
        lower = small(P)
        strict = small(P)
        dist = small(SEQ)
        iota = small(192)
        cols = small(P)
        rw = small(KT, NE)
        wdt = small(KT, 8)
        dtb, alog, sink, rbias, dsk8, dsk = small(8), small(8), small(8), small(NE), small(8), small(4)
        cond, mod1, a1 = small(16), small(32), small(16)
        sh2, a2 = small(16), small(16)
        ss, rs, rs2, rs3, eps = small(2), small(2), small(2), small(2), small(1)
        ss8, ssf = small(NT, 4), small(NT, 4)
        dtv, dtw, dt, da, cum = small(16), small(16), small(16), small(16), small(16)
        ea, d2e = small(8), small(8)
        mx, den, es = small(8), small(8), small(8)
        assert cur[0] <= 53120, cur[0]
        squares = [ac, at(WD + 1536, 4, SEQ), at(WC + 1024, 4, SEQ), at(WD + 1536, 4, SEQ)]
        c_c, c_n1, c_ca, c_cw, c_cb = 0, 16, 32, 44, 76
        c_gn = [84, 88, 92, 96]
        c_n2 = 100
        NPAR = 116

        sems = {}

        def ev(name):
            if name not in sems:
                sems[name] = ctx.enter_context(nc.semaphore(name))
            return sems[name]

        ITEMS = stream()
        where = {it: n for n, it in enumerate(ITEMS)}
        NITEMS = len(ITEMS)
        slot_full = [ev(f"slot_full{s}") for s in range(NSLOT)]
        mod_used, proj_used = ev("mod_used"), ev("proj_used")
        mods = [it for it in ITEMS if it[0] == "mod"]
        pes = [it for it in ITEMS if it[0] not in ("mod", "cols")]
        mod_no = {it: n for n, it in enumerate(mods)}
        pe_no = {it: n for n, it in enumerate(pes)}

        NFIRST = KT + KT // 2
        slot_of = [n % NSLOT if n < NFIRST else (n - NFIRST) % NSLOT_B for n in range(NITEMS)]

        def last_in(slot, before):
            return max((n for n in range(before) if slot_of[n] == slot), default=None)

        def transfers(last, slot):
            return sum(2 if n < NFIRST else 1 for n in range(last + 1) if slot_of[n] == slot)

        FILLS = [transfers(NITEMS - 1, s) for s in range(NSLOT)]

        def used(it):
            if it[0] == "cols":
                return ev("cols_summed"), it[1] + 1
            return (mod_used, mod_no[it] + 1) if it[0] == "mod" else (proj_used, pe_no[it] + 1)

        def arrived(eng, it):
            n = where[it]
            eng.wait_ge(slot_full[slot_of[n]], 16 * transfers(n, slot_of[n]))
            return at(slot_of[n] * SLOT, SLOT)

        def pair(g):
            return 2 if g in (G_XS, G_BQ, G_AB, G_AX) else 0

        def bcast_rows(src, n, rows=P):
            return bass.AP(src.tensor, src.offset, [[0, rows], [1, n]])

        def loop_sems(tag):
            return {n: ev(f"{tag}_{n}") for n in (
                "slot_used", "onehot_ready", "gathered", "xg_ready", "pg_transposed", "pg_ready", "silu_done",
                "hid_ready", "hid_transposed", "xg_scaled", "squared", "hidT_act", "hidT_dve", "y_ready", "combined", "added_lo", "added_hi")}

        main, over = loop_sems("main"), loop_sems("over")

        block = ctx.enter_context(nc.Block())

        @block.sync
        def _(sp):
            sp.dma_start(mem[0:16, XG:XG + P], c.rearrange("b (k p) -> (b k) p", p=P)).then_inc(ev("params_in"), 16)
            sp.dma_start(mem[16:32, XG:XG + P], norm1_g.rearrange("b (k p) -> (b k) p", p=P)).then_inc(ev("params_in"), 16)
            sp.dma_start(mem[32:44, XG:XG + P], conv_a_w.rearrange("b w (k p) -> (b w k) p", p=P)).then_inc(ev("params_in"), 16)
            sp.dma_start(mem[44:76, XG:XG + P], ssm_conv_w.rearrange("b w (k p) -> (b w k) p", p=P)).then_inc(ev("params_in"), 16)
            sp.dma_start(mem[76:84, XG:XG + P], ssm_conv_b.rearrange("b (k p) -> (b k) p", p=P)).then_inc(ev("params_in"), 16)
            for i, g in enumerate((gn_a, gn_b, ssm_norm_g, gn_d)):
                sp.dma_start(mem[84 + 4 * i:88 + 4 * i, XG:XG + P], g.rearrange("b (k p) -> (b k) p", p=P)).then_inc(ev("params_in"), 16)
            sp.dma_start(mem[100:116, XG:XG + P], norm2_g.rearrange("b (k p) -> (b k) p", p=P)).then_inc(ev("params_in"), 16)
            sp.dma_start(mem[0:32, XG + P:XG + 2 * P], b_mod[:, 0:4096].rearrange("b (k p) -> (b k) p", p=P)).then_inc(ev("params_in"), 16)
            for n, it in enumerate(ITEMS):
                slot = slot_of[n]
                if last_in(slot, n) is not None:
                    sp.wait_ge(*used(ITEMS[last_in(slot, n)]))
                dst = at(slot * SLOT, SLOT)
                if it[0] == "mod":
                    _, r, k = it
                    src = w_mod[0, k * P:(k + 1) * P, r * 4096:(r + 1) * 4096]
                elif it[0] == "cols":
                    dst = dst.rearrange("p (r m n) -> p r m n", m=2, n=P)
                    for m in range(2):
                        src = w_mod[0, :, m * D + it[1] * P:m * D + (it[1] + 1) * P]
                        sp.dma_start(dst[:, :, m, :], src.rearrange("(r p) n -> p r n", p=P))\
                          .then_inc(slot_full[slot], 16)
                    continue
                elif it[0] == "first":
                    rows = w_in[0, it[1] * 2 * P:(it[1] + 1) * 2 * P, :].rearrange("(k p) n -> p k n", p=P)
                    dst = dst[:, 0:2 * FIRSTW].rearrange("p (k n) -> p k n", k=2)
                    sp.dma_start(dst[:, :, 0:3 * GW], rows[:, :, D_Q:D_Q + 3 * GW]).then_inc(slot_full[slot], 16)
                    sp.dma_start(dst[:, :, 3 * GW:], rows[:, :, B_KV:B_KV + 2 * P]).then_inc(slot_full[slot], 16)
                    continue
                elif it[0] == "g":
                    _, g, half = it
                    dst = dst.rearrange("p (k n) -> p k n", n=512)
                    src = w_in[0, half * 1024:(half + 1) * 1024, GROUPS[g]:GROUPS[g] + 512]\
                        .rearrange("(k p) n -> p k n", p=P)
                else:
                    _, n4, half = it
                    r0 = 1024 * (1 - half)
                    dst = dst.rearrange("p (k n) -> p k n", n=512)
                    src = w_out[0, r0:r0 + 1024, n4 * 512:(n4 + 1) * 512].rearrange("(k p) n -> p k n", p=P)
                sp.dma_start(dst, src).then_inc(slot_full[slot], 16)

            def expert_chunk(j, start, sem=None, count=None):
                if sem is not None:
                    sp.wait_ge(sem, count)
                if j < 8:
                    w, first, pitch, width = (moe_w_gate, moe_w_up)[j % 2], (j // 2) * 512 * FF, FF, FF
                else:
                    w, first, pitch, width = moe_w_down, (j - 8) * 512, D, 512
                tiles = SLOT // width
                src = bass.AP(w.tensor, start + first, [[pitch, P], [P * pitch, tiles], [1, width]])
                dst = at((j % NSLOT) * SLOT, SLOT).rearrange("p (k n) -> p k n", n=width)
                sp.dma_start(dst, src).then_inc(slot_full[j % NSLOT], 16)

            for j in range(NSLOT):
                if j < NSLOT_B:
                    sp.wait_ge(*used(ITEMS[last_in(j, NITEMS)]))
                elif j == NSLOT_B:
                    sp.wait_ge(ev("N_scaled0"), 1)
                    sp.wait_ge(ev("N_scaled1"), 1)
                    sp.wait_ge(ev("N_scaled2"), 1)
                    sp.wait_ge(ev("N_scaled3"), 1)
                expert_chunk(j, 0)
            with sp.Fori(0, NE // 4 - 1) as a:
                starts = [(a + expert_at(q)) * EXPERT for q in range(5)]
                starts_down = [(a * 2) * (EXPERT // 2) + expert_at(q) * EXPERT for q in range(5)]
                for m in range(48):
                    q, j = divmod(m + 6, 12)
                    expert_chunk(j, (starts if j < 8 else starts_down)[q], main["slot_used"], a * 48 + (m + 1))
            for m in range(48 * (NE // 4 - 1), 12 * NE - 6):
                sp.wait_ge(main["slot_used"], m + 1)
                expert_chunk((m + 6) % 12, expert_at((m + 6) // 12) * EXPERT)
            sp.wait_ge(ev("main_done"), 1)
            n_over = sp.value_load(itab[0:1, 0:1], min_val=0, max_val=NOVER)
            with sp.If(n_over > 0):
                def first_element(at_v):
                    e = sp.value_load(itab[0:1, bass.ds(at_v, 1)], min_val=0, max_val=NE - 1)
                    return e * EXPERT, (e * 2) * (EXPERT // 2)

                start = first_element(32)
                for j in range(NSLOT):
                    expert_chunk(j, start[0])
                with sp.Fori(0, NOVER - 1) as v:
                    here, after = first_element(v + 32), first_element(v + 33)
                    for m in range(12):
                        q, j = divmod(m + 6, 12)
                        expert_chunk(j, (after if q else here)[j // 8], over["slot_used"], v * 12 + (m + 1))
                start = first_element(32 + NOVER - 1)
                for j in range(NSLOT, 12):
                    expert_chunk(j, start[j // 8], over["slot_used"], 12 * (NOVER - 1) + j - NSLOT + 1)
            for n in range(4):
                t, half = divmod(n, 2)
                sp.wait_ge(ev("out_ready"), n + 1)
                sp.dma_start(out[0, t * P:(t + 1) * P, half * 1024:(half + 1) * 1024],
                             xacc[:, t, half * 1024:(half + 1) * 1024]).then_inc(ev("out_written"), 16)
            sp.wait_ge(ev("out_written"), 64)

        @block.gpsimd
        def _(pool):
            nc.gpsimd.memset(ident, 0.0)
            nc.gpsimd.memset(upper, 1.0)
            nc.gpsimd.memset(lower, 1.0)
            nc.gpsimd.memset(strict, 1.0)
            nc.gpsimd.memset(ones, 1.0).then_inc(ev("masks_filled"), 1)
            pool.wait_ge(ev("masks_filled"), 1)

            def select(m, op, fill, base, step, mult, name):
                nc.gpsimd.affine_select(out=m, in_=m, compare_op=op, fill=fill, base=base,
                                        pattern=[[step, m.shape[1]]], channel_multiplier=mult)\
                  .then_inc(ev(name), 1)

            select(ident, ALU.not_equal, 1.0, 0, -1, 1, "ident_ready")
            select(upper, ALU.is_ge, 0.0, 0, 1, -1, "masks_ready")
            select(lower, ALU.is_ge, 0.0, 0, -1, 1, "masks_ready")
            select(strict, ALU.is_gt, 0.0, 0, 1, -1, "masks_ready")
            nc.gpsimd.iota(dist, pattern=[[-1, SEQ]], base=P, channel_multiplier=1,
                           allow_small_or_imprecise_dtypes=True).then_inc(ev("dist_filled"), 1)
            pool.wait_ge(ev("dist_filled"), 1)
            select(dist, ALU.is_ge, BIG, P, -1, 1, "dist_cut")
            pool.wait_ge(ev("dist_cut"), 1)
            select(dist, ALU.is_gt, BIG, 0, 1, -1, "masks_ready")
            nc.gpsimd.iota(iota[:, 0:P], pattern=[[1, P]], base=0, channel_multiplier=0,
                           allow_small_or_imprecise_dtypes=True)
            nc.gpsimd.iota(iota[:, P:192], pattern=[[1, XH]], base=0, channel_multiplier=0,
                           allow_small_or_imprecise_dtypes=True).then_inc(ev("masks_ready"), 1)
            nc.gpsimd.memset(acc[1], 0.0).then_inc(ev("acc_zeroed1"), 1)
            nc.gpsimd.memset(acc[2], 0.0).then_inc(ev("acc_zeroed2"), 1)
            pool.wait_ge(ev("x1_ready"), 4)
            nc.gpsimd.tensor_copy(xacc, x1).then_inc(ev("xacc_ready"), 1)

        @block.scalar
        def _(act):
            links = [0]

            def link(ins):
                links[0] += 1
                ins.then_inc(ev("act_link"), 1)
                act.wait_ge(ev("act_link"), links[0])

            act.dma_start(xtok, x[0].rearrange("(t p) d -> p t d", p=P)).then_inc(ev("x_in"), 16)

            act.wait_ge(ev("params_T"), 1)
            nc.scalar.activation(b1, bank(6)[:, P:P + 32], ACT.Copy)
            nc.scalar.activation(cols[:, 0:NPAR], bank(6)[:, 0:NPAR], ACT.Copy).then_inc(ev("cols_ready"), 1)
            act.wait_ge(ev("cols_ready"), 1)
            nc.scalar.activation(cond, cols[:, 0:16], ACT.Silu).then_inc(ev("cond_ready"), 1)

            def multiply_cols(k):
                w = arrived(act, ("cols", k)).rearrange("p (r n) -> p r n", n=2 * P)
                if k > 0:
                    act.wait_ge(ev("red_ready"), k)
                for r in range(ACT_TILES):
                    ins = nc.scalar.activation(prod[:, r, :], w[:, r, :], ACT.Copy, scale=cond[:, r:r + 1])
                ins.then_inc(ev("cols_multiplied"), 1)

            act.wait_ge(ev("x_in"), 16)
            for t in range(NT):
                link(nc.scalar.activation(at(H1, D), xtok[:, t, :], ACT.Square, accum_out=ss[:, t:t + 1]))
            act.wait_ge(ev("eps_ready"), 1)
            nc.scalar.activation(rs, ss, ACT.Sqrt, scale=1.0 / D, bias=eps).then_inc(ev("rms1"), 1)
            multiply_cols(0)
            act.dma_start(wdt, w_in[0, :, C_DT:C_DT + 8].rearrange("(k p) n -> p k n", p=P)).then_inc(ev("small_in"), 16)
            act.dma_start(rw, router_w.rearrange("(k p) n -> p k n", p=P)).then_inc(ev("small_in"), 16)
            act.dma_start(dtb, dt_bias[0].partition_broadcast(P)).then_inc(ev("small_in"), 16)
            act.dma_start(alog, a_log[0].partition_broadcast(P)).then_inc(ev("small_in"), 16)
            act.dma_start(sink, attn_sinks[0].partition_broadcast(P)).then_inc(ev("small_in"), 16)
            act.dma_start(rbias, router_bias.partition_broadcast(P)).then_inc(ev("small_in"), 16)
            act.dma_start(dsk8, d_skip[0].partition_broadcast(P)).then_inc(ev("small_in"), 16)
            act.wait_ge(ev("acc_zeroed1"), 1)
            act.dma_start(acc[1][0:1, :], b_mod[:, 4096:8192]).then_inc(ev("bias_in1"), 16)
            act.wait_ge(ev("acc_zeroed2"), 1)
            act.dma_start(acc[2][0:1, :], b_mod[:, 8192:12288]).then_inc(ev("bias_in2"), 16)
            for b in range(4):
                act.wait_ge(ev("xT"), b + 1)
                nc.scalar.activation(h1T[:, 4 * b:4 * b + 4, :], bank(2 * (b % 3), 2).rearrange("p (k n) -> p k n", n=SEQ),
                                     ACT.Copy).then_inc(ev("h1_raw"), 1)
            dest = {G_DQ: (dq, 0.125), G_DK: (dk, 1.0), G_DV: (dv, 1.0), G_XS: (xraw[:, 0:4, 3:], 1.0),
                    G_BC: (xraw[:, 4:8, 3:], 1.0), G_BQ: (bq, 0.125), G_Z: (zg, 1.0), G_AB: (ab, 1.0),
                    G_AC: (ac, 1.0)}
            for k in range(1, KT):
                multiply_cols(k)
            act.wait_ge(proj_used, KT // 2)
            for n in (G_DK, G_DQ, G_DV):
                d, sc = dest[n]
                src = bank(2 * n, 2).rearrange("p (a n) -> p a n", n=d.shape[2])
                nc.scalar.activation(d, src, ACT.Copy, scale=sc).then_inc(ev("group_out"), 1)
            for kv in range(2):
                for a in range(2):
                    nc.scalar.activation(kdup[64 * a:64 * a + 64, kv, :], bank(7)[64 * kv:64 * kv + 64, 0:SEQ], ACT.Copy)
            nc.scalar.activation(vB, bank(7)[:, SEQ:].rearrange("p (t n) -> p t n", n=P), ACT.Copy)\
              .then_inc(ev("group_out"), 1)

            for s in STEPS:
                k, n = s[0], s[1]
                if k == "g" and s[2] == 1:
                    two = bank(pair(n), 2)
                    if n == G_AX:
                        continue
                    act.wait_ge(proj_used, pe_no[s] + 1)
                    if n in (G_AB, G_AC):
                        act.wait_ge(ev("D_out"), 2)
                    if n == G_Z:
                        act.wait_ge(ev("conv_done"), 1)
                    d, sc = dest[n]
                    f = ACT.Silu if n == G_Z else ACT.Copy
                    nc.scalar.activation(d, two.rearrange("p (k n) -> p k n", n=SEQ), f, scale=sc)\
                      .then_inc(ev("group_out"), 1)
                elif k == "D1":
                    act.wait_ge(ev("D_scores"), n + 1)
                    if n == 1:
                        act.wait_ge(ev("D_out"), 1)
                    nc.scalar.activation(s_a, bank(4, 2).rearrange("p (h n) -> p h n", n=SEQ), ACT.Copy)
                    nc.scalar.activation(s_b.rearrange("p (a h) n -> p a h n", a=2),
                                         bank(6, 2).rearrange("p (a h n) -> p a h n", a=2, n=P)[:, :, 0:2, :],
                                         ACT.Copy).then_inc(ev("D_scores_out"), 1)
                    act.wait_ge(ev("D_scores_out"), n + 1)
                    link(nc.scalar.activation(t_all, s_all, ACT.Abs))
                    link(nc.scalar.activation(t_all, t_all, ACT.Exp, scale=-1.0))
                    nc.scalar.activation(t_all, t_all, ACT.Ln, bias=1.0).then_inc(ev("D_ln"), 1)
                elif k == "D2":
                    act.wait_ge(ev("D_logw"), n + 1)
                    nc.scalar.activation(s_all, s_all, ACT.Exp).then_inc(ev("D_exp"), 1)
                elif k in ("D3", "B3"):
                    act.wait_ge(ev(k[0] + "_mixed"), n + 1)
                    t0 = (12 if k == "D3" else 4) + 2 * n
                    nc.scalar.activation(yT[:, t0:t0 + 2, :], bank(7).rearrange("p (j n) -> p j n", n=SEQ),
                                         ACT.Copy).then_inc(ev(k[0] + "_out"), 1)
                elif k == "N":
                    act.wait_ge(ev(f"N_summed{n}"), 1)
                    nc.scalar.activation(rstd_b, bank(4)[:, 0:SEQ], ACT.Sqrt, scale=1.0 / GW, bias=eps)\
                      .then_inc(ev(f"N_root{n}"), 1)
                elif k == "DT":
                    act.wait_ge(ev("dtT_done"), 1)
                    nc.scalar.activation(dtT[0:8, :], bank(7)[0:8, 0:SEQ], ACT.Copy).then_inc(ev("dtT_out"), 1)
                    act.wait_ge(ev("dt_raw"), 1)
                    act.wait_ge(ev("small_in"), 112)
                    link(nc.scalar.activation(dtw, dtv, ACT.Abs))
                    nc.scalar.activation(ea, alog, ACT.Exp)
                    link(nc.scalar.activation(dtw, dtw, ACT.Exp, scale=-1.0))
                    nc.scalar.activation(dtw, dtw, ACT.Ln, bias=1.0).then_inc(ev("dt_ln"), 1)
                    act.wait_ge(ev("conv_done"), 1)
                    nc.scalar.activation(xc, xc, ACT.Silu).then_inc(ev("xc_ready"), 1)
                elif k == "C1":
                    act.wait_ge(ev("C_seg"), n + 1)
                    nc.scalar.activation(seg, seg, ACT.Exp).then_inc(ev("C_exp"), 1)
                    if n == 0:
                        nc.scalar.activation(d2e, d2e, ACT.Exp).then_inc(ev("C_exp2"), 1)
                    else:
                        nc.scalar.activation(cum_e, cum_e, ACT.Exp).then_inc(ev("C_exp2"), 1)
                elif k == "C2" and n == 0:
                    act.wait_ge(ev("C_state"), 1)
                    nc.scalar.activation(state, bank(6).rearrange("p (h n) -> p h n", n=64), ACT.Copy)\
                      .then_inc(ev("C_state_out"), 1)
                elif k == "B1":
                    act.wait_ge(ev("B_shifted"), n + 1)
                    nc.scalar.activation(s_all, s_all, ACT.Exp)
                    nc.scalar.activation(es, es, ACT.Exp).then_inc(ev("B_exp"), 1)
                elif k == "B2":
                    act.wait_ge(ev("B_probsT"), n + 1)
                    nc.scalar.activation(t_a, bank(4, 2).rearrange("p (h n) -> p h n", n=SEQ), ACT.Copy)
                    nc.scalar.activation(t_b, bank(6).rearrange("p (h n) -> p h n", n=P), ACT.Copy)\
                      .then_inc(ev("B_probsT_out"), 1)
                elif k == "M" and n == 0:
                    act.wait_ge(ev("M_summed0"), 1)
                    nc.scalar.activation(gate1_b, bank(4, 4), ACT.Copy).then_inc(ev("M_out0"), 1)
                elif k == "R":
                    act.wait_ge(ev("x1_ready"), n + 1)
                    for t in range(NT):
                        link(nc.scalar.activation(junk, x1[:, t, n * 512:(n + 1) * 512], ACT.Square,
                                                  accum_out=ss8[:, t, n:n + 1]))
                    act.wait_ge(ev("R_transposed"), n + 1)
                    act.wait_ge(ev("a2_ready"), 1)
                    for kk in range(4):
                        ins = nc.scalar.activation(xaT[:, 4 * n + kk, :], bank(4, 2)[:, kk * SEQ:(kk + 1) * SEQ],
                                                   ACT.Copy, scale=a2[:, 4 * n + kk:4 * n + kk + 1])
                    ins.then_inc(ev("xaT_ready"), 1)
                    if n == 3:
                        act.wait_ge(ev("ss_summed"), 1)
                        nc.scalar.activation(rs2, ss, ACT.Sqrt, scale=1.0 / D, bias=eps).then_inc(ev("rms2"), 1)
                if s == ("N", 0):
                    act.wait_ge(ev("N_scaled0"), 1)
                    act.wait_ge(ev("B_scores"), 2)
                    act.wait_ge(ev("D_mixed"), 2)
                    act.dma_start(xtok, x[0].rearrange("(t p) d -> p t d", p=P)).then_inc(ev("x_in"), 16)

            act.wait_ge(ev("r_shifted"), 1)
            nc.scalar.activation(probs, probs, ACT.Exp).then_inc(ev("r_exp"), 1)
            act.wait_ge(ev("M_summed3"), 1)
            nc.scalar.activation(gate2_b, bank(4, 4), ACT.Copy).then_inc(ev("M_out3"), 1)
            act.wait_ge(ev("M_summed2"), 1)
            act.dma_start(fin_b, final_g.partition_broadcast(P)).then_inc(ev("fin_in"), 16)

            def take_gathered(L, u, count):
                act.wait_ge(L["gathered"], count)
                for kt in range(KT):
                    ins = nc.scalar.activation(xg[u][:, kt, 0:P], bank(4, 4)[:, kt * P:(kt + 1) * P], ACT.Identity,
                                               scale=a2[:, kt:kt + 1], bias=sh2[:, kt:kt + 1])
                ins.then_inc(L["xg_scaled"], 1)
                act.wait_ge(L["xg_scaled"], count)
                nc.scalar.activation(xg[u][:, :, P:192], xg[u][:, :, 0:XH], ACT.Copy).then_inc(L["xg_ready"], 1)

            def final_squares(L, n):
                for q in range(4):
                    if q < 2:
                        act.wait_ge(L["added_lo"], 2 * n + q)
                    else:
                        act.wait_ge(L["added_hi"], 2 * n + q - 1)
                    for t in range(NT):
                        nc.scalar.activation(junk_f, xacc[:, t, q * 512:(q + 1) * 512], ACT.Square,
                                             accum_out=ss8[:, t, q:q + 1]).then_inc(L["squared"], 1)
                        act.wait_ge(L["squared"], NT * q + t + 1)

            def expert(L, i, u):
                take_gathered(L, 1 - u, i * 2 + (u + 2))
                act.wait_ge(L["slot_used"], i * 24 + (12 * u + 8))
                nc.scalar.activation(hid, bank(0, 2), ACT.Silu).then_inc(L["silu_done"], 1)
                act.wait_ge(L["hid_transposed"], i * 2 + (u + 1))
                src = bank(4).rearrange("p (f n) -> p f n", n=P)
                nc.scalar.activation(hidT[:, 0:4, 0:P], src, ACT.Copy)
                nc.scalar.activation(hidT[:, 0:4, P:192], src[:, :, 0:XH], ACT.Copy).then_inc(L["hidT_act"], 1)

            take_gathered(main, 0, 1)
            act.wait_ge(ev("over_tables_ready"), 1)
            n_over = act.value_load(itab[0:1, 0:1], min_val=0, max_val=NOVER)
            with act.Fori(0, NE // 2) as i:
                for u in range(2):
                    expert(main, i, u)
            final_squares(main, NE)
            with act.If(n_over > 0):
                take_gathered(over, 0, 1)
                with act.Fori(0, NOVER // 2) as i:
                    for u in range(2):
                        expert(over, i, u)
                final_squares(over, NOVER)
            nc.scalar.activation(ssf, ss8, ACT.Copy).then_inc(ev("final_squared"), 1)
            act.wait_ge(ev("final_summed"), 1)
            nc.scalar.activation(rs3, ss, ACT.Sqrt, scale=1.0 / D, bias=eps).then_inc(ev("rms3"), 1)

        @block.tensor
        def _(pe):
            mm, tr = nc.tensor.matmul, nc.tensor.transpose
            pe.wait_ge(ev("params_in"), 176)
            pe.wait_ge(ev("ident_ready"), 1)
            tr(bank(6)[:, 0:NPAR], params[0:NPAR, :], ident[0:NPAR, 0:NPAR])
            tr(bank(6)[:, P:P + 32], params_b[0:32, :], ident[0:32, 0:32]).then_inc(ev("params_T"), 1)

            def sum_cols(k):
                pe.wait_ge(ev("red_ready"), k + 1)
                if k > 0:
                    pe.wait_ge(ev("h1_ready"), k)
                for m in range(2):
                    ins = mm(bank(6)[:, m:m + 1], red[:, k % 2, m * P:(m + 1) * P], ones[:, 0:1],
                             start=True, stop=True)
                ins.then_inc(ev("cols_summed"), 1)

            def first_groups(k):
                pe.wait_ge(ev("h1_ready"), k + 1)
                w = arrived(pe, ("first", k // 2))[:, 0:2 * FIRSTW].rearrange("p (k n) -> p k n", k=2)[:, k % 2, :]
                for m in range(8):
                    mm(ps[:, m * SEQ:(m + 1) * SEQ], w[:, m * P:(m + 1) * P], h1T[:, k, :],
                       start=(k == 0 and m % 2 == 0), stop=(k == KT - 1 and m % 2 == 1), skip_group_check=True)
                for t in range(NT):
                    ins = mm(bank(4 + t), h1T[:, k, t * P:(t + 1) * P], w[:, 2 * GW:3 * GW],
                             start=(k == 0), stop=(k == KT - 1))
                mm(bank(7)[:, 0:SEQ], w[:, 3 * GW:3 * GW + P], h1T[:, k, :], start=(k == 0), stop=False,
                   skip_group_check=True)
                for t in range(NT):
                    ins = mm(bank(7)[:, SEQ + t * P:SEQ + (t + 1) * P], h1T[:, k, t * P:(t + 1) * P],
                             w[:, 3 * GW + P:], start=False, stop=(k == KT - 1), skip_group_check=True)
                if k % 2 == 1:
                    ins.then_inc(proj_used, 1)

            pe.wait_ge(ev("diag_ready"), 2)
            for b in range(4):
                if b == 3:
                    pe.wait_ge(ev("h1_raw"), 1)
                for kk in range(4):
                    for t in range(NT):
                        k = 4 * b + kk
                        ins = mm(bank(2 * (b % 3), 2)[:, kk * SEQ + t * P:kk * SEQ + (t + 1) * P],
                                 xtok[:, t, k * P:(k + 1) * P], diag[:, t, :], start=True, stop=True)
                ins.then_inc(ev("xT"), 1)
            pe.wait_ge(ev("cond_ready"), 1)
            sum_cols(0)
            pe.wait_ge(ev("h1_raw"), 4)
            for k in range(1, KT):
                sum_cols(k)
                first_groups(k - 1)
            first_groups(KT - 1)

            def group(g, half):
                if half == 0:
                    pe.wait_ge(ev("group_out"), {G_XS: 1, G_BC: 2, G_BQ: 5, G_Z: 6, G_AB: 7, G_AC: 8, G_AX: 9}[g])
                w = arrived(pe, ("g", g, half))
                two = bank(pair(g), 2)
                w = w.rearrange("p (k n) -> p k n", n=512)
                for kk in range(8):
                    for m in range(4):
                        k = 8 * half + kk
                        ins = mm(two[:, m * SEQ:(m + 1) * SEQ], w[:, kk, m * P:(m + 1) * P], h1T[:, k, :],
                                 start=(k == 0 and m % 2 == 0), stop=(k == KT - 1 and m % 2 == 1),
                                 skip_group_check=True)
                ins.then_inc(proj_used, 1)

            def both(n):
                return bank(n).rearrange("p (j n) -> p j n", n=P)

            def values(w_a, w_b, v, head, done):
                for j in range(2):
                    for a in range(2):
                        o = bank(7)[64 * a:64 * a + 64, j * SEQ:(j + 1) * SEQ]
                        h = head(j, a)
                        mm(o, v[:, 0, h * 64:h * 64 + 64], w_a[:, 2 * a + j, :], start=True, stop=False)
                        ins = mm(o[:, P:SEQ], v[:, 1, h * 64:h * 64 + 64], w_b[:, 2 * a + j, :],
                                 start=False, stop=True)
                ins.then_inc(ev(done), 1)

            def router(n):
                for kt in range(4 * n, 4 * n + 4):
                    for t in range(NT):
                        ins = mm(bank(6)[:, t * NE:(t + 1) * NE], xaT[:, kt, t * P:(t + 1) * P], rw[:, kt, :],
                                 start=(kt == 0 and t == 0), stop=(kt == KT - 1 and t == 1), skip_group_check=True)
                return ins

            for s in STEPS:
                k, n = s[0], s[1]
                if k == "g":
                    group(n, s[2])
                elif k == "D1":
                    pe.wait_ge(ev("group_out"), 4)
                    if n == 1:
                        pe.wait_ge(ev("D_logw"), 1)
                        pe.wait_ge(ev("D_out"), 1)
                    for j in range(2):
                        for a in range(2):
                            kT, qT = dk[64 * a:64 * a + 64, 2 * n + j, :], dq[64 * a:64 * a + 64, 2 * n + j, :]
                            mm(bank(4 + a)[:, j * SEQ:(j + 1) * SEQ], kT[:, 0:P], qT, start=True, stop=True)
                    for j in range(2):
                        for a in range(2):
                            kT, qT = dk[64 * a:64 * a + 64, 2 * n + j, :], dq[64 * a:64 * a + 64, 2 * n + j, :]
                            ins = mm(bank(6 + a)[:, j * P:(j + 1) * P], kT[:, P:SEQ], qT[:, P:SEQ],
                                     start=True, stop=True)
                    ins.then_inc(ev("D_scores"), 1)
                elif k == "D2":
                    pe.wait_ge(ev("D_softp"), n + 1)
                    for a in range(2):
                        mm(bank(4 + a), lower, t_a[:, 2 * a:2 * a + 2, :], start=True, stop=False)
                        mm(bank(4 + a).rearrange("p (j n) -> p j n", n=SEQ)[:, :, P:SEQ], ones,
                           t_b[:, 2 * a:2 * a + 2, :], start=False, stop=True)
                    mm(bank(6), lower, t_b, start=True, stop=True).then_inc(ev("D_sums"), 1)
                elif k == "D3":
                    pe.wait_ge(ev("group_out"), G_DV + 1)
                    pe.wait_ge(ev("D_weights"), n + 1)
                    values(s_a, s_b, dv, lambda j, a: 2 * (2 * n + j) + a, "D_mixed")
                elif k == "N":
                    pe.wait_ge(ev(f"N_squares{n}"), 1)
                    if n == 1:
                        pe.wait_ge(ev("N_root0"), 1)
                    for j in range(4):
                        ins = mm(bank(4)[:, 0:SEQ], ones, squares[n][:, j, :], start=(j == 0), stop=(j == 3))
                    ins.then_inc(ev(f"N_summed{n}"), 1)
                elif k == "DT":
                    pe.wait_ge(ev("small_in"), 112)
                    pe.wait_ge(ev("D_out"), 2)
                    for kk in range(KT):
                        ins = mm(bank(7)[0:8, 0:SEQ], wdt[:, kk, :], h1T[:, kk, :], start=(kk == 0), stop=(kk == KT - 1))
                    ins.then_inc(ev("dtT_done"), 1)
                    pe.wait_ge(ev("dtT_out"), 1)
                    for t in range(NT):
                        ins = tr(bank(7)[:, t * 8:(t + 1) * 8], dtT[0:8, t * P:(t + 1) * P], ident[0:8, 0:8])
                    ins.then_inc(ev("dt_done"), 1)
                elif k == "C0":
                    pe.wait_ge(ev("da_ready"), 1)
                    for ch in range(NT):
                        ins = mm(bank(7)[:, ch * 8:(ch + 1) * 8], upper, da[:, ch * 8:(ch + 1) * 8],
                                 start=True, stop=True)
                    ins.then_inc(ev("cum_done"), 1)
                elif k == "C1":
                    pe.wait_ge(ev("C_dau"), n + 1)
                    pe.wait_ge(ev("xc_ready"), 1)
                    if n == 1:
                        pe.wait_ge(ev("C_state_out"), 1)
                        pe.wait_ge(ev("C_y"), 1)
                    tok = slice(n * P, (n + 1) * P)
                    for q in range(2):
                        mm(bank(4 + q), ones, da_u[:, 4 * q:4 * q + 4, :], start=True, stop=True)
                    for g in range(2):
                        mm(bank(6)[:, g * P:(g + 1) * P], xc[:, 4 + g, tok], xc[:, 6 + g, tok], start=True, stop=True)
                    if n == 0:
                        for g in range(2):
                            tr(bank(6)[:, 256 + g * P:256 + (g + 1) * P], xc[:, 4 + g, tok], ident)
                    for j in range(4):
                        ins = tr(bank(7)[:, j * P:(j + 1) * P], xc[:, j, tok], ident)
                    ins.then_inc(ev("C_parts"), 1)
                elif k == "C2":
                    pe.wait_ge(ev("C_mix"), n + 1)
                    if n == 0:
                        for g in range(2):
                            ins = mm(bank(6)[:, g * 256:(g + 1) * 256], bm_tok[:, g * P:(g + 1) * P],
                                     xw[:, 4 * g:4 * g + 4, :], start=True, stop=True)
                        ins.then_inc(ev("C_state"), 1)
                    for h in range(8):
                        o = bank(7)[64 * (h % 2):64 * (h % 2) + 64, (h // 2) * P:(h // 2 + 1) * P]
                        ins = mm(o, xdt[:, h, :], seg[:, h, :], start=True, stop=(n == 0))
                        if n == 1:
                            ins = mm(o, state[:, h, :], cum_e[:, h, :], start=False, stop=True)
                    ins.then_inc(ev("C_mixed"), 1)
                elif k == "B1":
                    pe.wait_ge(ev("group_out"), G_BKV + 1)
                    if n == 0:
                        pe.wait_ge(ev("N_root2"), 1)
                    else:
                        pe.wait_ge(ev("B_out"), 1)
                    for t, b0, width in ((1, 4, SEQ), (0, 6, P)):
                        for j in range(2):
                            for a in range(2):
                                rows = slice(64 * a, 64 * a + 64)
                                ins = mm(bank(b0 + a)[:, j * width:(j + 1) * width],
                                         bq[rows, 2 * n + j, t * P:(t + 1) * P], kdup[rows, n, 0:width],
                                         start=True, stop=True)
                    ins.then_inc(ev("B_scores"), 1)
                elif k == "B2":
                    pe.wait_ge(ev("B_probs"), n + 1)
                    for a in range(2):
                        for j in range(2):
                            h = 2 * a + j
                            tr(bank(4 + a)[:, j * SEQ:j * SEQ + P], s_b[:, h, :], ident)
                            tr(bank(4 + a)[:, j * SEQ + P:(j + 1) * SEQ], s_a[:, h, 0:P], ident)
                            ins = tr(bank(6)[:, h * P:(h + 1) * P], s_a[:, h, P:SEQ], ident)
                    ins.then_inc(ev("B_probsT"), 1)
                elif k == "B3":
                    pe.wait_ge(ev("B_probsT_out"), n + 1)
                    values(t_a, t_b, vB, lambda j, a: n, "B_mixed")
                elif k == "M" and n in (0, 3):
                    a = acc[2][:, D:] if n else acc[1][:, 0:D]
                    pe.wait_ge(mod_used, 32 if n else 16)
                    if n == 0:
                        pe.wait_ge(ev("N_root1"), 1)
                        pe.wait_ge(ev("B_out"), 2)
                    else:
                        pe.wait_ge(ev("logits_read"), 1)
                    for q in range(4):
                        ins = mm(bank(4 + q), ones, a[:, q * 512:(q + 1) * 512], start=True, stop=True)
                    ins.then_inc(ev(f"M_summed{n}"), 1)
                elif k == "M":
                    a = acc[1][:, D:] if n == 1 else acc[2][:, 0:D]
                    pe.wait_ge(mod_used, 16 if n == 1 else 32)
                    pe.wait_ge(ev("M_out0"), 1)
                    if n == 2:
                        pe.wait_ge(ev("rw_sh_ready"), 1)
                    for j in range(KT):
                        ins = mm(bank(7)[:, 16 * (n - 1) + j:16 * (n - 1) + j + 1], a[:, j * P:(j + 1) * P],
                                 ones[:, 0:1], start=True, stop=True)
                    ins.then_inc(ev(f"M_summed{n}"), 1)
                elif k == "R":
                    pe.wait_ge(ev("x1_ready"), n + 1)
                    if n > 0:
                        pe.wait_ge(ev("xaT_ready"), n)
                    else:
                        pe.wait_ge(ev("M_out0"), 1)
                    for kk in range(4):
                        for t in range(NT):
                            kt = 4 * n + kk
                            ins = tr(bank(4, 2)[:, kk * SEQ + t * P:kk * SEQ + (t + 1) * P],
                                     x1[:, t, kt * P:(kt + 1) * P], ident)
                    ins.then_inc(ev("R_transposed"), 1)
                    if n == 1:
                        pe.wait_ge(ev("rw_sh_ready"), 1)
                        mm(bank(7)[:, 64:320], ones, rw_sh, start=True, stop=True)
                    if n > 0:
                        router(n - 1)
                    if n == 3:
                        pe.wait_ge(ev("xaT_ready"), 4)
                        router(3).then_inc(ev("r_logits"), 1)
                elif k == "wo":
                    half = s[2]
                    if half == 0:
                        pe.wait_ge(ev("N_scaled3"), 1)
                        pe.wait_ge(ev("N_scaled2"), 1)
                        if n == 1:
                            pe.wait_ge(ev("A_gated"), 1)
                        elif n == 0:
                            pe.wait_ge(ev("group_out"), 10)
                        else:
                            pe.wait_ge(ev("x1_ready"), n - 1)
                    else:
                        pe.wait_ge(ev("N_scaled1"), 1)
                        pe.wait_ge(ev("N_scaled0"), 1)
                    w = arrived(pe, s).rearrange("p (k n) -> p k n", n=512)
                    for t in range(NT):
                        for kk in range(8):
                            kt = 8 * (1 - half) + kk
                            ins = mm(bank(2 * (n % 2) + t), yT[:, kt, t * P:(t + 1) * P], w[:, kk, :],
                                     start=(half == 0 and kk == 0), stop=(half == 1 and kk == 7))
                        if t == 0 and half == 1:
                            ins.then_inc(ev("wo_tile0"), 1)
                    ins.then_inc(proj_used, 1)

            pe.wait_ge(ev("r_sel"), 1)
            mm(bank(1)[:, 0:16], strict, chosen[:, 0, :], start=True, stop=True)
            mm(bank(1)[:, 16:32], strict, chosen[:, 1, :], start=True, stop=False)
            mm(bank(1)[:, 16:32], ones, chosen[:, 0, :], start=False, stop=True)
            mm(bank(1)[:, 32:48], ones, chosen[:, 0, :], start=True, stop=False)
            mm(bank(1)[:, 32:48], ones, chosen[:, 1, :], start=False, stop=True).then_inc(ev("r_pos"), 1)

            for _ in range(8):
                mm(bank(2), ones, x1[:, 0, 0:512], start=True, stop=True)

            def many(at_v):
                return pe.value_load(itab[0:1, bass.ds(at_v, 1)], min_val=0, max_val=1)

            def gather(L, count, flag):
                pe.wait_ge(L["onehot_ready"], count)

                def columns(w):
                    for kt in range(KT):
                        for t in range(NT):
                            ins = mm(bank(4, 4)[:, kt * P:kt * P + w], x1[:, t, kt * P:(kt + 1) * P],
                                     pos1h[:, t, 0:w], start=(t == 0), stop=(t == NT - 1))
                    ins.then_inc(L["gathered"], 1)

                with pe.If(flag > 0):
                    columns(P)
                with pe.Else():
                    columns(XH)

            def transpose_gates(L, count):
                pe.wait_ge(L["xg_ready"], count)
                for r in range(2):
                    for t in range(NT):
                        ins = tr(bank(4)[:, (2 * r + t) * P:(2 * r + t + 1) * P],
                                 gate1h[:, t, XH * r:XH * r + P], ident)
                ins.then_inc(L["pg_transposed"], 1)

            def combine(L, u, q, b):
                for h in range(2):
                    c0 = q * 512 + 256 * h
                    for t in range(NT):
                        ins = mm(bank(b + t)[:, 256 * h:256 * h + 256], pgT[u][:, 2 * h + t, :],
                                 y_sb[:, c0:c0 + 256], start=True, stop=True)
                ins.then_inc(L["combined"], 1)

            def expert(L, i, u, base, fills):
                few0 = many(i * 2 + (base + 8 + u))
                few1 = many(i * 2 + (base + 9 + u))

                def chunk(j):
                    pe.wait_ge(slot_full[j % NSLOT], i * 64 + 16 * (fills[j % NSLOT] + 2 * u + j // NSLOT + 1))
                    return at((j % NSLOT) * SLOT, SLOT)

                def gate_up(q):
                    ws = [chunk(2 * q + m).rearrange("p (k n) -> p k n", n=FF) for m in range(2)]

                    def products(full):
                        for m in range(2):
                            for kk in range(4):
                                kt = 4 * q + kk
                                for hf in range(2):
                                    if full:
                                        o, x0 = bank(2 * m + hf), xg[u][:, kt, XH * hf:XH * hf + P]
                                    else:
                                        o = bank(2 * m + hf)[XH * hf:XH * hf + XH, :]
                                        x0 = xg[u][:, kt, 0:XH]
                                    ins = mm(o, x0, ws[m][:, kk, hf * 512:(hf + 1) * 512],
                                             start=(kt == 0), stop=(kt == KT - 1))
                            ins.then_inc(L["slot_used"], 1)

                    with pe.If(few0 > 0):
                        products(True)
                    with pe.Else():
                        products(False)

                def down(q):
                    w = chunk(8 + q).rearrange("p (k n) -> p k n", n=512)

                    def products(full):
                        for f in range(8):
                            for h in range(2):
                                cs = slice(256 * h, 256 * h + 256)
                                if full:
                                    ins = mm(bank(4 + q)[:, cs], hidT[:, f, XH * h:XH * h + P], w[:, f, cs],
                                             start=(f == 0 and h == 0), stop=(f == 7 and h == 1),
                                             skip_group_check=True)
                                else:
                                    ins = mm(bank(4 + q)[XH * h:XH * h + XH, cs], hidT[:, f, 0:XH], w[:, f, cs],
                                             start=(f == 0), stop=(f == 7))
                        ins.then_inc(L["slot_used"], 1)

                    with pe.If(few0 > 0):
                        products(True)
                    with pe.Else():
                        products(False)

                pe.wait_ge(L["xg_ready"], i * 2 + (u + 1))
                pe.wait_ge(L["hid_ready"], i * 2 + (u + 1))
                pe.wait_ge(L["added_lo"], i * 4 + (2 * u + 1))
                gate_up(0)
                pe.wait_ge(L["y_ready"], i * 8 + (4 * u + 1))
                pe.wait_ge(L["added_hi"], i * 4 + (2 * u + 1))
                combine(L, 1 - u, 3, 4)
                gate_up(1)
                pe.wait_ge(L["added_hi"], i * 4 + (2 * u + 2))
                gather(L, i * 2 + (u + 2), few1)
                gate_up(2)
                gate_up(3)
                transpose_gates(L, i * 2 + (u + 2))
                pe.wait_ge(L["pg_ready"], i * 2 + (u + 2))
                pe.wait_ge(L["hid_ready"], i * 2 + (u + 2))
                for f in range(8):
                    ins = tr(bank(4, 2)[:, f * P:(f + 1) * P], hid[:, f * P:(f + 1) * P], ident)
                ins.then_inc(L["hid_transposed"], 1)
                pe.wait_ge(L["hidT_act"], i * 2 + (u + 1))
                pe.wait_ge(L["hidT_dve"], i * 2 + (u + 1))
                down(0)
                down(1)
                pe.wait_ge(L["y_ready"], i * 8 + (4 * u + 2))
                combine(L, u, 0, 0)
                down(2)
                pe.wait_ge(L["y_ready"], i * 8 + (4 * u + 3))
                combine(L, u, 1, 2)
                down(3)
                pe.wait_ge(L["y_ready"], i * 8 + (4 * u + 4))
                combine(L, u, 2, 4)

            def last_combine(L, n):
                pe.wait_ge(L["y_ready"], 4 * n + 1)
                pe.wait_ge(L["added_hi"], 2 * n + 1)
                combine(L, 1, 3, 4)

            pe.wait_ge(ev("tables_ready"), 1)
            pe.wait_ge(ev("M_out3"), 1)
            gather(main, 1, many(8))
            transpose_gates(main, 1)
            pe.wait_ge(main["pg_ready"], 1)
            pe.wait_ge(ev("over_tables_ready"), 1)
            with pe.Fori(0, NE // 2) as i:
                for u in range(2):
                    expert(main, i, u, 0, FILLS)
            last_combine(main, NE)
            pe.wait_ge(ev("main_done"), 1)
            n_over = pe.value_load(itab[0:1, 0:1], min_val=0, max_val=NOVER)
            with pe.If(n_over > 0):
                gather(over, 1, many(8 + NE))
                transpose_gates(over, 1)
                pe.wait_ge(over["pg_ready"], 1)
                with pe.Fori(0, NOVER // 2) as i:
                    for u in range(2):
                        expert(over, i, u, NE, [f + 2 * NE for f in FILLS])
                last_combine(over, NOVER)

        @block.vector
        def _(dve):
            V = nc.vector
            links = [0]

            def link(ins):
                links[0] += 1
                ins.then_inc(ev("dve_link"), 1)
                dve.wait_ge(ev("dve_link"), links[0])

            def tt(o, a, b, op):
                return V.tensor_tensor(o, a, b, op)

            def over_heads(a, n, w):
                return a.unsqueeze(1).broadcast_to([P, n, w])

            def over_cols(a, n, w):
                return a.unsqueeze(2).broadcast_to([P, n, w])

            def modulate(it):
                _, r, k = it
                w = arrived(dve, it)
                if k == 0:
                    dve.wait_ge(ev(f"bias_in{r}"), 16)
                else:
                    dve.wait_ge(mod_used, mod_no[it])
                V.scalar_tensor_tensor(acc[r], w, cond[:, k:k + 1], acc[r], ALU.mult, ALU.add).then_inc(mod_used, 1)

            V.memset(eps, EPS).then_inc(ev("eps_ready"), 1)
            dve.wait_ge(ev("cond_ready"), 1)
            V.memset(xraw[:, :, 0:3], 0.0)
            dve.wait_ge(ev("rms1"), 1)
            dve.wait_ge(ev("ident_ready"), 1)
            link(V.reciprocal(rs, rs))
            for t in range(NT):
                V.tensor_scalar(diag[:, t, :], ident, rs[:, t:t + 1], None, ALU.mult).then_inc(ev("diag_ready"), 1)

            def finish_h1(k):
                dve.wait_ge(ev("cols_summed"), k + 1)
                link(tt(mod1[:, 2 * k:2 * k + 2], bank(6)[:, 0:2], b1.rearrange("p (m k) -> p k m", m=2)[:, k, :],
                        ALU.add))
                link(V.scalar_tensor_tensor(a1[:, k:k + 1], mod1[:, 2 * k + 1:2 * k + 2], 1.0,
                                            cols[:, c_n1 + k:c_n1 + k + 1], ALU.add, ALU.mult))
                if k % 4 == 0:
                    dve.wait_ge(ev("h1_raw"), k // 4 + 1)
                V.tensor_scalar(h1T[:, k, :], h1T[:, k, :], a1[:, k:k + 1], mod1[:, 2 * k:2 * k + 1], ALU.mult, ALU.add)\
                 .then_inc(ev("h1_ready"), 1)

            for k in range(KT):
                w = arrived(dve, ("cols", k)).rearrange("p (r n) -> p r n", n=2 * P)
                if k > 0:
                    dve.wait_ge(ev("red_ready"), k)
                link(tt(prod[:, ACT_TILES:, :], w[:, ACT_TILES:, :],
                        over_cols(cond[:, ACT_TILES:], KT - ACT_TILES, 2 * P), ALU.mult))
                dve.wait_ge(ev("cols_multiplied"), k + 1)
                if k > 1:
                    dve.wait_ge(ev("cols_summed"), k - 1)
                V.reduce_sum(red[:, k % 2, :], prod.rearrange("p r n -> p n r"), AX).then_inc(ev("red_ready"), 1)
                if k > 0:
                    finish_h1(k - 1)
            finish_h1(KT - 1)

            strict4 = over_heads(strict, 4, P)
            for n_step, s in enumerate(STEPS):
                k, n = s[0], s[1]
                if s == ("wo", 1, 0):
                    dve.wait_ge(ev("B_out"), 2)
                    tt(squares[1], yT[:, 4:8, :], yT[:, 4:8, :], ALU.mult).then_inc(ev("N_squares1"), 1)
                if k in ("g", "wo") and s != ("g", 10, 1):
                    at_item = where[s] + 1
                    while at_item < NITEMS and ITEMS[at_item][0] == "mod":
                        modulate(ITEMS[at_item])
                        at_item += 1
                if s == ("g", 10, 1):
                    dve.wait_ge(ev("group_out"), 10)
                    dve.wait_ge(proj_used, pe_no[s] + 1)
                    link(V.memset(au[:, :, 0:2], 0.0))
                    V.tensor_tensor(au[:, :, 2:], bank(pair(G_AX), 2).rearrange("p (k n) -> p k n", n=SEQ), ac, ALU.mult)\
                     .then_inc(ev("A_gated"), 1)
                    dve.wait_ge(ev("A_gated"), 1)
                    for w in range(3):
                        for j in range(4):
                            cf = cols[:, c_ca + 4 * w + j:c_ca + 4 * w + j + 1]
                            if w == 0:
                                ins = V.tensor_scalar(ac[:, j, :], au[:, j, 0:SEQ], cf, None, ALU.mult)
                            else:
                                ins = V.scalar_tensor_tensor(ac[:, j, :], au[:, j, w:w + SEQ], cf, ac[:, j, :],
                                                             ALU.mult, ALU.add)
                        link(ins)
                    link(tt(yT[:, 0:4, :], ac, ab, ALU.mult))
                    tt(squares[0], yT[:, 0:4, :], yT[:, 0:4, :], ALU.mult).then_inc(ev("N_squares0"), 1)
                    at_item = where[s] + 1
                    while at_item < NITEMS and ITEMS[at_item][0] == "mod":
                        modulate(ITEMS[at_item])
                        at_item += 1
                elif k == "D1":
                    dve.wait_ge(ev("D_ln"), n + 1)
                    link(V.scalar_tensor_tensor(t_all, s_all, 0.0, t_all, ALU.max, ALU.add))
                    tt(t_a[:, :, 0:P], t_a[:, :, 0:P], strict4, ALU.mult)
                    tt(t_b, t_b, strict4, ALU.mult).then_inc(ev("D_softp"), 1)
                elif k == "D2":
                    dve.wait_ge(ev("D_sums"), n + 1)
                    tt(s_a, s_a, bank(4, 2).rearrange("p (h n) -> p h n", n=SEQ), ALU.subtract)
                    link(tt(s_b, s_b, bank(6).rearrange("p (h n) -> p h n", n=P), ALU.subtract))
                    V.tensor_scalar(s_a[:, :, 0:P], s_a[:, :, 0:P], 0.0, None, ALU.min)
                    V.tensor_scalar(s_b, s_b, 0.0, None, ALU.min).then_inc(ev("D_logw"), 1)
                    dve.wait_ge(ev("D_exp"), n + 1)
                    tt(s_a[:, :, 0:P], s_a[:, :, 0:P], strict4, ALU.mult)
                    tt(s_b, s_b, strict4, ALU.mult).then_inc(ev("D_weights"), 1)
                elif k == "DT":
                    dve.wait_ge(ev("dt_done"), 1)
                    dve.wait_ge(ev("small_in"), 112)
                    tt(dtv.rearrange("p (t h) -> p t h", h=8), bank(7)[:, 0:16].rearrange("p (t h) -> p t h", h=8),
                       over_heads(dtb, NT, 8), ALU.add).then_inc(ev("dt_raw"), 1)
                    dve.wait_ge(ev("dt_ln"), 1)
                    link(V.scalar_tensor_tensor(dt, dtv, 0.0, dtw, ALU.max, ALU.add))
                    V.scalar_tensor_tensor(da.rearrange("p (t h) -> p t h", h=8), dt.rearrange("p (t h) -> p t h", h=8),
                                           -1.0, over_heads(ea, NT, 8), ALU.mult, ALU.mult).then_inc(ev("da_ready"), 1)
                    for a in range(2):
                        V.tensor_copy(dsk[64 * a:64 * a + 64, :],
                                      dsk8.rearrange("p (j a) -> p a j", a=2)[64 * a:64 * a + 64, a, :])
                    dve.wait_ge(ev("group_out"), 6)
                    for w in range(4):
                        for j in range(8):
                            cf = cols[:, c_cw + 8 * w + j:c_cw + 8 * w + j + 1]
                            if w == 0:
                                ins = V.tensor_scalar(xc[:, j, :], xraw[:, j, 0:SEQ], cf,
                                                      cols[:, c_cb + j:c_cb + j + 1], ALU.mult, ALU.add)
                            else:
                                ins = V.scalar_tensor_tensor(xc[:, j, :], xraw[:, j, w:w + SEQ], cf, xc[:, j, :],
                                                             ALU.mult, ALU.add)
                        if w < 3:
                            link(ins)
                    ins.then_inc(ev("conv_done"), 1)
                elif k == "C0":
                    dve.wait_ge(ev("cum_done"), 1)
                    V.tensor_copy(cum, bank(7)[:, 0:16])
                    tt(da_u, over_heads(upper, 8, P), over_cols(da[:, 0:8], 8, P), ALU.mult).then_inc(ev("C_dau"), 1)
                    dve.wait_ge(ev("C_dau"), 1)
                elif k == "C1":
                    dve.wait_ge(ev("C_parts"), n + 1)
                    cumb = bank(4, 2).rearrange("p (h n) -> p h n", n=P)
                    cc = cum[:, 8 * n:8 * n + 8]
                    tt(seg, cumb, over_cols(cc, 8, P), ALU.subtract)
                    if n == 0:
                        link(tt(d2e, cumb[:, :, P - 1], cc, ALU.subtract))
                    else:
                        link(V.tensor_copy(cum_e, cumb))
                    V.tensor_scalar(seg, seg, 0.0, None, ALU.min).then_inc(ev("C_seg"), 1)
                    tt(cbm, bank(6)[:, 0:256].rearrange("p (g n) -> p g n", n=P), over_heads(upper, 2, P), ALU.mult)
                    if n == 0:
                        V.tensor_copy(bm_tok, bank(6)[:, 256:512])
                    link(tt(xdt, bank(7).rearrange("p (h n) -> p h n", n=64), over_cols(dt[:, 8 * n:8 * n + 8], 8, 64),
                            ALU.mult))
                    dve.wait_ge(ev("C_exp2"), n + 1)
                    if n == 0:
                        tt(xw, xdt, over_cols(d2e, 8, 64), ALU.mult)
                    else:
                        for g in range(2):
                            ce = cum_e[:, 4 * g:4 * g + 4, :]
                            tt(ce, ce, over_heads(xc[:, 6 + g, P:SEQ], 4, P), ALU.mult)
                    dve.wait_ge(ev("C_exp"), n + 1)
                    for g in range(2):
                        sg = seg[:, 4 * g:4 * g + 4, :]
                        ins = tt(sg, sg, over_heads(cbm[:, g, :], 4, P), ALU.mult)
                    ins.then_inc(ev("C_mix"), 1)
                    if n == 0:
                        tt(da_u, over_heads(upper, 8, P), over_cols(da[:, 8:16], 8, P), ALU.mult)\
                            .then_inc(ev("C_dau"), 1)
                elif k == "C2":
                    dve.wait_ge(ev("C_mixed"), n + 1)
                    tok = slice(n * P, (n + 1) * P)
                    for j in range(4):
                        ins = V.scalar_tensor_tensor(yT[:, 8 + j, tok], xc[:, j, tok], dsk[:, j:j + 1],
                                                     bank(7)[:, j * P:(j + 1) * P], ALU.mult, ALU.add)
                    ins.then_inc(ev("C_y"), 1)
                elif k == "B1":
                    dve.wait_ge(ev("B_scores"), n + 1)
                    dve.wait_ge(ev("masks_ready"), 5)
                    if n == 1:
                        dve.wait_ge(ev("B_out"), 1)
                    for a in range(2):
                        for j in range(2):
                            slope = 2.0 ** -(4 * n + 2 * j + a + 1)
                            V.scalar_tensor_tensor(s_a[:, 2 * a + j, :], dist, -slope,
                                                   bank(4 + a)[:, j * SEQ:(j + 1) * SEQ], ALU.mult, ALU.add)
                            ins = V.scalar_tensor_tensor(s_b[:, 2 * a + j, :], dist[:, P:SEQ], -slope,
                                                         bank(6 + a)[:, j * P:(j + 1) * P], ALU.mult, ALU.add)
                    link(ins)
                    V.reduce_max(mx[:, 0:4], s_b, AX)
                    link(V.reduce_max(mx[:, 4:8], s_a, AX))
                    sk = sink[:, 4 * n:4 * n + 4].rearrange("p (j a) -> p a j", a=2)
                    for q in range(2):
                        m = mx[:, 4 * q:4 * q + 4].rearrange("p (a j) -> p a j", a=2)
                        ins = tt(m, m, sk, ALU.max)
                    link(ins)
                    for q in range(2):
                        m, e = (z[:, 4 * q:4 * q + 4].rearrange("p (a j) -> p a j", a=2) for z in (mx, es))
                        tt(e, sk, m, ALU.subtract)
                    tt(s_b, s_b, over_cols(mx[:, 0:4], 4, P), ALU.subtract)
                    tt(s_a, s_a, over_cols(mx[:, 4:8], 4, SEQ), ALU.subtract).then_inc(ev("B_shifted"), 1)
                    dve.wait_ge(ev("B_exp"), n + 1)
                    V.reduce_sum(den[:, 0:4], s_b, AX)
                    link(V.reduce_sum(den[:, 4:8], s_a, AX))
                    link(tt(den, den, es, ALU.add))
                    link(V.reciprocal(den, den))
                    tt(s_b, s_b, over_cols(den[:, 0:4], 4, P), ALU.mult)
                    tt(s_a, s_a, over_cols(den[:, 4:8], 4, SEQ), ALU.mult).then_inc(ev("B_probs"), 1)
                elif k == "N":
                    yg = yT[:, 4 * n:4 * n + 4, :]
                    if n == 3:
                        dve.wait_ge(ev("D_out"), 2)
                    elif n == 2:
                        dve.wait_ge(ev("C_y"), 2)
                        dve.wait_ge(ev("group_out"), G_Z + 1)
                        link(tt(yg, yg, zg, ALU.mult))
                    if n > 1:
                        tt(squares[n], yg, yg, ALU.mult).then_inc(ev(f"N_squares{n}"), 1)
                    dve.wait_ge(ev(f"N_root{n}"), 1)
                    link(V.reciprocal(rstd_b, rstd_b))
                    for j in range(4):
                        ins = V.scalar_tensor_tensor(yg[:, j, :], yg[:, j, :], cols[:, c_gn[n] + j:c_gn[n] + j + 1],
                                                     rstd_b, ALU.mult, ALU.mult)
                    ins.then_inc(ev(f"N_scaled{n}"), 1)
                elif k == "wo" and s[2] == 1:
                    dve.wait_ge(ev("wo_tile0"), n + 1)
                    dve.wait_ge(ev("M_out0"), 1)
                    dve.wait_ge(ev("x_in"), 32)
                    if n > 0:
                        dve.wait_ge(ev("x1_ready"), n)
                    c5 = slice(n * 512, (n + 1) * 512)
                    for t in range(NT):
                        if t == 1:
                            dve.wait_ge(proj_used, pe_no[s] + 1)
                        link(tt(wo_tmp[:, t, :], bank(2 * (n % 2) + t), gate1_b[:, c5], ALU.mult))
                        ins = tt(x1[:, t, c5], x1[:, t, c5], wo_tmp[:, t, :], ALU.add)
                    ins.then_inc(ev("x1_ready"), 1)
                elif s == ("M", 1):
                    dve.wait_ge(ev("M_summed1"), 1)
                    link(V.tensor_copy(sh2, bank(7)[:, 0:16]))
                    tt(rw_sh, rw, over_cols(sh2, KT, NE), ALU.mult).then_inc(ev("rw_sh_ready"), 1)
                elif s == ("M", 2):
                    dve.wait_ge(ev("M_summed2"), 1)
                    V.scalar_tensor_tensor(a2, bank(7)[:, 16:32], 1.0, cols[:, c_n2:c_n2 + 16], ALU.add, ALU.mult)\
                     .then_inc(ev("a2_ready"), 1)

            dve.wait_ge(ev("xaT_ready"), 4)
            V.reduce_sum(ss, ss8, AX).then_inc(ev("ss_summed"), 1)
            dve.wait_ge(ev("rms2"), 1)
            link(V.reciprocal(rs2, rs2))

            def per(a):
                return over_cols(a, NT, NE)

            dve.wait_ge(ev("r_logits"), 1)
            V.reduce_sum(shift_l, bank(7)[:, 64:320].rearrange("p (k e) -> p e k", e=NE), AX)
            link(tt(probs, bank(6)[:, 0:32].rearrange("p (t e) -> p t e", e=NE), per(rs2), ALU.mult))
            tt(probs, probs, over_heads(shift_l, NT, NE), ALU.add).then_inc(ev("logits_read"), 1)
            dve.wait_ge(ev("logits_read"), 1)
            link(V.reduce_max(r1, probs, AX))
            tt(probs, probs, per(r1), ALU.subtract).then_inc(ev("r_shifted"), 1)
            V.tensor_scalar(wdesc, iota[:, 0:NE], -1.0, 16.0, ALU.mult, ALU.add)
            dve.wait_ge(ev("r_exp"), 1)
            link(V.reduce_sum(r1, probs, AX))
            link(V.reciprocal(r1, r1))
            link(tt(probs, probs, per(r1), ALU.mult))
            link(tt(sel, probs, over_heads(rbias, NT, NE), ALU.add))
            s4 = sel.rearrange("p t (g e) -> p (t g) e", e=4)
            tt(q4[:, 0, :], s4[:, :, 0], s4[:, :, 1], ALU.max)
            tt(q4[:, 1, :], s4[:, :, 0], s4[:, :, 1], ALU.min)
            tt(q4[:, 2, :], s4[:, :, 2], s4[:, :, 3], ALU.max)
            link(tt(q4[:, 3, :], s4[:, :, 2], s4[:, :, 3], ALU.min))
            tt(q4[:, 4, :], q4[:, 0, :], q4[:, 2, :], ALU.max)
            tt(q4[:, 5, :], q4[:, 0, :], q4[:, 2, :], ALU.min)
            link(tt(q4[:, 6, :], q4[:, 1, :], q4[:, 3, :], ALU.max))
            link(tt(q4[:, 6, :], q4[:, 5, :], q4[:, 6, :], ALU.max))
            link(tt(gsc, q4[:, 4, :].rearrange("p (t g) -> p t g", g=4), q4[:, 6, :].rearrange("p (t g) -> p t g", g=4),
                    ALU.add))

            def first_best(o, v, n):
                link(V.reduce_max(r1, v, AX))
                link(tt(o, v, over_cols(r1, NT, n), ALU.is_equal))
                link(tt(o, o, over_heads(wdesc[:, 0:n], NT, n), ALU.mult))
                link(V.reduce_max(r1, o, AX))
                link(tt(o, o, over_cols(r1, NT, n), ALU.is_equal))

            first_best(gmask, gsc, 4)
            g8 = gmask.rearrange("p t g -> p (t g)")
            V.tensor_scalar(g8b, g8, -1.0, BIG, ALU.add, ALU.mult)
            link(tt(s4, s4, over_cols(g8, 8, 4), ALU.mult))
            link(tt(s4, s4, over_cols(g8b, 8, 4), ALU.add))
            first_best(chosen, sel, NE)
            link(V.scalar_tensor_tensor(sel, chosen, -3.0 * BIG, sel, ALU.mult, ALU.add))
            first_best(second, sel, NE)
            tt(chosen, chosen, second, ALU.add).then_inc(ev("r_sel"), 1)
            dve.wait_ge(ev("r_sel"), 1)
            link(tt(gates, probs, chosen, ALU.mult))
            link(V.reduce_sum(r1, gates, AX))
            link(V.reciprocal(r1, r1))
            link(tt(gates, gates, per(r1), ALU.mult))
            dve.wait_ge(ev("r_pos"), 1)
            V.tensor_copy(cnt, bank(1)[:, 32:48])
            link(V.scalar_tensor_tensor(pos, bank(1)[:, 0:32].rearrange("p (t e) -> p t e", e=NE), 1.0, chosen,
                                        ALU.add, ALU.mult))
            link(V.tensor_scalar(pos, pos, -1.0, None, ALU.add))
            for t in range(NT):
                for o, v in ((posx, pos), (gatex, gates)):
                    V.tensor_copy(o[:, 0:NE, t].rearrange("p (a q) -> p a q", q=4),
                                  v[:, t, :].rearrange("p (q a) -> p a q", a=4))
            V.memset(posx[:, NV, :], -1.0)
            V.memset(gatex[:, NV, :], 0.0)
            link(V.memset(flags, 0.0))
            link(V.tensor_scalar(flags[:, 8:8 + NE].rearrange("p (a q) -> p a q", q=4),
                                 cnt.rearrange("p (q a) -> p a q", a=4), float(XH), None, ALU.is_gt))
            V.tensor_copy(itab[0:1, 8:8 + NE], flags[0:1, 8:8 + NE]).then_inc(ev("tables_ready"), 1)

            def onehot(L, col):
                for t in range(NT):
                    pc = mem[:, bass.ds(col * NT + (posx_at + t), 1)]
                    gc = mem[:, bass.ds(col * NT + (gatex_at + t), 1)]
                    V.tensor_scalar(pos1h[:, t, :], iota[:, 0:P], pc, rs2[:, t:t + 1], ALU.is_equal, ALU.mult)
                    ins = V.tensor_scalar(gate1h[:, t, :], iota, pc, gc, ALU.is_equal, ALU.mult)
                ins.then_inc(L["onehot_ready"], 1)

            def take_gates(L, u, count):
                dve.wait_ge(L["pg_transposed"], count)
                V.tensor_copy(pgT[u], bank(4).rearrange("p (r n) -> p r n", n=P)).then_inc(L["pg_ready"], 1)

            def add_combined(L, q, b, sem, count):
                dve.wait_ge(L["combined"], count)
                xq = xacc[:, :, q * 512:(q + 1) * 512]
                tt(xq, xq, bank(b, 2).rearrange("p (t n) -> p t n", n=512), ALU.add).then_inc(L[sem], 1)

            def expert(L, i, u, base):
                dve.wait_ge(L["pg_transposed"], i * 2 + (u + 1))
                onehot(L, i * 2 + (base + u + 1))
                add_combined(L, 3, 4, "added_hi", i * 8 + (4 * u + 1))
                take_gates(L, 1 - u, i * 2 + (u + 2))
                dve.wait_ge(L["silu_done"], i * 2 + (u + 1))
                tt(hid, hid, bank(2, 2), ALU.mult).then_inc(L["hid_ready"], 1)
                dve.wait_ge(L["hid_transposed"], i * 2 + (u + 1))
                src = bank(5).rearrange("p (f n) -> p f n", n=P)
                V.tensor_copy(hidT[:, 4:8, XH:192], src)
                V.tensor_copy(hidT[:, 4:8, 0:XH], src[:, :, XH:P]).then_inc(L["hidT_dve"], 1)
                for q in range(4):
                    c5 = slice(q * 512, (q + 1) * 512)
                    dve.wait_ge(L["slot_used"], i * 24 + (12 * u + 9 + q))
                    tt(y_sb[:, c5], bank(4 + q), gate2_b[:, c5], ALU.mult).then_inc(L["y_ready"], 1)
                    if q > 0:
                        add_combined(L, q - 1, 2 * (q - 1) if q < 3 else 4, "added_lo" if q < 3 else "added_hi",
                                     i * 8 + (4 * u + q + 1))

            def start_pass(L, first):
                onehot(L, first)
                V.memset(hid, 0.0).then_inc(L["hid_ready"], 1)
                V.memset(pgT[1], 0.0).then_inc(L["added_lo"], 1)
                V.memset(y_sb[:, 0:1024], 0.0).then_inc(L["added_hi"], 1)
                V.memset(y_sb[:, 1024:D], 0.0).then_inc(L["y_ready"], 1)

            dve.wait_ge(ev("tables_ready"), 1)
            start_pass(main, 0)
            link(V.tensor_scalar(ovr, cnt, float(P), None, ALU.is_gt))
            link(V.tensor_tensor_scan(ovc, ones[:, 0:NE], ovr, 0.0, ALU.mult, ALU.add))
            link(tt(ovx, ovc, ovr, ALU.subtract))
            link(tt(ovm, over_heads(ovx, NOVER, NE), over_cols(iota[:, 0:NOVER], NOVER, NE), ALU.is_equal))
            link(tt(ovm, ovm, over_heads(ovr, NOVER, NE), ALU.mult))
            V.reduce_sum(ova, ovm, AX)
            link(tt(ovt, ovm, over_heads(iota[:, 0:NE], NOVER, NE), ALU.mult))
            link(V.reduce_sum(ove, ovt, AX))
            link(V.tensor_scalar(ova, ova, -1.0, None, ALU.add))

            def pick(o, table):
                link(tt(ovt, ovm, over_heads(table, NOVER, NE), ALU.mult))
                link(V.reduce_sum(o, ovt, AX))

            V.tensor_scalar(cntq, cnt, -float(P), None, ALU.add)
            link(V.tensor_scalar(posq, pos, -float(P), None, ALU.add))
            for t in range(NT):
                pick(ovo, posq[:, t, :])
                link(tt(posx[:, NE:NV, t], ovo, ova, ALU.add))
                pick(gatex[:, NE:NV, t], gates[:, t, :])
            pick(ovo, cntq)
            link(V.tensor_scalar(flags[:, 8 + NE:8 + NV], ovo, float(XH), None, ALU.is_gt))
            V.tensor_copy(flags[:, 0:1], ovc[:, NE - 1:NE])
            link(V.tensor_copy(flags[:, 32:32 + NOVER], ove))
            V.tensor_copy(itab[0:1, 0:8], flags[0:1, 0:8])
            V.tensor_copy(itab[0:1, 8 + NE:40], flags[0:1, 8 + NE:40]).then_inc(ev("over_tables_ready"), 1)
            dve.wait_ge(ev("over_tables_ready"), 1)
            take_gates(main, 0, 1)
            n_over = dve.value_load(itab[0:1, 0:1], min_val=0, max_val=NOVER)
            dve.wait_ge(ev("M_out3"), 1)
            dve.wait_ge(ev("xacc_ready"), 1)
            with dve.Fori(0, NE // 2) as i:
                for u in range(2):
                    expert(main, i, u, 0)
            add_combined(main, 3, 4, "added_hi", 4 * NE + 1)
            V.memset(r1, 0.0).then_inc(ev("main_done"), 1)
            with dve.If(n_over > 0):
                dve.wait_ge(main["squared"], 8)
                start_pass(over, NE)
                take_gates(over, 0, 1)
                with dve.Fori(0, NOVER // 2) as i:
                    for u in range(2):
                        expert(over, i, u, NE)
                add_combined(over, 3, 4, "added_hi", 4 * NOVER + 1)
            dve.wait_ge(ev("final_squared"), 1)
            V.reduce_sum(ss, ssf, AX).then_inc(ev("final_summed"), 1)
            dve.wait_ge(ev("rms3"), 1)
            dve.wait_ge(ev("fin_in"), 16)
            link(V.reciprocal(rs3, rs3))
            for t in range(NT):
                for h in range(2):
                    half = slice(h * 1024, (h + 1) * 1024)
                    V.scalar_tensor_tensor(xacc[:, t, half], xacc[:, t, half], rs3[:, t:t + 1], fin_b[:, half],
                                           ALU.mult, ALU.mult).then_inc(ev("out_ready"), 1)


_INS = ["x", "c", "w_mod", "b_mod", "norm1_g", "norm2_g", "w_in", "w_out", "conv_a_w", "gn_a", "attn_sinks",
        "gn_b", "ssm_conv_w", "ssm_conv_b", "dt_bias", "a_log", "d_skip", "ssm_norm_g", "gn_d", "router_w",
        "router_bias", "moe_w_gate", "moe_w_up", "moe_w_down", "final_g"]


def kernel(**inputs):
    import numpy as _np
    import concourse.bacc as _bacc
    from concourse import mybir as _mybir
    from concourse.bass_utils import run_bass_kernel_spmd as _run

    nc = _bacc.Bacc("TRN2", target_bir_lowering=False, num_devices=1)
    arrays, args = {}, []
    for name in _INS:
        a = _np.ascontiguousarray(inputs[name])
        arrays[f"in_{name}"] = a
        args.append(nc.dram_tensor(f"in_{name}", a.shape, _mybir.dt.from_np(a.dtype), kind="ExternalInput").ap())
    out = nc.dram_tensor("out_0", (1, SEQ, D), F32, kind="ExternalOutput").ap()
    trunk(nc, *args, out)
    r = _run(nc, [arrays], core_ids=[0])
    return r.results[0]["out_0"]
```
